# Optimizing a Trainium2 kernel written in Bass

```python
import jax, jax.numpy as jnp
from jax import lax
import numpy as np
import math

D_MODEL = 1024
BATCH = 1
SEQ = 1024
DEPTH = 1

N_MIXERS = 2
POOL_EXPAND = 2
D_POOL = POOL_EXPAND * D_MODEL
POOL_WINDOWS = (2, 4, 8, 16)
N_POOL_GROUPS = len(POOL_WINDOWS)
POOL_GROUP = D_POOL // N_POOL_GROUPS
HEAD_DIM = 64
N_HEADS = D_MODEL // HEAD_DIM
N_KV = 4
HPG = N_HEADS // N_KV
D_ATT = N_HEADS * HEAD_DIM
D_KV = N_KV * HEAD_DIM
N_BRANCH = 3
CMP_BLOCK = 32
CMP_STRIDE = 16
CMP_HIDDEN = 4 * HEAD_DIM
SEL_BLOCK = 64
SEL_TOPN = 8
WINDOW = 256
Q_BLOCK = 64
NSA_SPLITS = (D_ATT, D_KV, D_KV, D_KV, D_KV, D_KV, D_KV, D_ATT, N_BRANCH * N_HEADS)
NSA_VALUE_SLOTS = (2, 4, 6)
D_NSA_IN = sum(NSA_SPLITS)

N_POOL_LAYERS = (DEPTH + N_MIXERS - 1) // N_MIXERS
N_NSA_LAYERS = DEPTH // N_MIXERS

DN_ALPHA = (2.0 * DEPTH) ** 0.25
DN_BETA = (8.0 * DEPTH) ** -0.25
LN_EPS = 1e-5
NEG_INF = -1e30
FORCE_SCORE = 1e9


def layer_norm(x, g, b):
    xf = x.astype(jnp.float32)
    mu = jnp.mean(xf, axis=-1, keepdims=True)
    var = jnp.mean(jnp.square(xf - mu), axis=-1, keepdims=True)
    y = (xf - mu) * lax.rsqrt(var + LN_EPS) * g.astype(jnp.float32) + b.astype(jnp.float32)
    return y.astype(x.dtype)

def alibi_slopes():
    h = jnp.arange(1, N_HEADS + 1, dtype=jnp.float32)
    return (2.0 ** (-8.0 * h / N_HEADS)).reshape(N_KV, HPG)

def masked_softmax(s, valid):
    p = jax.nn.softmax(jnp.where(valid, s, NEG_INF), axis=-1)
    return jnp.where(valid, p, 0.0)

def pool_mixer(x, w_in, w_grp, scale, w_out):
    B, S, _ = x.shape
    h = x @ w_in
    u, z = h[..., :D_POOL], h[..., D_POOL:]
    u = u.astype(jnp.float32).reshape(B, S, N_POOL_GROUPS, POOL_GROUP)
    csum = jnp.cumsum(u, axis=1)
    t = jnp.arange(S)
    outs = []
    for g, w in enumerate(POOL_WINDOWS):
        c = csum[:, :, g]
        lag = jnp.pad(c, ((0, 0), (w, 0), (0, 0)))[:, :S]
        cnt = jnp.minimum(t + 1, w).astype(jnp.float32)[None, :, None]
        outs.append((c - lag) / cnt - u[:, :, g])
    m = jnp.stack(outs, axis=2).astype(x.dtype)
    m = jnp.einsum('bsgc,gcd->bsgd', m, w_grp).reshape(B, S, D_POOL) * scale
    return (m * jax.nn.silu(z)) @ w_out

def nsa_mixer(x, w_in, pos_k, w1_k, w2_k, pos_v, w1_v, w2_v, w_out):
    B, S, _ = x.shape
    dt = x.dtype
    h = x @ w_in
    q, kc, vc, ks, vs, kw, vw, z, gl = jnp.split(h, np.cumsum(NSA_SPLITS)[:-1].tolist(), axis=-1)
    q = q.reshape(B, S, N_KV, HPG, HEAD_DIM) * (HEAD_DIM ** -0.5)
    kc, vc, ks, vs, kw, vw = [a.reshape(B, S, N_KV, HEAD_DIM) for a in (kc, vc, ks, vs, kw, vw)]
    gates = jax.nn.sigmoid(gl.astype(jnp.float32)).reshape(B, S, N_KV, HPG, N_BRANCH)
    slopes = alibi_slopes()[None, :, :, None, None]

    n_cmp = (S - CMP_BLOCK) // CMP_STRIDE + 1
    cmp_idx = np.arange(n_cmp)[:, None] * CMP_STRIDE + np.arange(CMP_BLOCK)[None, :]
    cmp_end = jnp.asarray(cmp_idx[:, -1], dtype=jnp.int32)

    def compress(a, pos, w1, w2):
        blk = a[:, cmp_idx] + pos[None, None, :, None, :]
        blk = blk.transpose(0, 1, 3, 2, 4).reshape(B, n_cmp, N_KV, CMP_BLOCK * HEAD_DIM)
        return jax.nn.silu(blk @ w1) @ w2

    k_cmp = compress(kc, pos_k, w1_k, w2_k)
    v_cmp = compress(vc, pos_v, w1_v, w2_v)

    n_sel = S // SEL_BLOCK
    top_n = min(SEL_TOPN, n_sel)
    c0 = np.arange(n_cmp)[:, None] * CMP_STRIDE
    j0 = np.arange(n_sel)[None, :] * SEL_BLOCK
    overlap = jnp.asarray((c0 < j0 + SEL_BLOCK) & (c0 + CMP_BLOCK > j0), dtype=jnp.float32)
    ks_blk = ks.reshape(B, n_sel, SEL_BLOCK, N_KV, HEAD_DIM).transpose(0, 3, 1, 2, 4)
    vs_blk = vs.reshape(B, n_sel, SEL_BLOCK, N_KV, HEAD_DIM).transpose(0, 3, 1, 2, 4)
    b_ix = jnp.arange(B)[:, None, None, None]
    g_ix = jnp.arange(N_KV)[None, :, None, None]
    blk_ids = jnp.arange(n_sel)
    in_blk = jnp.arange(SEL_BLOCK)

    kw_pad = jnp.pad(kw, ((0, 0), (WINDOW, 0), (0, 0), (0, 0)))
    vw_pad = jnp.pad(vw, ((0, 0), (WINDOW, 0), (0, 0), (0, 0)))
    win_off = jnp.arange(WINDOW + Q_BLOCK) - WINDOW

    def block(i):
        q0 = i * Q_BLOCK
        qb = lax.dynamic_slice_in_dim(q, q0, Q_BLOCK, axis=1)
        gb = lax.dynamic_slice_in_dim(gates, q0, Q_BLOCK, axis=1)
        t = q0 + jnp.arange(Q_BLOCK)

        dist = t[:, None] - cmp_end[None, :]
        s = jnp.einsum('bqghd,bcgd->bghqc', qb, k_cmp).astype(jnp.float32)
        s = s - slopes * dist.astype(jnp.float32)
        p_cmp = masked_softmax(s, dist >= 0)
        o_cmp = jnp.einsum('bghqc,bcgd->bqghd', p_cmp.astype(dt), v_cmp)

        imp = jnp.einsum('bghqc,cn->bgqn', p_cmp, overlap)
        cur = t // SEL_BLOCK
        forced = (blk_ids[None] == 0) | (blk_ids[None] == cur[:, None]) | (blk_ids[None] == cur[:, None] - 1)
        future = blk_ids[None] > cur[:, None]
        imp = jnp.where(forced, FORCE_SCORE, jnp.where(future, NEG_INF, imp))
        _, sel = lax.top_k(imp, top_n)
        k_g = ks_blk[b_ix, g_ix, sel].reshape(B, N_KV, Q_BLOCK, top_n * SEL_BLOCK, HEAD_DIM)
        v_g = vs_blk[b_ix, g_ix, sel].reshape(B, N_KV, Q_BLOCK, top_n * SEL_BLOCK, HEAD_DIM)
        pos = (sel[..., None] * SEL_BLOCK + in_blk).reshape(B, N_KV, Q_BLOCK, top_n * SEL_BLOCK)
        dist = t[None, None, :, None] - pos
        s = jnp.einsum('bqghd,bgqkd->bghqk', qb, k_g).astype(jnp.float32)
        s = s - slopes * dist[:, :, None].astype(jnp.float32)
        p = masked_softmax(s, (dist >= 0)[:, :, None])
        o_sel = jnp.einsum('bghqk,bgqkd->bqghd', p.astype(dt), v_g)

        kwb = lax.dynamic_slice_in_dim(kw_pad, q0, WINDOW + Q_BLOCK, axis=1)
        vwb = lax.dynamic_slice_in_dim(vw_pad, q0, WINDOW + Q_BLOCK, axis=1)
        spos = q0 + win_off
        dist = t[:, None] - spos[None, :]
        valid = (dist >= 0) & (dist < WINDOW) & (spos[None, :] >= 0)
        s = jnp.einsum('bqghd,bkgd->bghqk', qb, kwb).astype(jnp.float32)
        s = s - slopes * dist.astype(jnp.float32)
        p = masked_softmax(s, valid)
        o_win = jnp.einsum('bghqk,bkgd->bqghd', p.astype(dt), vwb)

        o = gb[..., 0:1] * o_cmp + gb[..., 1:2] * o_sel + gb[..., 2:3] * o_win
        return o.astype(dt).reshape(B, Q_BLOCK, D_ATT)

    o = lax.map(block, jnp.arange(S // Q_BLOCK))
    o = o.transpose(1, 0, 2, 3).reshape(B, S, D_ATT)
    return (o * jax.nn.silu(z)) @ w_out

def first_inputs(seed: int = 0) -> dict:
    key = jax.random.key(seed)
    k = jax.random.split(key, 16)
    nA, nB = N_POOL_LAYERS, N_NSA_LAYERS

    def nrm(kk, shape, scale):
        return jax.random.normal(kk, shape, jnp.float32) * scale

    pool_col = jnp.asarray(np.concatenate([np.full(D_POOL, DN_BETA), np.ones(D_POOL)]), dtype=jnp.float32)
    nsa_col = jnp.asarray(np.concatenate([np.full(n, DN_BETA if s in NSA_VALUE_SLOTS else 1.0)
                                          for s, n in enumerate(NSA_SPLITS)]), dtype=jnp.float32)
    return {
        'x': nrm(k[0], (BATCH, SEQ, D_MODEL), 1.0),
        'ln_g': 1.0 + nrm(k[1], (DEPTH, D_MODEL), 0.02),
        'ln_b': nrm(k[2], (DEPTH, D_MODEL), 0.02),
        'pool_w_in': nrm(k[3], (nA, D_MODEL, 2 * D_POOL), D_MODEL ** -0.5) * pool_col,
        'pool_w_grp': nrm(k[4], (nA, N_POOL_GROUPS, POOL_GROUP, POOL_GROUP), POOL_GROUP ** -0.5),
        'pool_scale': 1.0 + nrm(k[5], (nA, D_POOL), 0.02),
        'pool_w_out': nrm(k[6], (nA, D_POOL, D_MODEL), D_POOL ** -0.5 * DN_BETA),
        'nsa_w_in': nrm(k[7], (nB, D_MODEL, D_NSA_IN), D_MODEL ** -0.5) * nsa_col,
        'nsa_cmp_pos_k': nrm(k[8], (nB, CMP_BLOCK, HEAD_DIM), 0.02),
        'nsa_cmp_w1_k': nrm(k[9], (nB, CMP_BLOCK * HEAD_DIM, CMP_HIDDEN), (CMP_BLOCK * HEAD_DIM) ** -0.5),
        'nsa_cmp_w2_k': nrm(k[10], (nB, CMP_HIDDEN, HEAD_DIM), CMP_HIDDEN ** -0.5),
        'nsa_cmp_pos_v': nrm(k[11], (nB, CMP_BLOCK, HEAD_DIM), 0.02),
        'nsa_cmp_w1_v': nrm(k[12], (nB, CMP_BLOCK * HEAD_DIM, CMP_HIDDEN), (CMP_BLOCK * HEAD_DIM) ** -0.5),
        'nsa_cmp_w2_v': nrm(k[13], (nB, CMP_HIDDEN, HEAD_DIM), CMP_HIDDEN ** -0.5),
        'nsa_w_out': nrm(k[14], (nB, D_ATT, D_MODEL), D_ATT ** -0.5 * DN_BETA),
    }

def first_block(x, ln_g, ln_b, pool_w_in, pool_w_grp, pool_scale, pool_w_out,
              nsa_w_in, nsa_cmp_pos_k, nsa_cmp_w1_k, nsa_cmp_w2_k,
              nsa_cmp_pos_v, nsa_cmp_w1_v, nsa_cmp_w2_v, nsa_w_out):
    for i in range(DEPTH):
        j = i // N_MIXERS
        if i % N_MIXERS == 0:
            y = pool_mixer(x, pool_w_in[j], pool_w_grp[j], pool_scale[j], pool_w_out[j])
        else:
            y = nsa_mixer(x, nsa_w_in[j], nsa_cmp_pos_k[j], nsa_cmp_w1_k[j], nsa_cmp_w2_k[j],
                          nsa_cmp_pos_v[j], nsa_cmp_w1_v[j], nsa_cmp_w2_v[j], nsa_w_out[j])
        x = layer_norm(DN_ALPHA * x + y, ln_g[i], ln_b[i])
    return x


DEPTH_2 = 2

GRID_W = 64
CTX_LEN = 256
N_HEADS_2 = D_MODEL // HEAD_DIM
A_KV_HEADS = 4
A_GROUPS = N_HEADS_2 // A_KV_HEADS
A_WINDOW = 128
A_BLOCK = 128
A_INNER = N_HEADS_2 * HEAD_DIM
A_KV_DIM = A_KV_HEADS * HEAD_DIM
A_IN_DIM = 2 * A_INNER + 2 * A_KV_DIM
B_KH_MAX = 8
B_KW = 16
B_QW = 16
B_REG_W = 2 * B_KW
B_INNER = N_HEADS_2 * HEAD_DIM
B_IN_DIM = 4 * B_INNER
ROPE_BASE = 10000.0
NEG_INF_2 = -1e30
DEEPNORM_ALPHA = (2.0 * DEPTH_2) ** 0.25
DEEPNORM_BETA = (8.0 * DEPTH_2) ** -0.25
N_LAYERS_A = (DEPTH_2 + 1) // 2
N_LAYERS_B = DEPTH_2 // 2


def layer_norm_2(x, g, b):
    xf = x.astype(jnp.float32)
    mu = jnp.mean(xf, axis=-1, keepdims=True)
    var = jnp.mean(jnp.square(xf - mu), axis=-1, keepdims=True)
    y = (xf - mu) * lax.rsqrt(var + LN_EPS)
    return (y * g.astype(jnp.float32) + b.astype(jnp.float32)).astype(x.dtype)

def axial_rope_tables(n_tok):
    t = jnp.arange(n_tok)
    row = (t // GRID_W).astype(jnp.float32)
    col = (t % GRID_W).astype(jnp.float32)
    n_freq = HEAD_DIM // 4
    inv = ROPE_BASE ** (-jnp.arange(n_freq, dtype=jnp.float32) / n_freq)
    ang_r = row[:, None] * inv[None]
    ang_c = col[:, None] * inv[None]
    return (jnp.cos(ang_r), jnp.sin(ang_r), jnp.cos(ang_c), jnp.sin(ang_c))

def _rotate(x, cos, sin):
    a, b = jnp.split(x, 2, axis=-1)
    cos = cos[None, :, None, :].astype(x.dtype)
    sin = sin[None, :, None, :].astype(x.dtype)
    return jnp.concatenate([a * cos - b * sin, b * cos + a * sin], axis=-1)

def apply_axial_rope(x, rope):
    cos_r, sin_r, cos_c, sin_c = rope
    xr, xc = jnp.split(x, 2, axis=-1)
    return jnp.concatenate([_rotate(xr, cos_r, sin_r), _rotate(xc, cos_c, sin_c)], axis=-1)

def ctx_attention(q, k, v, sink):
    B, C = q.shape[0], q.shape[1]
    s = jnp.einsum('bqkgd,bckd->bkgqc', q, k).astype(jnp.float32) * (HEAD_DIM ** -0.5)
    if sink is not None:
        s_sink = jnp.broadcast_to(sink[None, :, :, None, None], s.shape[:-1] + (1,))
        p = jax.nn.softmax(jnp.concatenate([s, s_sink], axis=-1), axis=-1)[..., :C]
    else:
        p = jax.nn.softmax(s, axis=-1)
    o = jnp.einsum('bkgqc,bckd->bqkgd', p.astype(v.dtype), v)
    return o.reshape(B, C, -1)

def _split_a(p):
    return jnp.split(p, [A_INNER, A_INNER + A_KV_DIM, A_INNER + 2 * A_KV_DIM], axis=-1)

def mixer_a(u, uc, w_in, w_out, sink, rope, ctx_out):
    B, S, _ = u.shape
    C = uc.shape[1]
    scale = HEAD_DIM ** -0.5
    q, k, v, g = _split_a(u @ w_in)
    q = apply_axial_rope(q.reshape(B, S, N_HEADS_2, HEAD_DIM), rope).reshape(B, S, A_KV_HEADS, A_GROUPS, HEAD_DIM)
    k = apply_axial_rope(k.reshape(B, S, A_KV_HEADS, HEAD_DIM), rope)
    v = v.reshape(B, S, A_KV_HEADS, HEAD_DIM)
    qc, kc, vc, gc = _split_a(uc @ w_in)
    kc = kc.reshape(B, C, A_KV_HEADS, HEAD_DIM)
    vc = vc.reshape(B, C, A_KV_HEADS, HEAD_DIM)
    sink_l = sink.reshape(A_KV_HEADS, A_GROUPS).astype(jnp.float32)
    span = A_BLOCK + 2 * A_WINDOW
    pad = ((0, 0), (A_WINDOW, A_WINDOW), (0, 0), (0, 0))
    kp = jnp.pad(k, pad)
    vp = jnp.pad(v, pad)

    def block(bi):
        start = bi * A_BLOCK
        qb = lax.dynamic_slice_in_dim(q, start, A_BLOCK, axis=1)
        kb = lax.dynamic_slice_in_dim(kp, start, span, axis=1)
        vb = lax.dynamic_slice_in_dim(vp, start, span, axis=1)
        qi = start + jnp.arange(A_BLOCK)
        kj = start - A_WINDOW + jnp.arange(span)
        mask = (jnp.abs(qi[:, None] - kj[None, :]) <= A_WINDOW) & (kj >= 0)[None, :] & (kj < S)[None, :]
        s_lat = jnp.einsum('bqkgd,bjkd->bkgqj', qb, kb).astype(jnp.float32) * scale
        s_lat = jnp.where(mask, s_lat, NEG_INF_2)
        s_ctx = jnp.einsum('bqkgd,bckd->bkgqc', qb, kc).astype(jnp.float32) * scale
        s_sink = jnp.broadcast_to(sink_l[None, :, :, None, None], s_lat.shape[:-1] + (1,))
        p = jax.nn.softmax(jnp.concatenate([s_lat, s_ctx, s_sink], axis=-1), axis=-1)
        p_lat = p[..., :span].astype(v.dtype)
        p_ctx = p[..., span:span + C].astype(v.dtype)
        o = jnp.einsum('bkgqj,bjkd->bqkgd', p_lat, vb) + jnp.einsum('bkgqc,bckd->bqkgd', p_ctx, vc)
        return o.reshape(B, A_BLOCK, A_INNER)

    o = lax.map(block, jnp.arange(S // A_BLOCK))
    o = jnp.transpose(o, (1, 0, 2, 3)).reshape(B, S, A_INNER)
    y = (o * jax.nn.silu(g)) @ w_out
    if not ctx_out:
        return y, None
    oc = ctx_attention(qc.reshape(B, C, A_KV_HEADS, A_GROUPS, HEAD_DIM), kc, vc, sink_l)
    yc = (oc * jax.nn.silu(gc)) @ w_out
    return y, yc

def mixer_b(u, uc, w_in, w_out, rel_bias, ctx_out):
    B, S, _ = u.shape
    C = uc.shape[1]
    rows = S // GRID_W
    kh = min(B_KH_MAX, rows)
    scale = HEAD_DIM ** -0.5
    q, k, v, g = jnp.split(u @ w_in, 4, axis=-1)
    q = q.reshape(B, rows, GRID_W, N_HEADS_2, HEAD_DIM)
    k = k.reshape(B, rows, GRID_W, N_HEADS_2, HEAD_DIM)
    v = v.reshape(B, rows, GRID_W, N_HEADS_2, HEAD_DIM)
    qc, kc, vc, gc = jnp.split(uc @ w_in, 4, axis=-1)
    kc = kc.reshape(B, C, N_HEADS_2, HEAD_DIM)
    vc = vc.reshape(B, C, N_HEADS_2, HEAD_DIM)

    n_cb = GRID_W // B_QW
    c0 = np.arange(n_cb) * B_QW
    cs_blk = np.clip(c0 - B_KW // 2, 0, GRID_W - B_REG_W)
    key_col = cs_blk[:, None] + np.arange(B_REG_W)
    q_col = c0[:, None] + np.arange(B_QW)
    cs_q = np.clip(q_col - B_KW // 2, 0, GRID_W - B_KW)
    col_mask = (key_col[:, None, :] >= cs_q[:, :, None]) & (key_col[:, None, :] < cs_q[:, :, None] + B_KW)
    col_idx = np.clip(key_col[:, None, :] - q_col[:, :, None] + (B_KW - 1), 0, 2 * B_KW - 2)
    key_col = jnp.asarray(key_col, dtype=jnp.int32)
    col_idx = jnp.asarray(col_idx, dtype=jnp.int32)
    col_mask = jnp.asarray(col_mask)[:, :, None, :]
    bias_tab = rel_bias.astype(jnp.float32)

    def row_block(r):
        rs = jnp.clip(r - kh // 2, 0, rows - kh)
        q_r = lax.dynamic_index_in_dim(q, r, axis=1, keepdims=False).reshape(B, n_cb, B_QW, N_HEADS_2, HEAD_DIM)
        k_rows = lax.dynamic_slice_in_dim(k, rs, kh, axis=1)
        v_rows = lax.dynamic_slice_in_dim(v, rs, kh, axis=1)
        k_reg = k_rows[:, :, key_col]
        v_reg = v_rows[:, :, key_col]
        s = jnp.einsum('bnqhd,brnjhd->bhnqrj', q_r, k_reg).astype(jnp.float32) * scale
        row_idx = rs + jnp.arange(kh) - r + (B_KH_MAX - 1)
        bias = bias_tab[:, row_idx[:, None, None, None], col_idx[None]]
        s = s + jnp.transpose(bias, (0, 2, 3, 1, 4))[None]
        s = jnp.where(col_mask, s, NEG_INF_2).reshape(B, N_HEADS_2, n_cb, B_QW, kh * B_REG_W)
        s_ctx = jnp.einsum('bnqhd,bchd->bhnqc', q_r, kc).astype(jnp.float32) * scale
        p = jax.nn.softmax(jnp.concatenate([s, s_ctx], axis=-1), axis=-1)
        p_lat = p[..., :kh * B_REG_W].reshape(B, N_HEADS_2, n_cb, B_QW, kh, B_REG_W).astype(v.dtype)
        p_ctx = p[..., kh * B_REG_W:].astype(v.dtype)
        o = jnp.einsum('bhnqrj,brnjhd->bnqhd', p_lat, v_reg) + jnp.einsum('bhnqc,bchd->bnqhd', p_ctx, vc)
        return o.reshape(B, GRID_W, B_INNER)

    o = lax.map(row_block, jnp.arange(rows))
    o = jnp.transpose(o, (1, 0, 2, 3)).reshape(B, S, B_INNER)
    y = (o * jax.nn.silu(g)) @ w_out
    if not ctx_out:
        return y, None
    oc = ctx_attention(qc.reshape(B, C, N_HEADS_2, 1, HEAD_DIM), kc[:, :, :, :], vc, None)
    yc = (oc * jax.nn.silu(gc)) @ w_out
    return y, yc

def second_inputs(seed: int = 0) -> dict:
    key = jax.random.key(seed)
    ks = jax.random.split(key, 14)
    f32 = jnp.float32
    d = D_MODEL
    return {
        "x": jax.random.normal(ks[0], (BATCH, SEQ, d), f32),
        "c": jax.random.normal(ks[1], (BATCH, d), f32),
        "ctx": jax.random.normal(ks[2], (BATCH, CTX_LEN, d), f32),
        "c_ctx": jax.random.normal(ks[3], (d,), f32),
        "w_ada": jax.random.normal(ks[4], (DEPTH_2, d, 3 * d), f32) * d ** -0.5,
        "b_ada": 0.01 * jax.random.normal(ks[5], (DEPTH_2, 3 * d), f32),
        "ln_g": 1.0 + 0.05 * jax.random.normal(ks[6], (DEPTH_2, d), f32),
        "ln_b": 0.02 * jax.random.normal(ks[7], (DEPTH_2, d), f32),
        "a_w_in": jax.random.normal(ks[8], (N_LAYERS_A, d, A_IN_DIM), f32) * d ** -0.5,
        "a_w_out": jax.random.normal(ks[9], (N_LAYERS_A, A_INNER, d), f32) * (A_INNER ** -0.5 * DEEPNORM_BETA),
        "a_sink": 0.5 * jax.random.normal(ks[10], (N_LAYERS_A, N_HEADS_2), f32),
        "b_w_in": jax.random.normal(ks[11], (N_LAYERS_B, d, B_IN_DIM), f32) * d ** -0.5,
        "b_w_out": jax.random.normal(ks[12], (N_LAYERS_B, B_INNER, d), f32) * (B_INNER ** -0.5 * DEEPNORM_BETA),
        "b_rel_bias": 0.5 * jax.random.normal(ks[13], (N_LAYERS_B, N_HEADS_2, 2 * B_KH_MAX - 1, 2 * B_KW - 1), f32),
    }

def second_block(x, c, ctx, c_ctx, w_ada, b_ada, ln_g, ln_b, a_w_in, a_w_out, a_sink, b_w_in, b_w_out, b_rel_bias):
    S = x.shape[1]
    rope = axial_rope_tables(S)
    silu_c = jax.nn.silu(c)
    silu_cc = jax.nn.silu(c_ctx)
    h, hc = x, ctx
    for i in range(DEPTH_2):
        shift, scale, gate = jnp.split(silu_c @ w_ada[i] + b_ada[i], 3, axis=-1)
        shift_c, scale_c, gate_c = jnp.split(silu_cc @ w_ada[i] + b_ada[i], 3, axis=-1)
        ctx_out = i < DEPTH_2 - 1
        u = h * (1.0 + scale[:, None, :]) + shift[:, None, :]
        uc = hc * (1.0 + scale_c) + shift_c
        j = i // N_MIXERS
        if i % N_MIXERS == 0:
            y, yc = mixer_a(u, uc, a_w_in[j], a_w_out[j], a_sink[j], rope, ctx_out)
        else:
            y, yc = mixer_b(u, uc, b_w_in[j], b_w_out[j], b_rel_bias[j], ctx_out)
        h = layer_norm_2(DEEPNORM_ALPHA * h + gate[:, None, :] * y, ln_g[i], ln_b[i])
        if ctx_out:
            hc = layer_norm_2(DEEPNORM_ALPHA * hc + gate_c * yc, ln_g[i], ln_b[i])
    return h


def setup_inputs(seed=0):
    out = dict(first_inputs(seed))
    for name, value in second_inputs(seed + 1).items():
        if name != "x":
            out[name + "_2"] = value
    return out


def reference(
    x, ln_g, ln_b, pool_w_in, pool_w_grp, pool_scale, pool_w_out, nsa_w_in, nsa_cmp_pos_k,
    nsa_cmp_w1_k, nsa_cmp_w2_k, nsa_cmp_pos_v, nsa_cmp_w1_v, nsa_cmp_w2_v, nsa_w_out, c_2,
    ctx_2, c_ctx_2, w_ada_2, b_ada_2, ln_g_2, ln_b_2, a_w_in_2, a_w_out_2, a_sink_2, b_w_in_2,
    b_w_out_2, b_rel_bias_2,
):
    x = first_block(
        x, ln_g, ln_b, pool_w_in, pool_w_grp, pool_scale, pool_w_out, nsa_w_in, nsa_cmp_pos_k,
        nsa_cmp_w1_k, nsa_cmp_w2_k, nsa_cmp_pos_v, nsa_cmp_w1_v, nsa_cmp_w2_v, nsa_w_out,
    )
    return second_block(
        x, c_2, ctx_2, c_ctx_2, w_ada_2, b_ada_2, ln_g_2, ln_b_2, a_w_in_2, a_w_out_2, a_sink_2,
        b_w_in_2, b_w_out_2, b_rel_bias_2,
    )


_drawn_inputs = setup_inputs


def setup_inputs(seed=0):
    import zlib

    import numpy as np

    out = dict(_drawn_inputs(seed))
    spreads = {}
    factors = {'ln_b': 2.734,
     'pool_scale': 79.561,
     'b_ada_2': 8.0,
     'a_sink_2': 44.691,
     'b_rel_bias_2': 4.474,
     'ctx_2': 2.864}
    for name, (base, spread) in spreads.items():
        noise = np.random.default_rng([zlib.crc32(name.encode()), seed]).standard_normal(out[name].shape)
        drawn = base * np.exp(spread * noise) if base else spread * noise
        out[name] = __import__('jax').numpy.asarray(drawn.astype(out[name].dtype))
    for name, factor in factors.items():
        out[name] = (out[name] * factor).astype(out[name].dtype)
    return out
```

```python
from contextlib import ExitStack

import numpy as np

import concourse.bass as bass
from concourse import mybir

F32 = mybir.dt.float32
F32R = mybir.dt.float32r
ALU = mybir.AluOpType
ACT = mybir.ActivationFunctionType

P = 128
D = 1024
S = 1024
C = 256
TC = S + C
KT = D // P
HALF = 512
UNIT = KT * P
HD = 64
HEADS = 16
PAIRS = HEADS // 2
Q_SCALE = HD ** -0.5
LN_EPS = 1e-5
ALPHA_1 = 2.0 ** 0.25
ALPHA_2 = 4.0 ** 0.25
MASKED = -1e30
NO_MAX = 3e38

GROUPS = 4
WINDOWS = (2, 4, 8, 16)
PAD = 16
L1_UNITS = 14
L1_CHUNKS = 8 * 2 + 2 * 4 + 4 * 4
L1_ENDS = [2 * (n + 1) for n in range(8)] + [20, 24] + [28, 32, 36, 40]
ADA = 12
ADA_UNITS = 48

A_UNIT = GROUPS * L1_UNITS
AO_UNIT = A_UNIT + 20
B_UNIT = AO_UNIT + KT
BO_UNIT = B_UNIT + 4 * PAIRS
ALL_UNITS = BO_UNIT + KT
A_CHUNK = GROUPS * L1_CHUNKS
AO_CHUNK = A_CHUNK + 20 * 3
B_CHUNK = AO_CHUNK + 8 * 3
BO_CHUNK = B_CHUNK + 10 * PAIRS
LAT_CHUNKS = [(0, HALF), (HALF, HALF)]
ALL_CHUNKS = LAT_CHUNKS + [(S, C)]

A_TILES = S // P + C // P
A_STEPS = 2 * A_TILES
GRID = 64
ROWS = S // GRID
B_TILES = 8
B_STEPS = 2 * B_TILES
KEY_COL = (0, 8, 24, 32)
COL_TYPE = (0, 1, 1, 2)
KEY_ROWS, KEY_COLS = 12, 32
LAT_KEYS = KEY_ROWS * KEY_COLS
KEYS = LAT_KEYS + C
TAB_R, TAB_C = 23, 63
TAB_RUN = TAB_R * TAB_C - (7 * TAB_C + 15)
TAB_ROWS = 16
B_BUILDS = 6
LAST_BIAS_USE = ((1, 6), (1, 7), (0, 0), (0, 2), (0, 3), (0, 4))
STEPS_A = PAIRS * A_STEPS
OT_A = PAIRS * A_TILES
VSETS_A, VSETS_B = 3, 5


def free_counts(first_half, l0, n):
    last = {}
    for l in range(l0, l0 + n):
        last[l % 2] = first_half + (l // 2 + 1)
    return last


class Chain:

    def __init__(self, eng, sem):
        self.eng, self.sem, self.base, self.local, self.at, self.per = eng, sem, 0, 0, 0, 0

    def begin(self, at, per):
        self.base += self.local if self.per == 0 else 0
        self.at, self.per, self.local = at, per, 0

    def end(self, times):
        assert self.local == self.per, (self.local, self.per)
        self.base += self.per * times
        self.at = self.per = self.local = 0

    def __call__(self, ins, alone=None):
        ins.then_inc(self.sem, 1)
        self.local += 1
        wait = self.eng.wait_ge(self.sem, self.at * self.per + (self.base + self.local))
        if alone is not None:
            wait.then_inc(alone, 1)


def build(nc, a):
    ctx = ExitStack()
    sems = {}

    def sem(name):
        sems[name] = ctx.enter_context(nc.semaphore(name))
        return sems[name]

    base = (nc.sbuf_base + 63) // 64 * 64
    at = [base]
    limit = nc.sbuf_usable_end

    def sb(name, shape, dt=F32, offset=None):
        size = 4 * int(np.prod(shape[1:]))
        size = (size + 31) // 32 * 32
        where = at[0] if offset is None else offset
        assert where + size <= limit, (name, where + size - limit)
        if offset is None:
            at[0] += size
        return nc.alloc_sbuf_tensor_at(name, shape, dt, offset=where)

    w_raw = sb("w_raw", [P, 2, UNIT])
    w_hi = sb("w_hi", [P, 2, UNIT], F32R)
    w_lo = sb("w_lo", [P, 2, UNIT], F32R)
    ident = sb("ident", [P, P])
    vecs = sb("vecs", [P, 4 * KT + 16 + ADA_UNITS])
    ln_g1, ln_b1, ln_g2, ln_b2 = (vecs[:, KT * n:KT * (n + 1)] for n in range(4))
    pool_scale = vecs[:, 4 * KT:4 * KT + 16]
    b_ada = vecs[:, 4 * KT + 16:]
    ada = sb("ada", [P, ADA_UNITS, 2])
    par = sb("par", [P, 12, KT])
    c_silu = sb("c_silu", [P, KT, 2])
    sink_neg = sb("sink_neg", [P, HEADS])
    corr = sb("corr", [P, GROUPS, PAD])
    minus_half = sb("minus_half", [P, 1])
    stats = sb("stats", [P, 2, 12])
    mean_var = sb("mean_var", [P, 2, 2])
    var_eps = sb("var_eps", [P, 2])
    rstd = sb("rstd", [P, 2])
    neg_max = sb("neg_max", [P, 2])
    row_sum = sb("row_sum", [P, 2])
    row_rec = sb("row_rec", [P, 2])
    row_mask = sb("row_mask", [P, 2, KEY_ROWS])
    col_mask = sb("col_mask", [P, 3, KEY_COLS])
    c_in = sb("c_in", [P, KT, 2])
    ada_at = at[0]
    w_ada = sb("w_ada", [P, UNIT])
    act_buf = sb("act_buf", [P, KT, TC])
    region = at[0]

    x_hi = sb("x_hi", [P, KT, S], F32R)
    x_lo = sb("x_lo", [P, KT, S], F32R)
    m_hi = sb("m_hi", [P, 4, S], F32R)
    m_lo = sb("m_lo", [P, 4, S], F32R)
    sz01 = sb("sz01", [P, 2, S])
    g_at = at[0]
    g_hi = sb("g_hi", [P, 4, S], F32R)
    g_lo = sb("g_lo", [P, 4, S], F32R)
    u_pad = sb("u_pad", [P, PAD + S], offset=g_at)
    win = [sb(f"win{n}", [P, PAD + S], offset=g_at + (n + 1) * 4 * (PAD + S)) for n in range(2)]

    def gate_tile(n):
        if n < 2:
            return sz01[:, n, :].rearrange("p (a b) -> p a b", b=C)
        return act_buf[:, 4 * (n - 2):4 * (n - 2) + 4, S:TC]

    at[0] = region
    u_hi = sb("u_hi", [P, KT, TC], F32R)
    u_lo = sb("u_lo", [P, KT, TC], F32R)
    after_u = at[0]
    z_tile = sb("z_tile", [P, 2, D], offset=after_u + 12288)
    x_hat = sb("x_hat", [P, 2, D], offset=after_u + 12288 + 8192)
    u_tmp = sb("u_tmp", [P, 2, TC], offset=after_u)
    out_tile = sb("out_tile", [P, 2, D], offset=after_u + 12288 + 16384)
    g_row = sb("g_row", [P, D], offset=after_u + 12288 + 24576)
    b_row = sb("b_row", [P, D], offset=after_u + 12288 + 28672)
    res = sb("res", [P, 2, TC], offset=after_u)

    def attention_part(x, q_len, v_tiles):
        q_hi = sb(x + "q_hi", [P, q_len], F32R)
        q_lo = sb(x + "q_lo", [P, q_len], F32R)
        k_hi = sb(x + "k_hi", [P, TC], F32R)
        k_lo = sb(x + "k_lo", [P, TC], F32R)
        v = sb(x + "v", [P, v_tiles, P])
        o_sb = sb(x + "o_sb", [P, 2, P])
        work = at[0]
        logits = [sb(f"{x}logits{n}", [P, KEYS + 1]) for n in range(2)]
        probs = [sb(f"{x}probs{n}", [P, KEYS + 1]) for n in range(2)]
        probs_t = sb(x + "probs_t", [P, KEYS])
        return q_hi, q_lo, k_hi, k_lo, v, o_sb, work, logits, probs, probs_t

    aq_hi, aq_lo, ak_hi, ak_lo, av, ao_sb, work_a, alog, aprob, aprob_t = attention_part("a_", TC, 10)
    rope_cos = sb("rope_cos", [P, S])
    rope_sin = sb("rope_sin", [P, S])
    a_mask = sb("a_mask", [P, KEYS])
    a_tmp = sb("a_tmp", [P, TC], offset=work_a)
    a_swap = sb("a_swap", [P, S], offset=work_a + 4 * TC)
    at[0] = after_u
    bq_hi, bq_lo, bk_hi, bk_lo, bv, bo_sb, work_b, blog, bprob, bprob_t = attention_part("b_", S, 18)
    bias = sb("bias", [P, 2, 2, KEYS])
    tab = [sb("tab0", [P, TAB_ROWS * TAB_C], offset=ada_at), sb("tab1", [P, TAB_ROWS * TAB_C])]
    b_tmp_q = sb("b_tmp_q", [P, S], offset=work_b)
    b_tmp_k = sb("b_tmp_k", [P, TC], offset=work_b + 4 * S)
    b_vt = sb("b_vt", [P, 4 * HALF + C], offset=work_b)

    psum = ctx.enter_context(nc.psum_tensor("psum", [P, 8 * HALF], F32))

    def bank(n, count=1):
        return psum[:, n * HALF:(n + count) * HALF]

    pj = [bank(6), bank(7)]
    ps_score = [bank(0, 2), bank(2, 2)]
    ps_pt = bank(4, 2)
    ps_o, ps_ot = bank(6), bank(7)

    residual = [nc.dram_tensor(f"residual{n}", [KT, P, TC if n == 0 else S], F32, kind="Internal").ap()
                for n in range(2)]

    w_loaded = [sem("w_loaded0"), sem("w_loaded1")]
    w_hi_done, w_split = sem("w_hi_done"), sem("w_split")
    ada_loaded, ada_done, ada_free = sem("ada_loaded"), sem("ada_done"), sem("ada_free")
    pj_done, pj_free = sem("pj_done"), [sem("pj_free0"), sem("pj_free1")]
    const_loaded, ctx_loaded = sem("const_loaded"), sem("ctx_loaded")
    x_loaded = [sem(f"x_loaded{k}") for k in range(KT)]
    x_hi_done, x_split, x_scaled, c_ready = sem("x_hi_done"), sem("x_split"), sem("x_scaled"), sem("c_ready")
    u_used, m_split, g_hi_done, g_split = sem("u_used"), sem("m_split"), sem("g_hi_done"), sem("g_split")
    ln_tile, ln_turned, ln_var, ln_rstd = sem("ln_tile"), sem("ln_turned"), sem("ln_var"), sem("ln_rstd")
    ln_norm, ln_back, ln_stored = sem("ln_norm"), sem("ln_back"), sem("ln_stored")
    par_ready = sem("par_ready")
    mod_done, mod_split, mod_hi = sem("mod_done"), sem("mod_split"), sem("mod_hi")
    res_ready, res_stored = sem("res_ready"), sem("res_stored")
    res_loaded = [sem("res_loaded0"), sem("res_loaded1")]
    q_split, k_split = sem("q_split"), sem("k_split")
    v_turned, v_ready = sem("v_turned"), sem("v_ready")
    tab_loaded, bias_ready = sem("tab_loaded"), sem("bias_ready")
    score_done, logit_done, prob_done = sem("score_done"), sem("logit_done"), sem("prob_done")
    pt_done, pt_dve, pt_act = sem("pt_done"), sem("pt_dve"), sem("pt_act")
    rec_done, pv_done, o_done = sem("rec_done"), sem("pv_done"), sem("o_done")
    ot_done, gated = sem("ot_done"), sem("gated")
    o_hi_done, o_split = sem("o_hi_done"), sem("o_split")
    out_scaled, out_ready = sem("out_scaled"), sem("out_ready")
    out_stored = [sem("out_stored0"), sem("out_stored1")]
    dve_step, pool_step = sem("dve_step"), sem("pool_step")
    dve_waited, pool_waited = sem("dve_waited"), sem("pool_waited")

    block = ctx.enter_context(nc.Block())

    def start_at_one(eng, ready, value, signals):
        for s in signals:
            eng.wait_ge(ready, value).then_inc(s, 1)

    def after(eng, signal, count):
        return eng.wait_ge(signal, count + 1)

    def one(ap):
        return ap.rearrange("a p n -> (a p) n")

    def col(t, n, lo=None, hi=None):
        lo, hi = lo or 0, hi or t.shape[2]
        return t[:, bass.ds(n, 1), lo:hi].rearrange("p a n -> p (a n)")

    def a_tile(t):
        if t >= S // P:
            return KEYS - C, [(KEYS - C, S, P), (KEYS - P, S + P, P)], [8, 9], P
        if t == 0:
            return P, [(P, 0, P), (2 * P, S, C), (4 * P, P, P)], [0, 8, 9, 1], P
        if t == S // P - 1:
            return P, [(P, (t - 1) * P, 2 * P), (3 * P, S, P), (4 * P, S + P, P)], [t - 1, t, 8, 9], 0
        return 0, [(0, (t - 1) * P, 2 * P), (2 * P, S, C), (4 * P, (t + 1) * P, P)], [t - 1, t, 8, 9, t + 1], 0

    def load_tab(sp, j, h):
        table = a["bias_tab"][bass.ds(2 * j + h, 1)]
        runs = bass.AP(tensor=table.tensor, offset=table.offset, ap=[[TAB_C, 8], [1, 16], [1, TAB_RUN]])
        sp.dma_start(tab[h][:, 0:TAB_RUN], runs).then_inc(tab_loaded, 16)

    def residual_loads(act, layer, c, chunks):
        tokens = (TC, S)[layer]

        def load(o, s):
            act.dma_start(res[:, s, 0:tokens], one(residual[layer][bass.ds(o, 1)])).then_inc(res_loaded[s], 16)

        act.wait_ge(res_stored, 16 * KT * (layer + 1))
        for s in range(2):
            load(s, s)
        with act.Fori(0, KT // 2 - 1) as i:
            for s in range(2):
                for b, v in free_counts(len(chunks) * i + c // 2, s * len(chunks), len(chunks)).items():
                    after(act, pj_free[b], v)
                load(2 * i + (2 + s), s)

    @block.sync
    def _(sp):
        def load_unit(n, slot):
            sp.dma_start(w_raw[:, slot, :], one(a["weights"][bass.ds(n, 1)])).then_inc(w_loaded[slot], 16)

        def next_unit(n, slot):
            sp.wait_ge(w_split, n + 1)
            load_unit(n + 2, slot)

        for k in range(KT):
            sp.dma_start(act_buf[:, k, 0:S], a["x_t"][:, k, :]).then_inc(x_loaded[k], 16)
            if k < 2:
                load_unit(k, k)
        with sp.Fori(0, GROUPS) as g:
            for l in range(L1_UNITS):
                next_unit(g * L1_UNITS + l, l % 2)
                if l < ADA:
                    after(sp, ada_done, g * ADA + l)
                    sp.dma_start(w_ada[:, :], one(a["w_ada"][bass.ds(g * ADA + l, 1)])).then_inc(ada_loaded, 16)
        sp.wait_ge(g_split, 4 * GROUPS)
        sp.dma_start(act_buf[:, :, S:TC], a["ctx_t"]).then_inc(ctx_loaded, 16)
        sp.wait_ge(pj_done, A_CHUNK)
        for dst, src in ((rope_cos, "rope_cos"), (rope_sin, "rope_sin"), (a_mask, "a_mask")):
            sp.dma_start(dst[:, :], a[src]).then_inc(ctx_loaded, 16)
        for n in (A_UNIT, A_UNIT + 1):
            next_unit(n, n % 2)
        with sp.Fori(0, KT) as k:
            sp.wait_ge(res_ready, k + 1)
            sp.dma_start(one(residual[0][bass.ds(k, 1)]), col(act_buf, k)).then_inc(res_stored, 16)
        with sp.Fori((A_UNIT + 2) // 2, B_UNIT // 2 + 1) as i:
            for s in range(2):
                next_unit(2 * i + s, s)
        for h in range(2):
            load_tab(sp, 0, h)
        with sp.Fori(0, KT) as k:
            sp.wait_ge(res_ready, k + (KT + 1))
            sp.dma_start(one(residual[1][bass.ds(k, 1)]), col(act_buf, k, 0, S)).then_inc(res_stored, 16)
        with sp.Fori(0, PAIRS - 1) as j:
            for l in range(4):
                next_unit(4 * j + (B_UNIT + 2 + l), l % 2)
            sp.wait_ge(bias_ready, (j + 1) * (2 * B_BUILDS))
            for h in range(2):
                load_tab(sp, j + 1, h)
        with sp.Fori((B_UNIT + 2 + 4 * (PAIRS - 1)) // 2, (ALL_UNITS - 2) // 2) as i:
            for s in range(2):
                next_unit(2 * i + s, s)
        after(sp, gated, OT_A + PAIRS * B_TILES)
        for dst, src in ((g_row, "ln_g3"), (b_row, "ln_b3")):
            sp.dma_start(dst[:, :], bass.AP(tensor=a[src].tensor, offset=0, ap=[[0, P], [1, D]])).then_inc(ctx_loaded, 16)
        for s in range(2):
            sp.wait_ge(ctx_loaded, 16 * 4).then_inc(out_stored[s], 16)
        with sp.Fori(0, S // P // 2) as i:
            for s in range(2):
                sp.wait_ge(out_ready, 2 * i + (s + 1))
                sp.dma_start(one(a["out"][bass.ds(2 * i + s, 1)]), out_tile[:, s, :]).then_inc(out_stored[s], 16)
        for s in range(2):
            sp.wait_ge(out_stored[s], 16 * (S // P // 2) + 16)
        sp.wait_ge(res_stored, 16 * 2 * KT)

    @block.gpsimd
    def _(pool):
        step = Chain(pool, pool_step)

        def loads(turn):
            return 16 * turn + 16

        def split(n, slot, loaded, used=None):
            pool.wait_ge(w_loaded[slot], loaded)
            if used is not None:
                pool.wait_ge(pj_done, used).then_inc(pool_waited, 1)
            pool.tensor_copy(w_hi[:, slot, :], w_raw[:, slot, :]).then_inc(w_hi_done, 1)
            pool.wait_ge(w_hi_done, n + 1)
            pool.tensor_tensor(w_lo[:, slot, :], w_raw[:, slot, :], w_hi[:, slot, :].bitcast(F32),
                               ALU.subtract).then_inc(w_split, 1)

        pool.memset(minus_half[:, :], -0.5).then_inc(pool_step, 1)
        step.base += 1
        for n in range(2):
            split(n, n, loads(0))
        with pool.Fori(0, GROUPS) as g:
            for l in range(L1_UNITS):
                split(g * L1_UNITS + (l + 2), l % 2,
                      loads(g * (L1_UNITS // 2) + (l + 2) // 2), g * L1_CHUNKS + L1_ENDS[l])

        def rstds(first, tiles):
            if first == 0:
                pool.wait_ge(pool_step, 1)
            with pool.Fori(0, tiles // 2) as i:
                for s in range(2):
                    t = 2 * i + (first + s)
                    pool.wait_ge(ln_var, t + 1)
                    if first or s:
                        after(pool, ln_norm, t - 1)
                    pool.tensor_tensor(rstd[:, s:s + 1], var_eps[:, s:s + 1], minus_half[:, :],
                                       ALU.pow).then_inc(ln_rstd, 1)

        def residuals(layer):
            pool.wait_ge(par_ready, layer + 1)
            for k in range(KT):
                pool.wait_ge(mod_done, layer * KT + k + 1)
                x = act_buf[:, k, 0:S]
                ins = pool.tensor_scalar(x, x, par[:, 4 + 6 * layer, k:k + 1], par[:, 5 + 6 * layer, k:k + 1],
                                         ALU.mult, ALU.add)
                if layer == 0:
                    x = act_buf[:, k, S:TC]
                    ins = pool.tensor_scalar(x, x, ALPHA_2, None, ALU.mult)
                ins.then_inc(res_ready, 1)

        rstds(0, S // P)
        residuals(0)
        for m in range(2):
            n, c = A_UNIT + 10 * m, A_CHUNK + 30 * m
            for l in range(2):
                split(n + l + 2, l, loads((n + l + 2) // 2), c + 3 * (l + 1))
            with pool.Fori(0, 4) as i:
                for l in range(2):
                    split(2 * i + (n + 4 + l), l, loads(i + (n + 4) // 2), 6 * i + (c + 9 + 3 * l))
        with pool.Fori(0, KT // 2) as i:
            for l in range(2):
                split(2 * i + (AO_UNIT + 2 + l), l, loads(i + (AO_UNIT + 2) // 2),
                      6 * i + (AO_CHUNK + 3 + 3 * l))
        after(pool, gated, OT_A)
        pool.memset(bias[:, :, :, LAT_KEYS:KEYS], 0.0).then_inc(pool_step, 1)
        step.base += 1
        rstds(S // P, TC // P)
        residuals(1)
        step.begin(0, 0)

        def bias_tile(j, b):
            half, kind, slot = b // 3, b % 3, b % 2
            d = -4 * half
            e = -8 * kind
            r0, c0 = 11 - d, 31 - e
            for h in range(2):
                back, tile = LAST_BIAS_USE[b]
                pool.wait_ge(logit_done, j * B_STEPS + (STEPS_A - back * B_STEPS + 2 * tile + h + 1))
                src = tab[h][:, :].rearrange("p (r c) -> p r c", c=TAB_C)
                src = src[:, r0 - KEY_ROWS + 1:r0 + 1, c0 - KEY_COLS + 1:c0 + 1][:, ::-1, ::-1]
                dst = bias[:, h, slot, 0:LAT_KEYS].rearrange("p (r c) -> p r c", c=KEY_COLS)
                cm = col_mask[:, kind, :].rearrange("p (a c) -> p a c", a=1).to_broadcast([P, KEY_ROWS, KEY_COLS])
                rm = row_mask[:, half, :].rearrange("p (r a) -> p r a", a=1).to_broadcast([P, KEY_ROWS, KEY_COLS])
                step(pool.tensor_tensor(dst, src, cm, ALU.add))
                pool.tensor_tensor(dst, dst, rm, ALU.add).then_inc(bias_ready, 1)

        with pool.Fori(0, PAIRS) as j:
            step.begin(j, 2 * B_BUILDS)
            pool.wait_ge(tab_loaded, (j + 1) * 32)
            for b in range(2):
                bias_tile(j, b)
            for l, end in enumerate((2, 5, 8, 10)):
                split(4 * j + (B_UNIT + 2 + l), l % 2,
                      loads(2 * j + (B_UNIT + 2 + l) // 2), 10 * j + (B_CHUNK + end))
            for b in range(2, B_BUILDS):
                bias_tile(j, b)
        step.end(PAIRS)
        with pool.Fori(0, KT // 2 - 1) as i:
            for l in range(2):
                split(2 * i + (BO_UNIT + 2 + l), l, loads(i + (BO_UNIT + 2) // 2),
                      4 * i + (BO_CHUNK + 2 + 2 * l))
        last = S // P + TC // P
        pool.wait_ge(ctx_loaded, 16 * 6)
        with pool.Fori(0, S // P // 2) as i:
            for s in range(2):
                t = 2 * i + (last + s)
                pool.wait_ge(ln_var, t + 1)
                after(pool, ln_norm, t - 1)
                pool.tensor_tensor(rstd[:, s:s + 1], var_eps[:, s:s + 1], minus_half[:, :],
                                   ALU.pow).then_inc(ln_rstd, 1)
                pool.wait_ge(out_scaled, 2 * i + (s + 1))
                pool.tensor_tensor(out_tile[:, s, :], out_tile[:, s, :], b_row[:, :], ALU.add).then_inc(out_ready, 1)

    @block.tensor
    def _(pe):
        def product(out, w, x, first, last):
            (wh, wl), (xh, xl) = w, x
            pe.matmul(out, wh, xh, start=first, stop=False)
            pe.matmul(out, wh, xl, start=False, stop=False)
            return pe.matmul(out, wl, xh, start=False, stop=last)

        def project(n, slot, half, l0, x_hi, x_lo, chunks, kts=KT):
            pe.wait_ge(w_split, n + 1)
            l = l0
            for o in range(KT // kts):
                for t0, tn in chunks:
                    after(pe, pj_free[l % 2], half + l // 2)
                    out = pj[l % 2][:, 0:tn]
                    for k in range(kts):
                        w = (o * kts + k) * P
                        mm = product(out, (w_hi[:, slot, w:w + P], w_lo[:, slot, w:w + P]),
                                     (x_hi[:, k, t0:t0 + tn], x_lo[:, k, t0:t0 + tn]), k == 0, k == kts - 1)
                    mm.then_inc(pj_done, 1)
                    l += 1

        start_at_one(pe, x_split, 1, (ada_done, ln_back, pv_done))
        pe.wait_ge(x_split, KT)
        pe.wait_ge(c_ready, 1)
        with pe.Fori(0, GROUPS) as g:
            def modulation(l):
                n = g * ADA + l
                pe.wait_ge(ada_loaded, n * 16 + 16)
                if l >= 2:
                    pe.wait_ge(ada_free, n - 1)
                for k in range(KT):
                    mm = pe.matmul(bank(4 + l % 2)[:, 0:2], w_ada[:, k * P:(k + 1) * P], c_silu[:, k, :],
                                   start=(k == 0), stop=(k == KT - 1))
                mm.then_inc(ada_done, 1)

            l = 0
            for u in range(L1_UNITS):
                if u == 8:
                    pe.wait_ge(m_split, g * 4 + 4)
                if u == 10:
                    pe.wait_ge(g_split, g * 4 + 4)
                n, half = g * L1_UNITS + u, g * (L1_CHUNKS // 2)
                if u < 8:
                    project(n, u % 2, half, l, x_hi, x_lo, LAT_CHUNKS)
                    l += 2
                else:
                    project(n, u % 2, half, l, *((m_hi, m_lo) if u < 10 else (g_hi, g_lo)), LAT_CHUNKS, kts=4)
                    l += 4
                if u < ADA:
                    modulation(u)

        def normalise(first, tiles, back=True):
            def to_rows(t, s):
                pe.wait_ge(ln_tile, t + 1)
                if not isinstance(t, int) or t >= 2:
                    after(pe, ln_norm, t - 1)
                for k in range(KT):
                    tr = pe.transpose(bank(2 * s, 2)[:, k * P:(k + 1) * P], z_tile[:, s, k * P:(k + 1) * P], ident[:, :])
                tr.then_inc(ln_turned, 1)

            def to_columns(t, s):
                after(pe, ln_norm, t + 1)
                if not isinstance(t, int) or t >= 1:
                    after(pe, ln_stored, t)
                for k in range(KT):
                    tr = pe.transpose(ps_pt[:, k * P:(k + 1) * P], x_hat[:, s, k * P:(k + 1) * P], ident[:, :])
                tr.then_inc(ln_back, 1)

            if not back:
                with pe.Fori(0, tiles // 2) as i:
                    for s in range(2):
                        to_rows(2 * i + (first + s), s)
                return
            to_rows(first, 0)
            with pe.Fori(0, tiles // 2 - 1) as i:
                to_rows(2 * i + (first + 1), 1)
                to_columns(2 * i + first, 0)
                to_rows(2 * i + (first + 2), 0)
                to_columns(2 * i + (first + 1), 1)
            to_rows(first + tiles - 1, 1)
            to_columns(first + tiles - 2, 0)
            to_columns(first + tiles - 1, 1)

        normalise(0, S // P)

        def values(vt, sets, base, v_base):
            for n, tiles in enumerate(sets):
                if n >= 2:
                    pe.wait_ge(v_ready, v_base + (n - 1))
                for i, t in enumerate(tiles):
                    tr = pe.transpose(bank(4 + n % 2)[:, i * P:(i + 1) * P], vt[:, t * P:(t + 1) * P], ident[:, :])
                tr.then_inc(v_turned, 1)

        def wait_read(counts):
            for b, v in counts.items():
                after(pe, pj_free[b], v)

        def attention(h0, p0, steps, scores, width, keys, prob, prob_t, v, o_sb):
            def score(s):
                if s >= 2:
                    pe.wait_ge(logit_done, h0 + (s - 1))
                mm = None
                for mm in scores(s):
                    pass
                mm.then_inc(score_done, 1)

            def turn_probs(s):
                pe.wait_ge(prob_done, h0 + (s + 1))
                after(pe, pt_dve, h0 + s)
                after(pe, pt_act, h0 + s)
                c0 = width(s)
                for c in range((KEYS - c0) // P):
                    at = c * P if c < (KEYS - c0) // P - 1 else HALF
                    tr = pe.transpose(ps_pt[:, at:at + P], prob[s % 2][:, c0 + c * P:c0 + (c + 1) * P], ident[:, :])
                tr.then_inc(pt_done, 1)

            def outputs(s):
                after(pe, pt_dve, h0 + (s + 1))
                after(pe, pt_act, h0 + (s + 1))
                after(pe, o_done, h0 + s)
                h, tiles = s % 2, keys(s)
                for c, t in enumerate(tiles):
                    mm = pe.matmul(ps_o[:, 0:HD], prob_t[:, c * P:(c + 1) * P], v[:, t, h * HD:(h + 1) * HD],
                                   start=(c == 0), stop=(c == len(tiles) - 1))
                mm.then_inc(pv_done, 1)

            def turn_output(p):
                after(pe, o_done, h0 + (2 * p + 2))
                after(pe, gated, p0 + p)
                pe.transpose(ps_ot[:, 0:P], o_sb[:, p % 2, :], ident[:, :]).then_inc(ot_done, 1)

            score(0)
            score(1)
            for s in range(steps):
                turn_probs(s)
                if s + 2 < steps:
                    score(s + 2)
                outputs(s)
                if s >= 2 and s % 2 == 0:
                    turn_output(s // 2 - 1)
            turn_output(steps // 2 - 1)

        def a_scores(s):
            t, h = s // 2, s % 2
            r = slice(h * HD, (h + 1) * HD)
            out, (_, parts, _, _) = ps_score[h], a_tile(t)
            for c, k0, n in parts:
                yield product(out[:, c:c + n], (aq_hi[r, t * P:(t + 1) * P], aq_lo[r, t * P:(t + 1) * P]),
                              (ak_hi[r, k0:k0 + n], ak_lo[r, k0:k0 + n]), True, True)

        after(pe, mod_split, KT)
        for m in range(2):
            n, c = A_UNIT + 10 * m, A_CHUNK + 30 * m
            if m:
                after(pe, o_done, 4 * A_STEPS)
                after(pe, gated, 4 * A_TILES)
            project(n, 0, c // 2, 0, u_hi, u_lo, ALL_CHUNKS)
            project(n + 1, 1, c // 2, 3, u_hi, u_lo, ALL_CHUNKS)
            wait_read(free_counts(c // 2, 3, 3))
            values(a_tmp, [range(0, 4), range(4, 8), range(8, 10)], VSETS_A * m, VSETS_A * m)
            with pe.Fori(0, 4) as i:
                half = 3 * i + (c // 2 + 3)
                h0, p0 = i * A_STEPS + 4 * m * A_STEPS, i * A_TILES + 4 * m * A_TILES
                after(pe, o_done, h0)
                after(pe, gated, p0)
                project(2 * i + (n + 2), 0, half, 0, u_hi, u_lo, ALL_CHUNKS)
                project(2 * i + (n + 3), 1, half, 3, u_hi, u_lo, ALL_CHUNKS)
                pe.wait_ge(k_split, m + 1)
                pe.wait_ge(q_split, i + (4 * m + 1))
                pe.wait_ge(v_ready, VSETS_A * (m + 1))
                wait_read(free_counts(half, 0, 6))
                attention(h0, p0, A_STEPS, a_scores, lambda s: a_tile(s // 2)[0], lambda s: a_tile(s // 2)[2],
                          aprob, aprob_t, av, ao_sb)

        def output_projection(n, c, chunks, layer):
            pe.wait_ge(o_split, KT * (layer + 1))
            count = 2 * len(chunks)
            with pe.Fori(0, KT // 2) as i:
                for s in range(2):
                    project(2 * i + (n + s), s, (count // 2) * i + c // 2, s * len(chunks), u_hi, u_lo, chunks)

        output_projection(AO_UNIT, AO_CHUNK, ALL_CHUNKS, 0)
        normalise(S // P, TC // P)

        def b_scores(s):
            t, h = s // 2, s % 2
            half, cb = t // 4, t % 4
            r = slice(h * HD, (h + 1) * HD)
            q = bq_hi[r, t * P:(t + 1) * P], bq_lo[r, t * P:(t + 1) * P]

            def near(k):
                return k[r, 0:S].rearrange("p (r c) -> p r c", c=GRID)[
                    :, 4 * half:4 * half + KEY_ROWS, KEY_COL[cb]:KEY_COL[cb] + KEY_COLS]

            out = ps_score[h]
            yield product(out[:, 0:LAT_KEYS], q, (near(bk_hi), near(bk_lo)), True, True)
            for n in range(2):
                c, k = LAT_KEYS + n * P, slice(S + n * P, S + (n + 1) * P)
                yield product(out[:, c:c + P], q, (bk_hi[r, k], bk_lo[r, k]), True, True)

        def b_keys(s):
            half, cb = s // 2 // 4, s // 2 % 4
            return [cb * 4 + half + n for n in range(3)] + [16, 17]

        after(pe, mod_split, 2 * KT)
        with pe.Fori(0, PAIRS) as j:
            n, half = 4 * j + B_UNIT, 5 * j + B_CHUNK // 2
            h0, p0 = j * B_STEPS + STEPS_A, j * B_TILES + OT_A
            after(pe, o_done, h0)
            after(pe, gated, p0)
            project(n, 0, half, 0, u_hi, u_lo, LAT_CHUNKS)
            project(n + 1, 1, half, 2, u_hi, u_lo, ALL_CHUNKS)
            project(n + 2, 0, half, 5, u_hi, u_lo, ALL_CHUNKS)
            wait_read(free_counts(half, 5, 3))
            v0 = j * VSETS_B + 2 * VSETS_A
            values(b_vt, [range(0, 4), range(4, 8), range(8, 12), range(12, 16), range(16, 18)], v0, v0)
            project(n + 3, 1, half, 8, u_hi, u_lo, LAT_CHUNKS)
            pe.wait_ge(k_split, j + 3)
            pe.wait_ge(q_split, j + (PAIRS + 1))
            pe.wait_ge(v_ready, v0 + VSETS_B)
            wait_read(free_counts(half, 0, 10))
            attention(h0, p0, B_STEPS, b_scores, lambda s: 0, b_keys, bprob, bprob_t, bv, bo_sb)
        output_projection(BO_UNIT, BO_CHUNK, LAT_CHUNKS, 1)
        normalise(S // P + TC // P, S // P, back=False)

    @block.scalar
    def _(act):
        loads = [(ident[:, :], a["ident"]), (vecs[:, :], a["vecs"]), (c_in[:, :, :], a["c_t"]),
                 (corr[:, :, :], a["corr"]), (row_mask[:, :, :], a["row_mask"]), (col_mask[:, :, :], a["col_mask"]),
                 (sink_neg[:, :], bass.AP(tensor=a["sink"].tensor, offset=0, ap=[[0, P], [1, HEADS]]))]
        for dst, src in loads:
            act.dma_start(dst, src).then_inc(const_loaded, 16)

        def wait_chunk(c):
            act.wait_ge(pj_done, c + 1)

        start_at_one(act, x_loaded[0], 16, (*pj_free, ln_stored, pt_act, o_done))
        for k in range(KT):
            act.wait_ge(x_loaded[k], 16)
            act.activation(x_hi[:, k, :], act_buf[:, k, 0:S], ACT.Copy).then_inc(x_hi_done, 1)
        act.wait_ge(const_loaded, 16 * len(loads))
        act.activation(c_silu[:, :, :], c_in[:, :, :], ACT.Silu).then_inc(c_ready, 1)
        for k in range(KT):
            act.wait_ge(x_split, k + 1)
            act.activation(act_buf[:, k, 0:S], act_buf[:, k, 0:S], ACT.Copy, scale=ALPHA_1).then_inc(x_scaled, 1)
        with act.Fori(0, GROUPS) as g:
            c, half = g * L1_CHUNKS, g * (L1_CHUNKS // 2)
            for i in range(4):
                after(act, u_used, g * 4 + i)
                for h in range(2):
                    wait_chunk(c + (2 * i + h))
                    act.activation(u_pad[:, PAD + h * HALF:PAD + (h + 1) * HALF], pj[h], ACT.Copy).then_inc(pj_free[h], 1)
            for i in range(4):
                for h in range(2):
                    wait_chunk(c + (8 + 2 * i + h))
                    act.activation(gate_tile(i)[:, 2 * h:2 * h + 2, :], pj[h].rearrange("p (a b) -> p a b", b=C),
                                   ACT.Silu).then_inc(pj_free[h], 1)
            for i in range(4):
                for b, v in free_counts(half, 16 + 2 * i, 2).items():
                    after(act, pj_free[b], v)
                act.activation(g_hi[:, i, :].rearrange("p (a b) -> p a b", b=C), gate_tile(i), ACT.Copy).then_inc(g_hi_done, 1)

        def normalise(first, tiles, back=True):
            def set_out(t, s, col0):
                if not isinstance(t, int) or t >= 2:
                    act.wait_ge(ln_turned, t - 1)
                act.activation(z_tile[:, s, :].rearrange("p (k n) -> p k n", n=P), act_buf[:, :, bass.ds(col0, P)],
                               ACT.Copy).then_inc(ln_tile, 1)

            def take(t, col0):
                after(act, ln_back, t + 1)
                act.activation(act_buf[:, :, bass.ds(col0, P)], ps_pt[:, :].rearrange("p (k n) -> p k n", n=P),
                               ACT.Copy).then_inc(ln_stored, 1)

            if not back:
                with act.Fori(0, tiles // 2) as i:
                    for s in range(2):
                        set_out(2 * i + (first + s), s, i * (2 * P) + s * P)
                return
            for s in range(2):
                set_out(first + s, s, s * P)
            with act.Fori(0, tiles // 2 - 1) as i:
                for s in range(2):
                    set_out(2 * i + (first + 2 + s), s, i * (2 * P) + (2 + s) * P)
                    take(2 * i + (first + s), i * (2 * P) + s * P)
            for s in range(2):
                take(first + tiles - 2 + s, (tiles - 2 + s) * P)

        def wait_sums(c):
            for b in range(2):
                after(act, pj_free[b], c // 2)

        def modulate(layer):
            act.wait_ge(par_ready, layer + 1)
            if layer == 0:
                act.wait_ge(ctx_loaded, 16 * 4)
            after(act, ln_stored, (S // P, S // P + TC // P)[layer])
            q = 6 * layer
            with act.Fori(0, KT // 2) as i:
                for s in range(2):
                    k = 2 * i + s
                    if layer or s:
                        after(act, mod_split, 2 * i + (layer * KT + s - 1))
                    elif s == 0:
                        after(act, mod_split, 2 * i)
                    for lo, hi, f in ((0, S, 0), (S, TC, 2)):
                        ins = act.activation(u_tmp[:, s, lo:hi], col(act_buf, k, lo, hi), ACT.Identity,
                                             scale=par[:, q + f, bass.ds(k, 1)], bias=par[:, q + f + 1, bass.ds(k, 1)])
                    ins.then_inc(mod_done, 1)

        def take_projection(c, half, l0, chunks, dst, func=ACT.Copy, scale=1.0):
            for n, (t0, tn) in enumerate(chunks):
                l = l0 + n
                wait_chunk(c + l)
                act.activation(dst[:, t0:t0 + tn], pj[l % 2][:, 0:tn], func, scale=scale).then_inc(pj_free[l % 2], 1)

        def softmax(h0, p0, steps, width, end, logits, prob, prob_t, o_sb):
            def probs(s):
                act.wait_ge(logit_done, h0 + (s + 1))
                if s >= 2:
                    act.wait_ge(pt_done, h0 + (s - 1))
                    act.wait_ge(rec_done, h0 + (s - 1))
                act.activation(prob[s % 2][:, width(s):end], logits[s % 2][:, width(s):end], ACT.Exp, scale=-1.0,
                               bias=neg_max[:, s % 2:s % 2 + 1], accum_out=row_sum[:, s % 2:s % 2 + 1]).then_inc(prob_done, 1)

            def take_last(s):
                act.wait_ge(pt_done, h0 + (s + 1))
                after(act, pv_done, h0 + s)
                c = KEYS - width(s) - P
                act.activation(prob_t[:, c:c + P], ps_pt[:, HALF:HALF + P], ACT.Copy).then_inc(pt_act, 1)

            def take_output(s):
                p, h = s // 2, s % 2
                after(act, pv_done, h0 + (s + 1))
                act.wait_ge(rec_done, h0 + (s + 1))
                if p >= 2:
                    act.wait_ge(ot_done, p0 + (p - 1))
                act.activation(o_sb[:, p % 2, h * HD:(h + 1) * HD], ps_o[:, 0:HD], ACT.Copy,
                               scale=row_rec[:, h:h + 1]).then_inc(o_done, 1)

            probs(0)
            probs(1)
            for s in range(steps):
                take_last(s)
                if s + 2 < steps:
                    probs(s + 2)
                take_output(s)

        def split_outputs(layer, tokens, tiles):
            after(act, gated, tiles)
            with act.Fori(0, KT) as k:
                act.activation(col(u_hi, k, 0, tokens), col(act_buf, k, 0, tokens), ACT.Copy).then_inc(o_hi_done, 1)

        wait_sums(A_CHUNK)
        normalise(0, S // P)
        modulate(0)
        for m in range(2):
            c = A_CHUNK + 30 * m
            take_projection(c, c // 2, 0, ALL_CHUNKS, a_tmp)
            act.wait_ge(k_split, m + 1)
            take_projection(c, c // 2, 3, ALL_CHUNKS, a_tmp)
            if m == 0:
                act.wait_ge(res_stored, 16 * KT)
            with act.Fori(0, 4) as i:
                ci = 6 * i + (c + 6)
                act.wait_ge(v_turned, VSETS_A * (m + 1))
                h0, p0 = i * A_STEPS + 4 * m * A_STEPS, i * A_TILES + 4 * m * A_TILES
                after(act, pv_done, h0)
                take_projection(ci, None, 0, ALL_CHUNKS, a_tmp, scale=Q_SCALE)
                take_projection(ci, None, 3, ALL_CHUNKS, col(act_buf, i + 4 * m), func=ACT.Silu)
                softmax(h0, p0, A_STEPS, lambda s: a_tile(s // 2)[0], KEYS + 1, alog, aprob, aprob_t, ao_sb)
        split_outputs(0, TC, OT_A)
        residual_loads(act, 0, AO_CHUNK, ALL_CHUNKS)
        wait_sums(B_CHUNK)
        normalise(S // P, TC // P)
        modulate(1)
        act.wait_ge(res_stored, 16 * 2 * KT)
        with act.Fori(0, PAIRS) as j:
            c = 10 * j + B_CHUNK
            h0, p0 = j * B_STEPS + STEPS_A, j * B_TILES + OT_A
            after(act, pv_done, h0)
            for h in range(2):
                wait_chunk(c + h)
                act.activation(b_tmp_q[:, h * HALF:(h + 1) * HALF].rearrange("p (b r c) -> p b r c", b=4, r=8),
                               pj[h].rearrange("p (r b c) -> p b r c", b=4, r=8), ACT.Copy,
                               scale=Q_SCALE).then_inc(pj_free[h], 1)
            take_projection(c, None, 2, ALL_CHUNKS, b_tmp_k)
            act.wait_ge(k_split, j + 3)
            for n, (t0, tn) in enumerate(ALL_CHUNKS):
                l = 5 + n
                wait_chunk(c + l)
                if n < 2:
                    src = pj[l % 2].rearrange("p (r c) -> p r c", c=GRID)
                    for cb in range(4):
                        dst = b_vt[:, cb * HALF + n * C:cb * HALF + (n + 1) * C].rearrange("p (r c) -> p r c", c=KEY_COLS)
                        ins = act.activation(dst, src[:, :, KEY_COL[cb]:KEY_COL[cb] + KEY_COLS], ACT.Copy)
                else:
                    ins = act.activation(b_vt[:, 4 * HALF:4 * HALF + C], pj[l % 2][:, 0:tn], ACT.Copy)
                ins.then_inc(pj_free[l % 2], 1)
            take_projection(c, None, 8, LAT_CHUNKS, col(act_buf, j, 0, S), func=ACT.Silu)
            softmax(h0, p0, B_STEPS, lambda s: 0, KEYS, blog, bprob, bprob_t, bo_sb)
        split_outputs(1, S, OT_A + PAIRS * B_TILES)
        residual_loads(act, 1, BO_CHUNK, LAT_CHUNKS)
        wait_sums(BO_CHUNK + 2 * KT)
        normalise(S // P + TC // P, S // P, back=False)

    @block.vector
    def _(dve):
        step = Chain(dve, dve_step)

        def wait_chunk(c):
            dve.wait_ge(pj_done, c + 1)

        start_at_one(dve, x_loaded[0], 16, (u_used, ln_norm, mod_split, pt_dve, gated))
        dve.wait_ge(const_loaded, 16 * 7)
        step(dve.tensor_scalar(sink_neg[:, :], sink_neg[:, :], -1.0, None, ALU.mult))
        for k in range(KT):
            dve.wait_ge(x_hi_done, k + 1)
            dve.tensor_tensor(x_lo[:, k, :], act_buf[:, k, 0:S], x_hi[:, k, :].bitcast(F32), ALU.subtract).then_inc(x_split, 1)

        def window(g, i):
            w, half = WINDOWS[g], g * (L1_CHUNKS // 2)
            for b, v in free_counts(half, 2 * i, 2).items():
                after(dve, pj_free[b], v)
            src, lo, sh = u_pad, 0, 1
            for n in range(g + 1):
                dst = win[n % 2]
                lo += sh
                step(dve.tensor_tensor(dst[:, lo:PAD + S], src[:, lo:PAD + S], src[:, lo - sh:PAD + S - sh], ALU.add))
                src, sh = dst, 2 * sh
            step(dve.tensor_tensor(src[:, PAD:2 * PAD], src[:, PAD:2 * PAD], corr[:, g, :], ALU.mult))
            m = win[(g + 1) % 2]
            dve.scalar_tensor_tensor(m[:, PAD:], src[:, PAD:], 1.0 / w, u_pad[:, PAD:], ALU.mult,
                                     ALU.subtract).then_inc(u_used, 1)
            after(dve, u_used, 4 * g + i + 1)
            step(dve.tensor_copy(m_hi[:, i, :], m[:, PAD:]))
            dve.tensor_tensor(m_lo[:, i, :], m[:, PAD:], m_hi[:, i, :].bitcast(F32), ALU.subtract).then_inc(m_split, 1)
            dve.wait_ge(m_split, 4 * g + i + 1)

        def modulation(n):
            after(dve, ada_done, n + 1)
            dve.tensor_scalar(ada[:, n, :], bank(4 + n % 2)[:, 0:2], b_ada[:, n:n + 1], None, ALU.add).then_inc(ada_free, 1)

        for g in range(GROUPS):
            c = g * L1_CHUNKS
            step(dve.memset(u_pad[:, 0:PAD], 0.0))
            for i in range(4):
                window(g, i)
                modulation(ADA * g + i)
            for i in range(4, 8):
                modulation(ADA * g + i)
            for i in range(4):
                for h in range(2):
                    wait_chunk(c + 16 + 2 * i + h)
                    gt = gate_tile(i)[:, 2 * h:2 * h + 2, :]
                    dve.scalar_tensor_tensor(gt, pj[h].rearrange("p (a b) -> p a b", b=C), pool_scale[:, 4 * g + i:4 * g + i + 1],
                                             gt, ALU.mult, ALU.mult).then_inc(pj_free[h], 1)
                if i == 1:
                    modulation(ADA * g + 8)
                if i % 2:
                    for n in (i - 1, i):
                        dve.wait_ge(g_hi_done, 4 * g + n + 1)
                        dve.tensor_tensor(g_lo[:, n, :].rearrange("p (a b) -> p a b", b=C), gate_tile(n),
                                          g_hi[:, n, :].bitcast(F32).rearrange("p (a b) -> p a b", b=C),
                                          ALU.subtract).then_inc(g_split, 1)
            modulation(ADA * g + 9)
            if g == 0:
                dve.wait_ge(x_scaled, KT)
            for o in range(KT):
                for h in range(2):
                    wait_chunk(c + 24 + 2 * o + h)
                    y = act_buf[:, o, h * HALF:(h + 1) * HALF]
                    dve.tensor_tensor(y, pj[h], y, ALU.add).then_inc(pj_free[h], 1)
                if o in (1, 3):
                    modulation(ADA * g + 10 + o // 2)

        dve.wait_ge(ada_free, ADA_UNITS)
        for layer, g, b in ((0, ln_g1, ln_b1), (1, ln_g2, ln_b2)):
            n, q = 24 * layer, 6 * layer
            for who in range(2):
                shift, scale = ada[:, n:n + KT, who], ada[:, n + KT:n + 2 * KT, who]
                f, o = par[:, q + 2 * who, :], par[:, q + 2 * who + 1, :]
                if layer == 0 and who == 1:
                    step(dve.tensor_scalar(f, scale, 1.0, None, ALU.add))
                    step(dve.tensor_copy(o, shift))
                    continue
                step(dve.tensor_scalar(f, scale, 1.0, None, ALU.add))
                step(dve.tensor_tensor(o, f, b, ALU.mult))
                step(dve.tensor_tensor(o, o, shift, ALU.add))
                step(dve.tensor_tensor(f, f, g, ALU.mult))
            step(dve.tensor_scalar(par[:, q + 4, :], g, ALPHA_2, None, ALU.mult))
            dve.tensor_scalar(par[:, q + 5, :], b, ALPHA_2, None, ALU.mult).then_inc(par_ready, 1)

        def normalise(first, tiles, last=False):
            with dve.Fori(0, tiles // 2) as i:
                step.begin(i, 6)
                for s in range(2):
                    t = 2 * i + (first + s)
                    rows = bank(2 * s, 2)
                    dve.wait_ge(ln_turned, t + 1)
                    step(dve.bn_stats(stats[:, s, 0:6], rows[:, 0:HALF]))
                    step(dve.bn_stats(stats[:, s, 6:12], rows[:, HALF:D]), dve_waited)
                    step(dve.bn_aggr(mean_var[:, s, :], stats[:, s, :]))
                    dve.tensor_scalar(var_eps[:, s:s + 1], mean_var[:, s, 1:2], LN_EPS, None, ALU.add).then_inc(ln_var, 1)
                    dve.wait_ge(ln_rstd, t + 1)
                    if first or s:
                        if not last:
                            after(dve, ln_back, t - 1)
                    elif not last:
                        after(dve, ln_back, 2 * i)
                    dve.tensor_scalar(x_hat[:, s, :], rows, mean_var[:, s, 0:1], rstd[:, s:s + 1], ALU.subtract,
                                      ALU.mult).then_inc(ln_norm, 1)
                    if last:
                        after(dve, ln_norm, t + 1)
                        dve.wait_ge(out_stored[s], i * 16 + 16)
                        dve.tensor_tensor(out_tile[:, s, :], x_hat[:, s, :], g_row[:, :], ALU.mult).then_inc(out_scaled, 1)
            step.end(tiles // 2)

        def split_modulated(layer):
            with dve.Fori(0, KT // 2) as i:
                for s in range(2):
                    k = 2 * i + s
                    dve.wait_ge(mod_done, 2 * i + (layer * KT + s + 1))
                    dve.tensor_copy(col(u_hi, k), u_tmp[:, s, :]).then_inc(mod_hi, 1)
                    dve.wait_ge(mod_hi, 2 * i + (layer * KT + s + 1))
                    dve.tensor_tensor(col(u_lo, k), u_tmp[:, s, :], col(u_hi, k).bitcast(F32), ALU.subtract).then_inc(mod_split, 1)

        def split_in_two(hi, lo, src, done):
            step(dve.tensor_copy(hi, src))
            dve.tensor_tensor(lo, src, hi.bitcast(F32), ALU.subtract).then_inc(done, 1)

        swap = [(n + 16) % 32 for n in range(32)]

        def rotate():
            step(dve.stream_shuffle(a_swap[:, :], a_tmp[:, 0:S], swap))
            step(dve.tensor_tensor(a_swap[:, :], a_swap[:, :], rope_sin[:, :], ALU.mult))
            step(dve.tensor_tensor(a_tmp[:, 0:S], a_tmp[:, 0:S], rope_cos[:, :], ALU.mult))
            step(dve.tensor_tensor(a_tmp[:, 0:S], a_tmp[:, 0:S], a_swap[:, :], ALU.add))

        def take_values(v, sets, v_base):
            for n, tiles in enumerate(sets):
                dve.wait_ge(v_turned, v_base + (n + 1))
                dve.tensor_copy(v[:, tiles[0]:tiles[-1] + 1, :],
                                bank(4 + n % 2)[:, 0:len(tiles) * P].rearrange("p (t n) -> p t n", n=P)).then_inc(v_ready, 1)

        def softmax(h0, p0, steps, width, mask, start, prob_t, logits, ready, gate):
            def logit(s):
                if s >= 2:
                    dve.wait_ge(prob_done, h0 + (s - 1))
                ready(s)
                dve.wait_ge(score_done, h0 + (s + 1)).then_inc(dve_waited, 1)
                c0 = width(s)
                dve.tensor_tensor_reduce(logits[s % 2][:, c0:KEYS], ps_score[s % 2][:, c0:KEYS], mask(s), -1.0, start(s),
                                         ALU.add, ALU.min, neg_max[:, s % 2:s % 2 + 1]).then_inc(logit_done, 1)

            def take_probs(s):
                dve.wait_ge(pt_done, h0 + (s + 1))
                after(dve, pv_done, h0 + s)
                n = KEYS - width(s) - P
                dve.tensor_copy(prob_t[:, 0:n], ps_pt[:, 0:n]).then_inc(pt_dve, 1)

            def reciprocal(s):
                dve.wait_ge(prob_done, h0 + (s + 1))
                if s >= 2:
                    after(dve, o_done, h0 + (s - 1))
                dve.reciprocal(row_rec[:, s % 2:s % 2 + 1], row_sum[:, s % 2:s % 2 + 1]).then_inc(rec_done, 1)

            def gate_output(p):
                dve.wait_ge(ot_done, p0 + (p + 1))
                gate(p)

            logit(0)
            logit(1)
            for s in range(steps):
                take_probs(s)
                if s + 2 < steps:
                    logit(s + 2)
                reciprocal(s)
                if s >= 2 and s % 2 == 0:
                    gate_output(s // 2 - 1)
            gate_output(steps // 2 - 1)

        def split_outputs(layer, tokens):
            with dve.Fori(0, KT) as k:
                dve.wait_ge(o_hi_done, k + (layer * KT + 1))
                dve.tensor_tensor(col(u_lo, k, 0, tokens), col(act_buf, k, 0, tokens),
                                  col(u_hi, k, 0, tokens).bitcast(F32), ALU.subtract).then_inc(o_split, 1)

        def residual_sums(layer, c, chunks):
            if layer == 0:
                dve.wait_ge(o_split, KT)
            else:
                dve.wait_ge(o_split, 2 * KT)
            count = len(chunks)
            with dve.Fori(0, KT // 2) as i:
                for s in range(2):
                    o = 2 * i + s
                    dve.wait_ge(res_loaded[s], i * 16 + (layer * 16 * (KT // 2) + 16))
                    for n, (t0, tn) in enumerate(chunks):
                        l = s * count + n
                        wait_chunk(2 * count * i + (c + l))
                        g = ada[:, bass.ds(o + (24 * layer + 16), 1), n // 2].rearrange("p a -> p a")
                        dve.scalar_tensor_tensor(col(act_buf, o, t0, t0 + tn), pj[l % 2][:, 0:tn], g, res[:, s, t0:t0 + tn],
                                                 ALU.mult, ALU.add).then_inc(pj_free[l % 2], 1)

        normalise(0, S // P)
        split_modulated(0)
        dve.wait_ge(ctx_loaded, 16 * 4)
        for m in range(2):
            c = A_CHUNK + 30 * m
            for b, v in free_counts(c // 2, 0, 3).items():
                after(dve, pj_free[b], v)
            rotate()
            split_in_two(ak_hi[:, :], ak_lo[:, :], a_tmp[:, :], k_split)
            take_values(av, [range(0, 4), range(4, 8), range(8, 10)], VSETS_A * m)
            with dve.Fori(0, 4) as i:
                step.begin(i, 6)
                half = 3 * i + (c // 2 + 3)
                h0, p0 = i * A_STEPS + 4 * m * A_STEPS, i * A_TILES + 4 * m * A_TILES
                for b, v in free_counts(half, 0, 3).items():
                    after(dve, pj_free[b], v).then_inc(dve_waited, 1)
                rotate()
                split_in_two(aq_hi[:, :], aq_lo[:, :], a_tmp[:, :], q_split)
                dve.wait_ge(q_split, i + (4 * m + 1))
                for h in range(2):
                    ins = dve.tensor_copy(alog[h][:, KEYS:KEYS + 1], sink_neg[:, bass.ds(2 * i + (8 * m + h), 1)])
                step(ins)

                def gate(p, i=i, m=m):
                    y = col(act_buf, i + 4 * m, p * P, (p + 1) * P)
                    dve.tensor_tensor(y, ps_ot[:, 0:P], y, ALU.mult).then_inc(gated, 1)

                softmax(h0, p0, A_STEPS, lambda s: a_tile(s // 2)[0],
                        lambda s: a_mask[:, a_tile(s // 2)[3]:a_tile(s // 2)[3] + KEYS - a_tile(s // 2)[0]],
                        lambda s: alog[s % 2][:, KEYS:KEYS + 1], aprob_t, alog, lambda s: None, gate)
            step.end(4)
        split_outputs(0, TC)
        residual_sums(0, AO_CHUNK, ALL_CHUNKS)
        normalise(S // P, TC // P)
        split_modulated(1)
        with dve.Fori(0, PAIRS) as j:
            step.begin(j, 2)
            half = 5 * j + B_CHUNK // 2
            h0, p0 = j * B_STEPS + STEPS_A, j * B_TILES + OT_A
            for b, v in free_counts(half, 0, 2).items():
                after(dve, pj_free[b], v)
            split_in_two(bq_hi[:, :], bq_lo[:, :], b_tmp_q[:, :], q_split)
            for b, v in free_counts(half, 2, 3).items():
                after(dve, pj_free[b], v)
            split_in_two(bk_hi[:, :], bk_lo[:, :], b_tmp_k[:, :], k_split)
            take_values(bv, [range(0, 4), range(4, 8), range(8, 12), range(12, 16), range(16, 18)],
                        j * VSETS_B + 2 * VSETS_A)

            def built(s):
                t, h = s // 2, s % 2
                b = 3 * (t // 4) + COL_TYPE[t % 4]
                dve.wait_ge(bias_ready, j * (2 * B_BUILDS) + (2 * b + h + 1))

            def bias_of(s):
                t, h = s // 2, s % 2
                return bias[:, h, (3 * (t // 4) + COL_TYPE[t % 4]) % 2, :]

            def gate(p):
                h, cb = p // 4, p % 4
                y = act_buf[:, bass.ds(j, 1), h * HALF:(h + 1) * HALF].rearrange("p a (r c) -> p (a r) c", c=GRID)
                y = y[:, :, cb * 16:(cb + 1) * 16]
                dve.tensor_tensor(y, ps_ot[:, 0:P].rearrange("p (r c) -> p r c", c=16), y, ALU.mult).then_inc(gated, 1)

            softmax(h0, p0, B_STEPS, lambda s: 0, bias_of, lambda s: NO_MAX, bprob_t, blog, built, gate)
        step.end(PAIRS)
        split_outputs(1, S)
        residual_sums(1, BO_CHUNK, LAT_CHUNKS)
        dve.wait_ge(ctx_loaded, 16 * 6)
        normalise(S // P + TC // P, S // P, last=True)

    ctx.close()


def columns_of(w, cols):
    return w[:, cols].reshape(KT, P, P).transpose(1, 0, 2).reshape(P, UNIT)


def four_tiles(w, ot):
    return w[:, ot * P:(ot + 2) * P].reshape(4, P, 2, P).transpose(1, 2, 0, 3).reshape(P, UNIT)


def weight_units(w_in, w_grp, w_out, a_in, a_out, b_in, b_out):
    units, span = [], np.arange(P)
    width = GROUPS * HALF
    for g in range(GROUPS):
        units += [columns_of(w_in, g * HALF + i * P + span) for i in range(4)]
        units += [columns_of(w_in, width + g * HALF + i * P + span) for i in range(4)]
        units += [four_tiles(w_grp[g], ot) for ot in (0, 2)]
        units += [four_tiles(w_out[g * HALF:(g + 1) * HALF], ot) for ot in (0, 2, 4, 6)]
    pairs = np.concatenate([pair_heads(jj) for jj in range(PAIRS)])
    for m in range(2):
        units += [columns_of(a_in, D + m * P + span), columns_of(a_in, D + 2 * P + m * P + span)]
        for i in range(4):
            heads = pair_heads(4 * m + i)
            units += [columns_of(a_in, heads), columns_of(a_in, D + 4 * P + heads)]
    units += [columns_of(a_out[pairs], ot * P + span) for ot in range(KT)]
    for j in range(PAIRS):
        units += [columns_of(b_in, part * D + j * P + span) for part in range(4)]
    units += [columns_of(b_out, ot * P + span) for ot in range(KT)]
    assert len(units) == ALL_UNITS
    return np.stack(units)


def pair_heads(jj):
    m, i = jj // 4, jj % 4
    return np.concatenate([(8 * m + 4 * h + i) * HD + np.arange(HD) for h in range(2)])


def turned(x):
    return x.T.reshape(KT, P, -1).transpose(1, 0, 2)


def by_feature(v):
    return v.reshape(-1, P).T


def shape_tables():
    t = {"ident": np.eye(P)}
    n = np.arange(PAD)
    t["corr"] = np.broadcast_to(np.stack([w / np.minimum(n + 1, w) for w in WINDOWS]), (P, GROUPS, PAD))
    p = np.arange(P)
    rr, qq = p // 16, p % 16
    row_mask = np.zeros((P, 2, KEY_ROWS))
    for half in range(2):
        first = np.clip(8 * half + rr - 4, 0, ROWS - 8)[:, None]
        key = 4 * half + np.arange(KEY_ROWS)
        row_mask[:, half] = np.where((key >= first) & (key < first + 8), 0, MASKED)
    col_mask = np.zeros((P, 3, KEY_COLS))
    for kind, cb in enumerate((0, 1, 3)):
        first = np.clip(cb * 16 + qq - 8, 0, GRID - 16)[:, None]
        key = KEY_COL[cb] + np.arange(KEY_COLS)
        col_mask[:, kind] = np.where((key >= first) & (key < first + 16), 0, MASKED)
    t["row_mask"], t["col_mask"] = row_mask, col_mask
    col = np.arange(P)
    a_mask = np.zeros((P, KEYS))
    a_mask[:, 0:P] = np.where(col[None] >= p[:, None], 0, MASKED)
    a_mask[:, 4 * P:] = np.where(col[None] <= p[:, None], 0, MASKED)
    t["a_mask"] = a_mask
    freq = np.float32(10000.0) ** (-(p % 16).astype(np.float32) / np.float32(16))
    tok = np.arange(S)
    place = np.where((p // 32 % 2 == 0)[:, None], tok // GRID, tok % GRID).astype(np.float32)
    angle = place * freq[:, None]
    t["rope_cos"] = np.cos(angle)
    t["rope_sin"] = np.sin(angle) * np.where(p % 32 < 16, -1, 1)[:, None]
    return t


def kernel(**inputs):
    import concourse.bacc as bacc
    from concourse.bass_utils import run_bass_kernel_spmd

    x = {n: np.asarray(v) for n, v in inputs.items()}
    arrays = shape_tables()
    arrays["weights"] = weight_units(x["pool_w_in"][0], x["pool_w_grp"][0], x["pool_w_out"][0], x["a_w_in_2"][0],
                                     x["a_w_out_2"][0], x["b_w_in_2"][0], x["b_w_out_2"][0])
    arrays["w_ada"] = np.stack([columns_of(x["w_ada_2"][n // 24], (n % 24) * P + np.arange(P)) for n in range(ADA_UNITS)])
    arrays["x_t"], arrays["ctx_t"] = turned(x["x"][0]), turned(x["ctx_2"][0])
    arrays["c_t"] = turned(np.stack([x["c_2"][0], x["c_ctx_2"]]))
    arrays["vecs"] = np.concatenate([by_feature(x[n]) for n in ("ln_g", "ln_b")]
                                    + [by_feature(x[n][0]) for n in ("ln_g_2", "ln_b_2")]
                                    + [by_feature(x["pool_scale"][0]), by_feature(x["b_ada_2"])], axis=1)
    arrays["ln_g3"], arrays["ln_b3"] = x["ln_g_2"][1:2], x["ln_b_2"][1:2]
    arrays["sink"] = x["a_sink_2"][:, [8 * (jj // 4) + 4 * h + jj % 4 for jj in range(PAIRS) for h in range(2)]]
    tab = np.zeros((HEADS, TAB_R, TAB_C), np.float32)
    tab[:, 4:19, 16:47] = x["b_rel_bias_2"][0]
    arrays["bias_tab"] = tab[:, ::-1, ::-1].reshape(HEADS, TAB_R * TAB_C)
    arrays = {n: np.ascontiguousarray(v, dtype=np.float32) for n, v in arrays.items()}

    nc = bacc.Bacc("TRN2", target_bir_lowering=False, num_devices=1)
    aps = {n: nc.dram_tensor(n + "_in", v.shape, F32, kind="ExternalInput").ap() for n, v in arrays.items()}
    aps["out"] = nc.dram_tensor("out", (S // P, P, D), F32, kind="ExternalOutput").ap()
    build(nc, aps)
    r = run_bass_kernel_spmd(nc, [{n + "_in": v for n, v in arrays.items()}], core_ids=[0])
    return r.results[0]["out"].reshape(1, S, D)
```

```python
from contextlib import ExitStack

import numpy as np

import concourse.bass as bass
from concourse import mybir

F32 = mybir.dt.float32
F32R = mybir.dt.float32r
ALU = mybir.AluOpType
ACT = mybir.ActivationFunctionType

P = 128
D = 1024
S = 1024
C = 256
TC = S + C
KT = D // P
HALF = 512
UNIT = KT * P
HD = 64
HEADS = 16
PAIRS = HEADS // 2
Q_SCALE = HD ** -0.5
LN_EPS = 1e-5
ALPHA_1 = 2.0 ** 0.25
ALPHA_2 = 4.0 ** 0.25
MASKED = -1e30
NO_MAX = 3e38
SLOTS = 4

GROUPS = 4
WINDOWS = (2, 4, 8, 16)
PAD = 16
L1_UNITS = 14
L1_CHUNKS = 8 * 2 + 2 * 4 + 4 * 4
L1_ENDS = [2 * (n + 1) for n in range(8)] + [20, 24] + [28, 32, 36, 40]
ADA = 12
ADA_UNITS = 48

A_UNIT = GROUPS * L1_UNITS
AO_UNIT = A_UNIT + 20
B_UNIT = AO_UNIT + KT
BO_UNIT = B_UNIT + 4 * PAIRS
ALL_UNITS = BO_UNIT + KT
A_CHUNK = GROUPS * L1_CHUNKS
AO_CHUNK = A_CHUNK + 20 * 3
B_CHUNK = AO_CHUNK + 8 * 3
BO_CHUNK = B_CHUNK + 10 * PAIRS
LAT_CHUNKS = [(0, HALF), (HALF, HALF)]
ALL_CHUNKS = LAT_CHUNKS + [(S, C)]

A_TILES = S // P + C // P
A_STEPS = 2 * A_TILES
GRID = 64
ROWS = S // GRID
B_TILES = 8
B_STEPS = 2 * B_TILES
KEY_COL = (0, 8, 24, 32)
COL_TYPE = (0, 1, 1, 2)
KEY_ROWS, KEY_COLS = 12, 32
LAT_KEYS = KEY_ROWS * KEY_COLS
KEYS = LAT_KEYS + C
TAB_R, TAB_C = 23, 63
TAB_RUN = TAB_R * TAB_C - (7 * TAB_C + 15)
TAB_ROWS = 16
B_BUILDS = 6
LAST_BIAS_USE = ((1, 6), (1, 7), (0, 0), (0, 2), (0, 3), (0, 4))
STEPS_A = PAIRS * A_STEPS
OT_A = PAIRS * A_TILES
VSETS_A, VSETS_B = 3, 5


def free_counts(first_half, l0, n):
    last = {}
    for l in range(l0, l0 + n):
        last[l % 2] = first_half + (l // 2 + 1)
    return last


class Chain:

    def __init__(self, eng, sem):
        self.eng, self.sem, self.base, self.local, self.at, self.per = eng, sem, 0, 0, 0, 0

    def begin(self, at, per):
        self.base += self.local if self.per == 0 else 0
        self.at, self.per, self.local = at, per, 0

    def end(self, times):
        assert self.local == self.per, (self.local, self.per)
        self.base += self.per * times
        self.at = self.per = self.local = 0

    def __call__(self, ins, alone=None):
        ins.then_inc(self.sem, 1)
        self.local += 1
        wait = self.eng.wait_ge(self.sem, self.at * self.per + (self.base + self.local))
        if alone is not None:
            wait.then_inc(alone, 1)


def build(nc, a):
    ctx = ExitStack()
    sems = {}

    def sem(name):
        sems[name] = ctx.enter_context(nc.semaphore(name))
        return sems[name]

    base = (nc.sbuf_base + 63) // 64 * 64
    at = [base]
    limit = nc.sbuf_usable_end

    def sb(name, shape, dt=F32, offset=None):
        size = 4 * int(np.prod(shape[1:]))
        size = (size + 31) // 32 * 32
        where = at[0] if offset is None else offset
        assert where + size <= limit, (name, where + size - limit)
        if offset is None:
            at[0] += size
        return nc.alloc_sbuf_tensor_at(name, shape, dt, offset=where)

    w_raw = sb("w_raw", [P, 2, UNIT])
    w_hi = sb("w_hi", [P, 2, UNIT], F32R)
    w_lo = sb("w_lo", [P, 2, UNIT], F32R)
    ident = sb("ident", [P, P])
    vecs = sb("vecs", [P, 4 * KT + 16 + ADA_UNITS])
    ln_g1, ln_b1, ln_g2, ln_b2 = (vecs[:, KT * n:KT * (n + 1)] for n in range(4))
    pool_scale = vecs[:, 4 * KT:4 * KT + 16]
    b_ada = vecs[:, 4 * KT + 16:]
    ada = sb("ada", [P, ADA_UNITS, 2])
    par = sb("par", [P, 12, KT])
    sink_neg = sb("sink_neg", [P, HEADS])
    corr = sb("corr", [P, GROUPS, PAD])
    minus_half = sb("minus_half", [P, 1])
    stats = sb("stats", [P, 2, 12])
    mean_var = sb("mean_var", [P, 2, 2])
    var_eps = sb("var_eps", [P, 2])
    rstd = sb("rstd", [P, 2])
    neg_max = sb("neg_max", [P, SLOTS])
    row_sum = sb("row_sum", [P, SLOTS])
    row_rec = sb("row_rec", [P, SLOTS])
    row_mask = sb("row_mask", [P, 2, KEY_ROWS])
    col_mask = sb("col_mask", [P, 3, KEY_COLS])
    ada_at = at[0]
    w_ada = sb("w_ada", [P, UNIT])
    act_buf = sb("act_buf", [P, KT, TC])
    region = at[0]

    x_hi = sb("x_hi", [P, KT, S], F32R)
    x_lo = sb("x_lo", [P, KT, S], F32R)
    m_hi = sb("m_hi", [P, 4, S], F32R)
    m_lo = sb("m_lo", [P, 4, S], F32R)
    sz01 = sb("sz01", [P, 2, S])
    g_at = at[0]
    g_hi = sb("g_hi", [P, 4, S], F32R)
    g_lo = sb("g_lo", [P, 4, S], F32R)
    u_pad = sb("u_pad", [P, PAD + S], offset=g_at)
    win = [sb(f"win{n}", [P, PAD + S], offset=g_at + (n + 1) * 4 * (PAD + S)) for n in range(2)]
    c_in = sb("c_in", [P, 2, D], offset=g_at + 3 * 4 * (PAD + S))

    def gate_tile(n):
        if n < 2:
            return sz01[:, n, :].rearrange("p (a b) -> p a b", b=C)
        return act_buf[:, 4 * (n - 2):4 * (n - 2) + 4, S:TC]

    at[0] = region
    u_hi = sb("u_hi", [P, KT, TC], F32R)
    u_lo = sb("u_lo", [P, KT, TC], F32R)
    after_u = at[0]
    z_tile = sb("z_tile", [P, 2, D], offset=after_u + 12288)
    x_hat = sb("x_hat", [P, 2, D], offset=after_u + 12288 + 8192)
    u_tmp = sb("u_tmp", [P, 2, TC], offset=after_u)
    out_tile = sb("out_tile", [P, 2, D], offset=after_u + 12288 + 16384)
    g_row = sb("g_row", [P, D], offset=after_u + 12288 + 24576)
    b_row = sb("b_row", [P, D], offset=after_u + 12288 + 28672)
    res = sb("res", [P, 2, TC], offset=after_u)

    def attention_part(x, q_len, v_tiles, slots):
        q_parts = [sb(f"{x}q_parts{h}", [P, q_len], F32R) for h in range(2)]
        k_hi = [sb(f"{x}k_hi{h}", [P, TC], F32R) for h in range(2)]
        k_lo = sb(x + "k_lo", [P, TC], F32R)
        v = sb(x + "v", [P, v_tiles, P])
        work = at[0]
        logits = [sb(f"{x}logits{n}", [P, KEYS + 2]) for n in range(slots)]
        probs_t = sb(x + "probs_t", [P, KEYS // P, 2, P])
        return q_parts, k_hi, k_lo, v, work, logits, probs_t

    aq_parts, ak_hi, ak_lo, av, work_a, alog, aprob_t = attention_part("a_", TC, 10, SLOTS - 1)
    alog.append(sb("a_logits_last", [P, KEYS + 2], offset=ada_at))
    rope_cos = sb("rope_cos", [P, S])
    rope_sin = sb("rope_sin", [P, S])
    a_mask = sb("a_mask", [P, 9 * P])
    a_tmp = sb("a_tmp", [P, TC], offset=work_a)
    a_swap = sb("a_swap", [P, S], offset=work_a + 4 * TC)
    at[0] = after_u
    bq_parts, bk_hi, bk_lo, bv_ctx, work_b, blog, bprob_t = attention_part("b_", S, C // P, SLOTS)
    bias = sb("bias", [P, 2, 2, KEYS])
    tab = [sb("tab0", [P, TAB_ROWS * TAB_C], offset=ada_at), sb("tab1", [P, TAB_ROWS * TAB_C])]

    def b_value(t):
        return bv_ctx[:, t - 16, :] if t >= 16 else act_buf[:, t // 2, S + t % 2 * P:S + (t % 2 + 1) * P]

    b_tmp_q = sb("b_tmp_q", [P, S], offset=work_b)
    b_tmp_k = sb("b_tmp_k", [P, TC], offset=work_b + 4 * S)
    b_vt = sb("b_vt", [P, 4 * HALF + C], offset=work_b)

    psum = ctx.enter_context(nc.psum_tensor("psum", [P, 8 * HALF], F32))

    def bank(n, count=1):
        return psum[:, n * HALF:(n + count) * HALF]

    pj = [bank(6), bank(7)]
    ps_score = [bank(0, 2), bank(2, 2)]
    ps_pt = bank(4, 2)
    PT_ACT = HALF
    ps_out = [t[:, 0:2 * P] for t in pj]
    c_silu = [bank(2 * who, 2) for who in range(2)]
    ada_products = bank(4, 2)

    residual = [nc.dram_tensor(f"residual{n}", [KT, P, TC if n == 0 else S], F32, kind="Internal").ap()
                for n in range(2)]

    w_loaded = [sem("w_loaded0"), sem("w_loaded1")]
    w_hi_done, w_split = sem("w_hi_done"), sem("w_split")
    ada_loaded, ada_done = sem("ada_loaded"), sem("ada_done")
    pj_done, pj_free = sem("pj_done"), [sem("pj_free0"), sem("pj_free1")]
    const_loaded, ctx_loaded = sem("const_loaded"), sem("ctx_loaded")
    x_loaded = [sem(f"x_loaded{k}") for k in range(KT)]
    x_hi_done, x_split, x_scaled, c_ready = sem("x_hi_done"), sem("x_split"), sem("x_scaled"), sem("c_ready")
    u_used, m_split, g_hi_done, g_split = sem("u_used"), sem("m_split"), sem("g_hi_done"), sem("g_split")
    ln_tile, ln_turned, ln_var, ln_rstd = sem("ln_tile"), sem("ln_turned"), sem("ln_var"), sem("ln_rstd")
    ln_norm, ln_back, ln_stored = sem("ln_norm"), sem("ln_back"), sem("ln_stored")
    par_ready = sem("par_ready")
    mod_done, mod_split, mod_hi = sem("mod_done"), sem("mod_split"), sem("mod_hi")
    res_ready, res_stored = sem("res_ready"), sem("res_stored")
    res_loaded = [sem("res_loaded0"), sem("res_loaded1")]
    q_split, k_split = sem("q_split"), sem("k_split")
    v_turned, v_ready = sem("v_turned"), sem("v_ready")
    tab_loaded, bias_ready = sem("tab_loaded"), sem("bias_ready")
    score_done, logit_done, prob_done = sem("score_done"), sem("logit_done"), sem("prob_done")
    rec_done, prob_scaled = sem("rec_done"), sem("prob_scaled")
    pt_done, pt_dve, pt_act = sem("pt_done"), sem("pt_dve"), sem("pt_act")
    pv_done, gated = sem("pv_done"), sem("gated")
    o_hi_done, o_split = sem("o_hi_done"), sem("o_split")
    out_scaled, out_ready = sem("out_scaled"), sem("out_ready")
    out_stored = [sem("out_stored0"), sem("out_stored1")]
    dve_step, pool_step = sem("dve_step"), sem("pool_step")
    dve_waited, pool_waited = sem("dve_waited"), sem("pool_waited")

    block = ctx.enter_context(nc.Block())

    def start_at_one(eng, ready, value, signals):
        for s in signals:
            eng.wait_ge(ready, value).then_inc(s, 1)

    def after(eng, signal, count):
        return eng.wait_ge(signal, count + 1)

    def dve_tiles(n):
        return max(1, n - 2)

    def one(ap):
        return ap.rearrange("a p n -> (a p) n")

    def col(t, n, lo=None, hi=None):
        lo, hi = lo or 0, hi or t.shape[2]
        return t[:, bass.ds(n, 1), lo:hi].rearrange("p a n -> p (a n)")

    def a_tile(t):
        latent, ctx = KEYS - C, (KEYS - C, S, C)
        if t >= S // P:
            return latent, [ctx], [8, 9], 3 * P
        if t == 0:
            return P, [(P, 0, 2 * P), ctx], [0, 1, 8, 9], P
        if t == S // P - 1:
            return P, [(P, (t - 1) * P, 2 * P), ctx], [t - 1, t, 8, 9], 5 * P
        return 0, [(0, (t - 1) * P, 3 * P), ctx], [t - 1, t, t + 1, 8, 9], 0

    def load_tab(sp, j, h):
        table = a["bias_tab"][bass.ds(2 * j + h, 1)]
        runs = bass.AP(tensor=table.tensor, offset=table.offset, ap=[[TAB_C, 8], [1, 16], [1, TAB_RUN]])
        sp.dma_start(tab[h][:, 0:TAB_RUN], runs).then_inc(tab_loaded, 16)

    def residual_loads(act, layer, c, chunks):
        tokens = (TC, S)[layer]

        def load(o, s):
            act.dma_start(res[:, s, 0:tokens], one(residual[layer][bass.ds(o, 1)])).then_inc(res_loaded[s], 16)

        act.wait_ge(res_stored, 16 * KT * (layer + 1))
        for s in range(2):
            load(s, s)
        with act.Fori(0, KT // 2 - 1) as i:
            for s in range(2):
                for b, v in free_counts(len(chunks) * i + c // 2, s * len(chunks), len(chunks)).items():
                    after(act, pj_free[b], v)
                load(2 * i + (2 + s), s)

    @block.sync
    def _(sp):
        def load_unit(n, slot):
            sp.dma_start(w_raw[:, slot, :], one(a["weights"][bass.ds(n, 1)])).then_inc(w_loaded[slot], 16)

        def next_unit(n, slot):
            sp.wait_ge(w_split, n + 1)
            load_unit(n + 2, slot)

        for k in range(KT):
            sp.dma_start(act_buf[:, k, 0:S], a["x_t"][:, k, :]).then_inc(x_loaded[k], 16)
            if k < 2:
                load_unit(k, k)
        with sp.Fori(0, GROUPS) as g:
            for l in range(L1_UNITS):
                next_unit(g * L1_UNITS + l, l % 2)
                if l < ADA:
                    after(sp, ada_done, g * ADA + l)
                    sp.dma_start(w_ada[:, :], one(a["w_ada"][bass.ds(g * ADA + l, 1)])).then_inc(ada_loaded, 16)
        sp.wait_ge(g_split, 4 * GROUPS)
        sp.dma_start(act_buf[:, :, S:TC], a["ctx_t"]).then_inc(ctx_loaded, 16)
        sp.wait_ge(pj_done, A_CHUNK)
        for dst, src in ((rope_cos, "rope_cos"), (rope_sin, "rope_sin"), (a_mask, "a_mask")):
            sp.dma_start(dst[:, :], a[src]).then_inc(ctx_loaded, 16)
        for n in (A_UNIT, A_UNIT + 1):
            next_unit(n, n % 2)
        with sp.Fori(0, KT) as k:
            sp.wait_ge(res_ready, k + 1)
            sp.dma_start(one(residual[0][bass.ds(k, 1)]), col(act_buf, k)).then_inc(res_stored, 16)
        with sp.Fori((A_UNIT + 2) // 2, B_UNIT // 2 + 1) as i:
            for s in range(2):
                next_unit(2 * i + s, s)
        for h in range(2):
            load_tab(sp, 0, h)
        with sp.Fori(0, KT) as k:
            sp.wait_ge(res_ready, k + (KT + 1))
            sp.dma_start(one(residual[1][bass.ds(k, 1)]), col(act_buf, k, 0, S)).then_inc(res_stored, 16)
        with sp.Fori(0, PAIRS - 1) as j:
            for l in range(4):
                next_unit(4 * j + (B_UNIT + 2 + l), l % 2)
            sp.wait_ge(bias_ready, (j + 1) * (2 * B_BUILDS))
            for h in range(2):
                load_tab(sp, j + 1, h)
        with sp.Fori((B_UNIT + 2 + 4 * (PAIRS - 1)) // 2, (ALL_UNITS - 2) // 2) as i:
            for s in range(2):
                next_unit(2 * i + s, s)
        after(sp, gated, 2 * (OT_A + PAIRS * B_TILES))
        for dst, src in ((g_row, "ln_g3"), (b_row, "ln_b3")):
            sp.dma_start(dst[:, :], bass.AP(tensor=a[src].tensor, offset=0, ap=[[0, P], [1, D]])).then_inc(ctx_loaded, 16)
        for s in range(2):
            sp.wait_ge(ctx_loaded, 16 * 4).then_inc(out_stored[s], 16)
        with sp.Fori(0, S // P // 2) as i:
            for s in range(2):
                sp.wait_ge(out_ready, 2 * i + (s + 1))
                sp.dma_start(one(a["out"][bass.ds(2 * i + s, 1)]), out_tile[:, s, :]).then_inc(out_stored[s], 16)
        for s in range(2):
            sp.wait_ge(out_stored[s], 16 * (S // P // 2) + 16)
        sp.wait_ge(res_stored, 16 * 2 * KT)

    @block.gpsimd
    def _(pool):
        step = Chain(pool, pool_step)

        def loads(turn):
            return 16 * turn + 16

        def split(n, slot, loaded, used=None):
            pool.wait_ge(w_loaded[slot], loaded)
            if used is not None:
                pool.wait_ge(pj_done, used).then_inc(pool_waited, 1)
            pool.tensor_copy(w_hi[:, slot, :], w_raw[:, slot, :]).then_inc(w_hi_done, 1)
            pool.wait_ge(w_hi_done, n + 1)
            pool.tensor_tensor(w_lo[:, slot, :], w_raw[:, slot, :], w_hi[:, slot, :].bitcast(F32),
                               ALU.subtract).then_inc(w_split, 1)

        pool.memset(minus_half[:, :], -0.5).then_inc(pool_step, 1)
        step.base += 1
        for n in range(2):
            split(n, n, loads(0))
        with pool.Fori(0, GROUPS) as g:
            for l in range(L1_UNITS):
                split(g * L1_UNITS + (l + 2), l % 2,
                      loads(g * (L1_UNITS // 2) + (l + 2) // 2), g * L1_CHUNKS + L1_ENDS[l])

        def rstds(first, tiles):
            if first == 0:
                pool.wait_ge(pool_step, 1)
            with pool.Fori(0, tiles // 2) as i:
                for s in range(2):
                    t = 2 * i + (first + s)
                    pool.wait_ge(ln_var, t + 1)
                    if first or s:
                        after(pool, ln_norm, t - 1)
                    pool.tensor_tensor(rstd[:, s:s + 1], var_eps[:, s:s + 1], minus_half[:, :],
                                       ALU.pow).then_inc(ln_rstd, 1)

        def residuals(layer):
            pool.wait_ge(par_ready, layer + 1)
            for k in range(KT):
                pool.wait_ge(mod_done, layer * KT + k + 1)
                x = act_buf[:, k, 0:S]
                ins = pool.tensor_scalar(x, x, par[:, 4 + 6 * layer, k:k + 1], par[:, 5 + 6 * layer, k:k + 1],
                                         ALU.mult, ALU.add)
                if layer == 0:
                    x = act_buf[:, k, S:TC]
                    ins = pool.tensor_scalar(x, x, ALPHA_2, None, ALU.mult)
                ins.then_inc(res_ready, 1)

        rstds(0, S // P)
        residuals(0)
        for m in range(2):
            n, c = A_UNIT + 10 * m, A_CHUNK + 30 * m
            for l in range(2):
                split(n + l + 2, l, loads((n + l + 2) // 2), c + 3 * (l + 1))
            with pool.Fori(0, 4) as i:
                for l in range(2):
                    split(2 * i + (n + 4 + l), l, loads(i + (n + 4) // 2), 6 * i + (c + 9 + 3 * l))
        with pool.Fori(0, KT // 2) as i:
            for l in range(2):
                split(2 * i + (AO_UNIT + 2 + l), l, loads(i + (AO_UNIT + 2) // 2),
                      6 * i + (AO_CHUNK + 3 + 3 * l))
        after(pool, gated, 2 * OT_A)
        pool.memset(bias[:, :, :, LAT_KEYS:KEYS], 0.0).then_inc(pool_step, 1)
        step.base += 1
        rstds(S // P, TC // P)
        residuals(1)
        step.begin(0, 0)

        def bias_tile(j, b):
            half, kind, slot = b // 3, b % 3, b % 2
            d = -4 * half
            e = -8 * kind
            r0, c0 = 11 - d, 31 - e
            for h in range(2):
                back, tile = LAST_BIAS_USE[b]
                pool.wait_ge(logit_done, j * B_STEPS + (STEPS_A - back * B_STEPS + 2 * tile + h + 1))
                src = tab[h][:, :].rearrange("p (r c) -> p r c", c=TAB_C)
                src = src[:, r0 - KEY_ROWS + 1:r0 + 1, c0 - KEY_COLS + 1:c0 + 1][:, ::-1, ::-1]
                dst = bias[:, h, slot, 0:LAT_KEYS].rearrange("p (r c) -> p r c", c=KEY_COLS)
                cm = col_mask[:, kind, :].rearrange("p (a c) -> p a c", a=1).to_broadcast([P, KEY_ROWS, KEY_COLS])
                rm = row_mask[:, half, :].rearrange("p (r a) -> p r a", a=1).to_broadcast([P, KEY_ROWS, KEY_COLS])
                step(pool.tensor_tensor(dst, src, cm, ALU.add))
                pool.tensor_tensor(dst, dst, rm, ALU.add).then_inc(bias_ready, 1)

        with pool.Fori(0, PAIRS) as j:
            step.begin(j, 2 * B_BUILDS)
            pool.wait_ge(tab_loaded, (j + 1) * 32)
            for b in range(2):
                bias_tile(j, b)
            for l, end in enumerate((2, 5, 8, 10)):
                split(4 * j + (B_UNIT + 2 + l), l % 2,
                      loads(2 * j + (B_UNIT + 2 + l) // 2), 10 * j + (B_CHUNK + end))
            for b in range(2, B_BUILDS):
                bias_tile(j, b)
        step.end(PAIRS)
        with pool.Fori(0, KT // 2 - 1) as i:
            for l in range(2):
                split(2 * i + (BO_UNIT + 2 + l), l, loads(i + (BO_UNIT + 2) // 2),
                      4 * i + (BO_CHUNK + 2 + 2 * l))
        last = S // P + TC // P
        pool.wait_ge(ctx_loaded, 16 * 6)
        with pool.Fori(0, S // P // 2) as i:
            for s in range(2):
                t = 2 * i + (last + s)
                pool.wait_ge(ln_var, t + 1)
                after(pool, ln_norm, t - 1)
                pool.tensor_tensor(rstd[:, s:s + 1], var_eps[:, s:s + 1], minus_half[:, :],
                                   ALU.pow).then_inc(ln_rstd, 1)
                pool.wait_ge(out_scaled, 2 * i + (s + 1))
                pool.tensor_tensor(out_tile[:, s, :], out_tile[:, s, :], b_row[:, :], ALU.add).then_inc(out_ready, 1)

    @block.tensor
    def _(pe):
        def product(out, w, x, first, last):
            (wh, wl), (xh, xl) = w, x
            pe.matmul(out, wh, xh, start=first, stop=False)
            pe.matmul(out, wh, xl, start=False, stop=False)
            return pe.matmul(out, wl, xh, start=False, stop=last)

        def project(n, slot, half, l0, x_hi, x_lo, chunks, kts=KT):
            pe.wait_ge(w_split, n + 1)
            l = l0
            for o in range(KT // kts):
                for t0, tn in chunks:
                    after(pe, pj_free[l % 2], half + l // 2)
                    out = pj[l % 2][:, 0:tn]
                    for k in range(kts):
                        w = (o * kts + k) * P
                        mm = product(out, (w_hi[:, slot, w:w + P], w_lo[:, slot, w:w + P]),
                                     (x_hi[:, k, t0:t0 + tn], x_lo[:, k, t0:t0 + tn]), k == 0, k == kts - 1)
                    mm.then_inc(pj_done, 1)
                    l += 1

        start_at_one(pe, x_split, 1, (ln_back, pv_done))
        pe.wait_ge(x_split, KT)
        with pe.Fori(0, GROUPS) as g:
            l = 0
            for u in range(L1_UNITS):
                if u == 8:
                    pe.wait_ge(m_split, g * 4 + 4)
                if u == 10:
                    pe.wait_ge(g_split, g * 4 + 4)
                n, half = g * L1_UNITS + u, g * (L1_CHUNKS // 2)
                if u < 8:
                    project(n, u % 2, half, l, x_hi, x_lo, LAT_CHUNKS)
                    l += 2
                else:
                    project(n, u % 2, half, l, *((m_hi, m_lo) if u < 10 else (g_hi, g_lo)), LAT_CHUNKS, kts=4)
                    l += 4

        def normalise(first, tiles, back=True):
            def to_rows(t, s):
                pe.wait_ge(ln_tile, t + 1)
                if not isinstance(t, int) or t >= 2:
                    after(pe, ln_norm, t - 1)
                for k in range(KT):
                    tr = pe.transpose(bank(2 * s, 2)[:, k * P:(k + 1) * P], z_tile[:, s, k * P:(k + 1) * P], ident[:, :])
                tr.then_inc(ln_turned, 1)

            def to_columns(t, s):
                after(pe, ln_norm, t + 1)
                if not isinstance(t, int) or t >= 1:
                    after(pe, ln_stored, t)
                for k in range(KT):
                    tr = pe.transpose(ps_pt[:, k * P:(k + 1) * P], x_hat[:, s, k * P:(k + 1) * P], ident[:, :])
                tr.then_inc(ln_back, 1)

            if not back:
                with pe.Fori(0, tiles // 2) as i:
                    for s in range(2):
                        to_rows(2 * i + (first + s), s)
                return
            to_rows(first, 0)
            with pe.Fori(0, tiles // 2 - 1) as i:
                to_rows(2 * i + (first + 1), 1)
                to_columns(2 * i + first, 0)
                to_rows(2 * i + (first + 2), 0)
                to_columns(2 * i + (first + 1), 1)
            to_rows(first + tiles - 1, 1)
            to_columns(first + tiles - 2, 0)
            to_columns(first + tiles - 1, 1)

        normalise(0, S // P)

        def values(vt, sets, base, v_base):
            for n, tiles in enumerate(sets):
                if n >= 2:
                    pe.wait_ge(v_ready, v_base + (n - 1))
                for i, t in enumerate(tiles):
                    tr = pe.transpose(bank(4 + n % 2)[:, i * P:(i + 1) * P], vt[:, t * P:(t + 1) * P], ident[:, :])
                tr.then_inc(v_turned, 1)

        def wait_read(counts):
            for b, v in counts.items():
                after(pe, pj_free[b], v)

        def score(s, h0, scores):
            if s >= 2:
                pe.wait_ge(logit_done, h0 + (s - 1))
            for out, q, k in scores(s):
                mm = pe.matmul(out, q[0], k[0], start=True, stop=False)
                mm = pe.matmul(out, q[1], k[1], start=False, stop=True)
            mm.then_inc(score_done, 1)

        def attention(h0, p0, steps, scores, width, keys, logits, prob_t, v, free):
            def turn_probs(s):
                pe.wait_ge(prob_scaled, h0 + (s + 1))
                after(pe, pt_dve, h0 + s)
                after(pe, pt_act, h0 + s)
                c0, n = width(s), (KEYS - width(s)) // P
                for c in range(n):
                    at = c * P if c < dve_tiles(n) else PT_ACT + (c - dve_tiles(n)) * P
                    tr = pe.transpose(ps_pt[:, at:at + P], logits[s % SLOTS][:, c0 + c * P:c0 + (c + 1) * P], ident[:, :])
                tr.then_inc(pt_done, 1)

            def outputs(p):
                pe.wait_ge(pt_dve, h0 + (2 * p + 3))
                pe.wait_ge(pt_act, h0 + (2 * p + 3))
                if p < 2:
                    after(pe, pj_free[p], free[p])
                else:
                    after(pe, gated, 2 * p0 + 2 * (p - 1))
                tiles = keys(p)
                for c, t in enumerate(tiles):
                    mm = pe.matmul(ps_out[p % 2], v(t), prob_t[:, c, :, :], start=(c == 0), stop=(c == len(tiles) - 1))
                mm.then_inc(pv_done, 1)

            for s in range(steps):
                turn_probs(s)
                if s + 4 < steps:
                    score(s + 4, h0, scores)
                if s % 2:
                    outputs(s // 2)

        def head_scores(h, q_parts, k_hi, k_lo, c, q, k):
            r = slice(h * HD, (h + 1) * HD)
            return c, (q(q_parts[h][:, :]), q(q_parts[h][r, :])), (k(k_hi[h][:, :]), k(k_lo[r, :]))

        def a_scores(s):
            t, h = s // 2, s % 2
            for c, k0, n in a_tile(t)[1]:
                yield head_scores(h, aq_parts, ak_hi, ak_lo, ps_score[h][:, P + c:P + c + n],
                                  lambda q: q[:, t * P:(t + 1) * P], lambda k: k[:, k0:k0 + n])

        after(pe, mod_split, KT)
        for m in range(2):
            n, c = A_UNIT + 10 * m, A_CHUNK + 30 * m
            if m:
                after(pe, gated, 2 * 4 * A_TILES)
            project(n, 0, c // 2, 0, u_hi, u_lo, ALL_CHUNKS)
            project(n + 1, 1, c // 2, 3, u_hi, u_lo, ALL_CHUNKS)
            wait_read(free_counts(c // 2, 3, 3))
            values(a_tmp, [range(0, 4), range(4, 8), range(8, 10)], VSETS_A * m, VSETS_A * m)
            with pe.Fori(0, 4) as i:
                half = 3 * i + (c // 2 + 3)
                h0, p0 = i * A_STEPS + 4 * m * A_STEPS, i * A_TILES + 4 * m * A_TILES
                after(pe, gated, 2 * p0)
                project(2 * i + (n + 2), 0, half, 0, u_hi, u_lo, ALL_CHUNKS)
                project(2 * i + (n + 3), 1, half, 3, u_hi, u_lo, LAT_CHUNKS)
                pe.wait_ge(k_split, 4 * (m + 1))
                pe.wait_ge(q_split, 2 * i + 2 * (4 * m + 1))
                pe.wait_ge(v_ready, VSETS_A * (m + 1))
                for s in range(2):
                    score(s, h0, a_scores)
                project(2 * i + (n + 3), 1, half, 5, u_hi, u_lo, ALL_CHUNKS[2:])
                for s in range(2, 4):
                    score(s, h0, a_scores)
                attention(h0, p0, A_STEPS, a_scores, lambda s: a_tile(s // 2)[0], lambda p: a_tile(p)[2],
                          alog, aprob_t, lambda t: av[:, t, :], free_counts(half, 0, 6))

        def output_projection(n, c, chunks, layer):
            pe.wait_ge(o_split, KT * (layer + 1))
            count = 2 * len(chunks)
            with pe.Fori(0, KT // 2) as i:
                for s in range(2):
                    project(2 * i + (n + s), s, (count // 2) * i + c // 2, s * len(chunks), u_hi, u_lo, chunks)

        output_projection(AO_UNIT, AO_CHUNK, ALL_CHUNKS, 0)
        normalise(S // P, TC // P)

        def b_scores(s):
            t, h = s // 2, s % 2
            half, cb = t // 4, t % 4

            def near(k):
                return k[:, 0:S].rearrange("p (r c) -> p r c", c=GRID)[
                    :, 4 * half:4 * half + KEY_ROWS, KEY_COL[cb]:KEY_COL[cb] + KEY_COLS]

            for c, n, k in ((0, LAT_KEYS, near), (LAT_KEYS, C, lambda k: k[:, S:TC])):
                yield head_scores(h, bq_parts, bk_hi, bk_lo, ps_score[h][:, P + c:P + c + n],
                                  lambda q: q[:, t * P:(t + 1) * P], k)

        def b_keys(p):
            half, cb = p // 4, p % 4
            return [cb * 4 + half + n for n in range(3)] + [16, 17]

        after(pe, mod_split, 2 * KT)
        with pe.Fori(0, PAIRS) as j:
            n, half = 4 * j + B_UNIT, 5 * j + B_CHUNK // 2
            h0, p0 = j * B_STEPS + STEPS_A, j * B_TILES + OT_A
            after(pe, gated, 2 * p0)
            project(n, 0, half, 0, u_hi, u_lo, LAT_CHUNKS)
            project(n + 1, 1, half, 2, u_hi, u_lo, ALL_CHUNKS)
            project(n + 2, 0, half, 5, u_hi, u_lo, ALL_CHUNKS)
            project(n + 3, 1, half, 8, u_hi, u_lo, LAT_CHUNKS[:1])
            wait_read(free_counts(half, 5, 3))
            v0 = j * VSETS_B + 2 * VSETS_A
            values(b_vt, [range(0, 4), range(4, 8), range(8, 12), range(12, 16), range(16, 18)], v0, v0)
            pe.wait_ge(k_split, 4 * j + 4 * 3)
            pe.wait_ge(q_split, 2 * j + 2 * (PAIRS + 1))
            for s in range(2):
                score(s, h0, b_scores)
            project(n + 3, 1, half, 9, u_hi, u_lo, LAT_CHUNKS[1:])
            for s in range(2, 4):
                score(s, h0, b_scores)
            pe.wait_ge(v_ready, v0 + VSETS_B)
            attention(h0, p0, B_STEPS, b_scores, lambda s: 0, b_keys, blog, bprob_t, b_value, free_counts(half, 0, 10))
        output_projection(BO_UNIT, BO_CHUNK, LAT_CHUNKS, 1)
        normalise(S // P + TC // P, S // P, back=False)

    @block.scalar
    def _(act):
        loads = [(ident[:, :], a["ident"]), (vecs[:, :], a["vecs"]),
                 (corr[:, :, :], a["corr"]), (row_mask[:, :, :], a["row_mask"]), (col_mask[:, :, :], a["col_mask"]),
                 (sink_neg[:, :], bass.AP(tensor=a["sink"].tensor, offset=0, ap=[[0, P], [1, HEADS]])),
                 (c_in[:, :, :], bass.AP(tensor=a["c_rows"].tensor, offset=0, ap=[[0, P], [D, 2], [1, D]]))]
        for dst, src in loads:
            act.dma_start(dst, src).then_inc(const_loaded, 16)

        def wait_chunk(c):
            act.wait_ge(pj_done, c + 1)

        start_at_one(act, x_loaded[0], 16, (*pj_free, ln_stored, pt_act))
        for k in range(KT):
            act.wait_ge(x_loaded[k], 16)
            act.activation(x_hi[:, k, :], act_buf[:, k, 0:S], ACT.Copy).then_inc(x_hi_done, 1)
        act.wait_ge(const_loaded, 16 * len(loads))
        for who in range(2):
            act.activation(c_silu[who], c_in[:, who, :], ACT.Silu).then_inc(c_ready, 1)
        for k in range(KT):
            act.wait_ge(x_split, k + 1)
            act.activation(act_buf[:, k, 0:S], act_buf[:, k, 0:S], ACT.Copy, scale=ALPHA_1).then_inc(x_scaled, 1)
        with act.Fori(0, GROUPS) as g:
            c, half = g * L1_CHUNKS, g * (L1_CHUNKS // 2)
            for i in range(4):
                after(act, u_used, g * 4 + i)
                for h in range(2):
                    wait_chunk(c + (2 * i + h))
                    act.activation(u_pad[:, PAD + h * HALF:PAD + (h + 1) * HALF], pj[h], ACT.Copy).then_inc(pj_free[h], 1)
            for i in range(4):
                for h in range(2):
                    wait_chunk(c + (8 + 2 * i + h))
                    act.activation(gate_tile(i)[:, 2 * h:2 * h + 2, :], pj[h].rearrange("p (a b) -> p a b", b=C),
                                   ACT.Silu).then_inc(pj_free[h], 1)
            for i in range(4):
                for b, v in free_counts(half, 16 + 2 * i, 2).items():
                    after(act, pj_free[b], v)
                act.activation(g_hi[:, i, :].rearrange("p (a b) -> p a b", b=C), gate_tile(i), ACT.Copy).then_inc(g_hi_done, 1)

        def normalise(first, tiles, back=True):
            def set_out(t, s, col0):
                if not isinstance(t, int) or t >= 2:
                    act.wait_ge(ln_turned, t - 1)
                act.activation(z_tile[:, s, :].rearrange("p (k n) -> p k n", n=P), act_buf[:, :, bass.ds(col0, P)],
                               ACT.Copy).then_inc(ln_tile, 1)

            def take(t, col0):
                after(act, ln_back, t + 1)
                act.activation(act_buf[:, :, bass.ds(col0, P)], ps_pt[:, :].rearrange("p (k n) -> p k n", n=P),
                               ACT.Copy).then_inc(ln_stored, 1)

            if not back:
                with act.Fori(0, tiles // 2) as i:
                    for s in range(2):
                        set_out(2 * i + (first + s), s, i * (2 * P) + s * P)
                return
            for s in range(2):
                set_out(first + s, s, s * P)
            with act.Fori(0, tiles // 2 - 1) as i:
                for s in range(2):
                    set_out(2 * i + (first + 2 + s), s, i * (2 * P) + (2 + s) * P)
                    take(2 * i + (first + s), i * (2 * P) + s * P)
            for s in range(2):
                take(first + tiles - 2 + s, (tiles - 2 + s) * P)

        def wait_sums(c):
            for b in range(2):
                after(act, pj_free[b], c // 2)

        def modulate(layer):
            act.wait_ge(par_ready, layer + 1)
            if layer == 0:
                act.wait_ge(ctx_loaded, 16 * 4)
            after(act, ln_stored, (S // P, S // P + TC // P)[layer])
            q = 6 * layer
            with act.Fori(0, KT // 2) as i:
                for s in range(2):
                    k = 2 * i + s
                    if layer or s:
                        after(act, mod_split, 2 * i + (layer * KT + s - 1))
                    elif s == 0:
                        after(act, mod_split, 2 * i)
                    for lo, hi, f in ((0, S, 0), (S, TC, 2)):
                        ins = act.activation(u_tmp[:, s, lo:hi], col(act_buf, k, lo, hi), ACT.Identity,
                                             scale=par[:, q + f, bass.ds(k, 1)], bias=par[:, q + f + 1, bass.ds(k, 1)])
                    ins.then_inc(mod_done, 1)

        def take_projection(c, half, l0, chunks, dst, func=ACT.Copy, scale=1.0):
            for n, (t0, tn) in enumerate(chunks):
                l = l0 + n
                wait_chunk(c + l)
                act.activation(dst[:, t0:t0 + tn], pj[l % 2][:, 0:tn], func, scale=scale).then_inc(pj_free[l % 2], 1)

        def probs(s, h0, width, end, logits):
            act.wait_ge(logit_done, h0 + (s + 1))
            c0, n, lg = width(s), s % SLOTS, logits[s % SLOTS]
            act.activation(lg[:, c0:end], lg[:, c0 + 1:end + 1], ACT.Exp, scale=-1.0,
                           bias=neg_max[:, n:n + 1], accum_out=row_sum[:, n:n + 1]).then_inc(prob_done, 1)

        def scale(s, h0, width, end, logits):
            act.wait_ge(rec_done, h0 + (s + 1))
            n, pr = s % SLOTS, logits[s % SLOTS][:, width(s):KEYS]
            act.activation(pr, pr, ACT.Copy, scale=row_rec[:, n:n + 1]).then_inc(prob_scaled, 1)

        def first_probs(*soft):
            for s in range(2):
                probs(s, *soft)
            for s in range(2):
                scale(s, *soft)

        def softmax(p0, steps, prob_t, *soft):
            h0, width = soft[:2]
            for p in range(steps // 2):
                for s in (2 * p, 2 * p + 1):
                    act.wait_ge(pt_done, h0 + (s + 1))
                    after(act, pv_done, p0 + p)
                    n = (KEYS - width(s)) // P
                    d = dve_tiles(n)
                    act.activation(prob_t[:, d:n, s % 2, :], ps_pt[:, PT_ACT:PT_ACT + (n - d) * P].rearrange(
                        "p (t q) -> p t q", q=P), ACT.Copy).then_inc(pt_act, 1)
                    if s + 2 < steps:
                        probs(s + 2, *soft)
                for s in (2 * p + 2, 2 * p + 3):
                    if s < steps:
                        scale(s, *soft)

        def split_outputs(layer, tokens, tiles):
            after(act, gated, 2 * tiles)
            with act.Fori(0, KT) as k:
                act.activation(col(u_hi, k, 0, tokens), col(act_buf, k, 0, tokens), ACT.Copy).then_inc(o_hi_done, 1)

        wait_sums(A_CHUNK)
        normalise(0, S // P)
        modulate(0)
        for m in range(2):
            c = A_CHUNK + 30 * m
            if m:
                after(act, pv_done, 4 * A_TILES)
            take_projection(c, None, 0, ALL_CHUNKS, a_tmp)
            act.wait_ge(k_split, 4 * (m + 1))
            take_projection(c, None, 3, ALL_CHUNKS, a_tmp)
            if m == 0:
                act.wait_ge(res_stored, 16 * KT)
            with act.Fori(0, 4) as i:
                ci = 6 * i + (c + 6)
                act.wait_ge(v_turned, VSETS_A * (m + 1))
                h0, p0 = i * A_STEPS + 4 * m * A_STEPS, i * A_TILES + 4 * m * A_TILES
                after(act, pv_done, p0)
                take_projection(ci, None, 0, ALL_CHUNKS, a_tmp, scale=Q_SCALE)
                gates = col(act_buf, i + 4 * m)
                take_projection(ci, None, 3, LAT_CHUNKS, gates, func=ACT.Silu)
                soft = h0, lambda s: a_tile(s // 2)[0], KEYS + 1, alog
                first_probs(*soft)
                take_projection(ci, None, 5, ALL_CHUNKS[2:], gates, func=ACT.Silu)
                softmax(p0, A_STEPS, aprob_t, *soft)
        split_outputs(0, TC, OT_A)
        residual_loads(act, 0, AO_CHUNK, ALL_CHUNKS)
        wait_sums(B_CHUNK)
        normalise(S // P, TC // P)
        modulate(1)
        act.wait_ge(res_stored, 16 * 2 * KT)
        with act.Fori(0, PAIRS) as j:
            c = 10 * j + B_CHUNK
            h0, p0 = j * B_STEPS + STEPS_A, j * B_TILES + OT_A
            after(act, pv_done, p0)
            for h in range(2):
                wait_chunk(c + h)
                act.activation(b_tmp_q[:, h * HALF:(h + 1) * HALF].rearrange("p (b r c) -> p b r c", b=4, r=8),
                               pj[h].rearrange("p (r b c) -> p b r c", b=4, r=8), ACT.Copy,
                               scale=Q_SCALE).then_inc(pj_free[h], 1)
            take_projection(c, None, 2, ALL_CHUNKS, b_tmp_k)
            act.wait_ge(k_split, 4 * j + 4 * 3)
            for n, (t0, tn) in enumerate(ALL_CHUNKS):
                l = 5 + n
                wait_chunk(c + l)
                if n < 2:
                    src = pj[l % 2].rearrange("p (r c) -> p r c", c=GRID)
                    for cb in range(4):
                        dst = b_vt[:, cb * HALF + n * C:cb * HALF + (n + 1) * C].rearrange("p (r c) -> p r c", c=KEY_COLS)
                        ins = act.activation(dst, src[:, :, KEY_COL[cb]:KEY_COL[cb] + KEY_COLS], ACT.Copy)
                else:
                    ins = act.activation(b_vt[:, 4 * HALF:4 * HALF + C], pj[l % 2][:, 0:tn], ACT.Copy)
                ins.then_inc(pj_free[l % 2], 1)
            gates = col(act_buf, j, 0, S)
            take_projection(c, None, 8, LAT_CHUNKS[:1], gates, func=ACT.Silu)
            soft = h0, lambda s: 0, KEYS, blog
            first_probs(*soft)
            take_projection(c, None, 9, LAT_CHUNKS[1:], gates, func=ACT.Silu)
            softmax(p0, B_STEPS, bprob_t, *soft)
        split_outputs(1, S, OT_A + PAIRS * B_TILES)
        residual_loads(act, 1, BO_CHUNK, LAT_CHUNKS)
        wait_sums(BO_CHUNK + 2 * KT)
        normalise(S // P + TC // P, S // P, back=False)

    @block.vector
    def _(dve):
        step = Chain(dve, dve_step)

        def wait_chunk(c):
            dve.wait_ge(pj_done, c + 1)

        start_at_one(dve, x_loaded[0], 16, (ada_done, u_used, ln_norm, mod_split, pt_dve, gated))
        dve.wait_ge(const_loaded, 16 * 7)
        step(dve.tensor_scalar(sink_neg[:, :], sink_neg[:, :], -1.0, None, ALU.mult))
        for k in range(KT):
            dve.wait_ge(x_hi_done, k + 1)
            dve.tensor_tensor(x_lo[:, k, :], act_buf[:, k, 0:S], x_hi[:, k, :].bitcast(F32), ALU.subtract).then_inc(x_split, 1)

        def window(g, i):
            w, half = WINDOWS[g], g * (L1_CHUNKS // 2)
            for b, v in free_counts(half, 2 * i, 2).items():
                after(dve, pj_free[b], v)
            src, lo, sh = u_pad, 0, 1
            for n in range(g + 1):
                dst = win[n % 2]
                lo += sh
                step(dve.tensor_tensor(dst[:, lo:PAD + S], src[:, lo:PAD + S], src[:, lo - sh:PAD + S - sh], ALU.add))
                src, sh = dst, 2 * sh
            step(dve.tensor_tensor(src[:, PAD:2 * PAD], src[:, PAD:2 * PAD], corr[:, g, :], ALU.mult))
            m = win[(g + 1) % 2]
            dve.scalar_tensor_tensor(m[:, PAD:], src[:, PAD:], 1.0 / w, u_pad[:, PAD:], ALU.mult,
                                     ALU.subtract).then_inc(u_used, 1)
            after(dve, u_used, 4 * g + i + 1)
            step(dve.tensor_copy(m_hi[:, i, :], m[:, PAD:]))
            dve.tensor_tensor(m_lo[:, i, :], m[:, PAD:], m_hi[:, i, :].bitcast(F32), ALU.subtract).then_inc(m_split, 1)
            dve.wait_ge(m_split, 4 * g + i + 1)

        def modulation(n):
            dve.wait_ge(ada_loaded, 16 * (n + 1))
            dve.wait_ge(c_ready, 2)
            for who in range(2):
                ins = dve.tensor_tensor_reduce(ada_products, w_ada[:, :], c_silu[who], 1.0, b_ada[:, n:n + 1], ALU.mult, ALU.add,
                                               ada[:, n, who:who + 1])
                if who == 0:
                    step(ins)
            ins.then_inc(ada_done, 1)
            after(dve, ada_done, n + 1)

        for g in range(GROUPS):
            c = g * L1_CHUNKS
            step(dve.memset(u_pad[:, 0:PAD], 0.0))
            for i in range(4):
                window(g, i)
                modulation(ADA * g + i)
            for i in range(4, 8):
                modulation(ADA * g + i)
            for i in range(4):
                for h in range(2):
                    wait_chunk(c + 16 + 2 * i + h)
                    gt = gate_tile(i)[:, 2 * h:2 * h + 2, :]
                    dve.scalar_tensor_tensor(gt, pj[h].rearrange("p (a b) -> p a b", b=C), pool_scale[:, 4 * g + i:4 * g + i + 1],
                                             gt, ALU.mult, ALU.mult).then_inc(pj_free[h], 1)
                if i == 1:
                    modulation(ADA * g + 8)
                if i % 2:
                    for n in (i - 1, i):
                        dve.wait_ge(g_hi_done, 4 * g + n + 1)
                        dve.tensor_tensor(g_lo[:, n, :].rearrange("p (a b) -> p a b", b=C), gate_tile(n),
                                          g_hi[:, n, :].bitcast(F32).rearrange("p (a b) -> p a b", b=C),
                                          ALU.subtract).then_inc(g_split, 1)
            modulation(ADA * g + 9)
            if g == 0:
                dve.wait_ge(x_scaled, KT)
            for o in range(KT):
                for h in range(2):
                    wait_chunk(c + 24 + 2 * o + h)
                    y = act_buf[:, o, h * HALF:(h + 1) * HALF]
                    dve.tensor_tensor(y, pj[h], y, ALU.add).then_inc(pj_free[h], 1)
                if o in (1, 3):
                    modulation(ADA * g + 10 + o // 2)

        after(dve, ada_done, ADA_UNITS)
        for layer, g, b in ((0, ln_g1, ln_b1), (1, ln_g2, ln_b2)):
            n, q = 24 * layer, 6 * layer
            for who in range(2):
                shift, scale = ada[:, n:n + KT, who], ada[:, n + KT:n + 2 * KT, who]
                f, o = par[:, q + 2 * who, :], par[:, q + 2 * who + 1, :]
                if layer == 0 and who == 1:
                    step(dve.tensor_scalar(f, scale, 1.0, None, ALU.add))
                    step(dve.tensor_copy(o, shift))
                    continue
                step(dve.tensor_scalar(f, scale, 1.0, None, ALU.add))
                step(dve.tensor_tensor(o, f, b, ALU.mult))
                step(dve.tensor_tensor(o, o, shift, ALU.add))
                step(dve.tensor_tensor(f, f, g, ALU.mult))
            step(dve.tensor_scalar(par[:, q + 4, :], g, ALPHA_2, None, ALU.mult))
            dve.tensor_scalar(par[:, q + 5, :], b, ALPHA_2, None, ALU.mult).then_inc(par_ready, 1)

        def normalise(first, tiles, last=False):
            with dve.Fori(0, tiles // 2) as i:
                step.begin(i, 6)
                for s in range(2):
                    t = 2 * i + (first + s)
                    rows = bank(2 * s, 2)
                    dve.wait_ge(ln_turned, t + 1)
                    step(dve.bn_stats(stats[:, s, 0:6], rows[:, 0:HALF]))
                    step(dve.bn_stats(stats[:, s, 6:12], rows[:, HALF:D]), dve_waited)
                    step(dve.bn_aggr(mean_var[:, s, :], stats[:, s, :]))
                    dve.tensor_scalar(var_eps[:, s:s + 1], mean_var[:, s, 1:2], LN_EPS, None, ALU.add).then_inc(ln_var, 1)
                    dve.wait_ge(ln_rstd, t + 1)
                    if first or s:
                        if not last:
                            after(dve, ln_back, t - 1)
                    elif not last:
                        after(dve, ln_back, 2 * i)
                    dve.tensor_scalar(x_hat[:, s, :], rows, mean_var[:, s, 0:1], rstd[:, s:s + 1], ALU.subtract,
                                      ALU.mult).then_inc(ln_norm, 1)
                    if last:
                        after(dve, ln_norm, t + 1)
                        dve.wait_ge(out_stored[s], i * 16 + 16)
                        dve.tensor_tensor(out_tile[:, s, :], x_hat[:, s, :], g_row[:, :], ALU.mult).then_inc(out_scaled, 1)
            step.end(tiles // 2)

        def split_modulated(layer):
            with dve.Fori(0, KT // 2) as i:
                for s in range(2):
                    k = 2 * i + s
                    dve.wait_ge(mod_done, 2 * i + (layer * KT + s + 1))
                    dve.tensor_copy(col(u_hi, k), u_tmp[:, s, :]).then_inc(mod_hi, 1)
                    dve.wait_ge(mod_hi, 2 * i + (layer * KT + s + 1))
                    dve.tensor_tensor(col(u_lo, k), u_tmp[:, s, :], col(u_hi, k).bitcast(F32), ALU.subtract).then_inc(mod_split, 1)

        heads = (slice(0, HD), slice(HD, P))

        def split_queries(parts, src):
            for r, part in zip(heads, parts):
                step(dve.tensor_copy(part[r, :], src[r, :]))
            for r, o, part in zip(heads, heads[::-1], parts):
                dve.tensor_tensor(part[o, :], src[r, :], part[r, :].bitcast(F32), ALU.subtract).then_inc(q_split, 1)

        def split_keys(hi, lo, src):
            for r, part in zip(heads, hi):
                step(dve.tensor_copy(part[r, :], src[r, :]))
            for r, o, part in zip(heads, heads[::-1], hi):
                dve.tensor_copy(part[o, :], src[r, :]).then_inc(k_split, 1)
                dve.tensor_tensor(lo[r, :], src[r, :], part[r, :].bitcast(F32), ALU.subtract).then_inc(k_split, 1)

        swap = [(n + 16) % 32 for n in range(32)]

        def rotate():
            step(dve.stream_shuffle(a_swap[:, :], a_tmp[:, 0:S], swap))
            step(dve.tensor_tensor(a_swap[:, :], a_swap[:, :], rope_sin[:, :], ALU.mult))
            step(dve.tensor_tensor(a_tmp[:, 0:S], a_tmp[:, 0:S], rope_cos[:, :], ALU.mult))
            step(dve.tensor_tensor(a_tmp[:, 0:S], a_tmp[:, 0:S], a_swap[:, :], ALU.add))

        def take_values(places, v_base):
            for n, v in enumerate(places):
                dve.wait_ge(v_turned, v_base + (n + 1))
                rows, width = v.shape[1:]
                dve.tensor_copy(v, bank(4 + n % 2)[:, 0:rows * width].rearrange("p (t n) -> p t n", n=width)).then_inc(v_ready, 1)

        def softmax(h0, p0, steps, width, mask, start, prob_t, logits, ready, gate):
            def logit(s):
                if s >= SLOTS:
                    dve.wait_ge(pt_done, h0 + (s - SLOTS + 1))
                ready(s)
                dve.wait_ge(score_done, h0 + (s + 1)).then_inc(dve_waited, 1)
                c0, n = width(s), s % SLOTS
                dve.tensor_tensor_reduce(logits[n][:, c0 + 1:KEYS + 1], ps_score[s % 2][:, P + c0:P + KEYS], mask(s), -1.0,
                                         start(s), ALU.add, ALU.min, neg_max[:, n:n + 1]).then_inc(logit_done, 1)

            def reciprocal(s):
                dve.wait_ge(prob_done, h0 + (s + 1))
                n = s % SLOTS
                dve.reciprocal(row_rec[:, n:n + 1], row_sum[:, n:n + 1]).then_inc(rec_done, 1)

            def take_probs(s):
                dve.wait_ge(pt_done, h0 + (s + 1))
                after(dve, pv_done, p0 + s // 2)
                d = dve_tiles((KEYS - width(s)) // P)
                dve.tensor_copy(prob_t[:, 0:d, s % 2, :], ps_pt[:, 0:d * P].rearrange("p (t q) -> p t q", q=P)).then_inc(pt_dve, 1)

            def gate_output(p):
                after(dve, pv_done, p0 + (p + 1))
                for h, r in enumerate(heads):
                    out, y = gate(p, ps_out[p % 2][r, h * P:(h + 1) * P], r)
                    dve.tensor_tensor(y, out, y, ALU.mult).then_inc(gated, 1)

            for s in range(2):
                logit(s)
            for s in range(2):
                reciprocal(s)
            for s in range(2, 4):
                logit(s)
            for p in range(steps // 2):
                for s in (2 * p, 2 * p + 1):
                    take_probs(s)
                    if s % 2 and s + 1 < steps:
                        reciprocal(s + 1)
                    if s + 4 < steps:
                        logit(s + 4)
                if 2 * p + 3 < steps:
                    reciprocal(2 * p + 3)
                if p:
                    gate_output(p - 1)
            gate_output(steps // 2 - 1)

        def split_outputs(layer, tokens):
            with dve.Fori(0, KT) as k:
                dve.wait_ge(o_hi_done, k + (layer * KT + 1))
                dve.tensor_tensor(col(u_lo, k, 0, tokens), col(act_buf, k, 0, tokens),
                                  col(u_hi, k, 0, tokens).bitcast(F32), ALU.subtract).then_inc(o_split, 1)

        def residual_sums(layer, c, chunks):
            if layer == 0:
                dve.wait_ge(o_split, KT)
            else:
                dve.wait_ge(o_split, 2 * KT)
            count = len(chunks)
            with dve.Fori(0, KT // 2) as i:
                for s in range(2):
                    o = 2 * i + s
                    dve.wait_ge(res_loaded[s], i * 16 + (layer * 16 * (KT // 2) + 16))
                    for n, (t0, tn) in enumerate(chunks):
                        l = s * count + n
                        wait_chunk(2 * count * i + (c + l))
                        g = ada[:, bass.ds(o + (24 * layer + 16), 1), n // 2].rearrange("p a -> p a")
                        dve.scalar_tensor_tensor(col(act_buf, o, t0, t0 + tn), pj[l % 2][:, 0:tn], g, res[:, s, t0:t0 + tn],
                                                 ALU.mult, ALU.add).then_inc(pj_free[l % 2], 1)

        normalise(0, S // P)
        split_modulated(0)
        dve.wait_ge(ctx_loaded, 16 * 4)
        for m in range(2):
            c = A_CHUNK + 30 * m
            for b, v in free_counts(c // 2, 0, 3).items():
                after(dve, pj_free[b], v)
            rotate()
            split_keys(ak_hi, ak_lo, a_tmp)
            take_values([av[:, 0:4, :], av[:, 4:8, :], av[:, 8:10, :]], VSETS_A * m)
            with dve.Fori(0, 4) as i:
                step.begin(i, 7)
                half = 3 * i + (c // 2 + 3)
                h0, p0 = i * A_STEPS + 4 * m * A_STEPS, i * A_TILES + 4 * m * A_TILES
                for b, v in free_counts(half, 0, 3).items():
                    after(dve, pj_free[b], v).then_inc(dve_waited, 1)
                rotate()
                split_queries(aq_parts, a_tmp)
                dve.wait_ge(q_split, 2 * i + 2 * (4 * m + 1))
                for n in range(SLOTS):
                    ins = dve.tensor_copy(alog[n][:, KEYS + 1:KEYS + 2], sink_neg[:, bass.ds(2 * i + (8 * m + n % 2), 1)])
                step(ins)

                def gate(p, out, r):
                    return out, act_buf[r, bass.ds(i + 4 * m, 1), p * P:(p + 1) * P].rearrange("p a n -> p (a n)")

                softmax(h0, p0, A_STEPS, lambda s: a_tile(s // 2)[0],
                        lambda s: a_mask[:, a_tile(s // 2)[3]:a_tile(s // 2)[3] + KEYS - a_tile(s // 2)[0]],
                        lambda s: alog[s % SLOTS][:, KEYS + 1:KEYS + 2], aprob_t, alog, lambda s: None, gate)
            step.end(4)
        split_outputs(0, TC)
        residual_sums(0, AO_CHUNK, ALL_CHUNKS)
        normalise(S // P, TC // P)
        split_modulated(1)
        with dve.Fori(0, PAIRS) as j:
            step.begin(j, 4)
            half = 5 * j + B_CHUNK // 2
            h0, p0 = j * B_STEPS + STEPS_A, j * B_TILES + OT_A
            for b, v in free_counts(half, 0, 2).items():
                after(dve, pj_free[b], v)
            split_queries(bq_parts, b_tmp_q)
            for b, v in free_counts(half, 2, 3).items():
                after(dve, pj_free[b], v)
            split_keys(bk_hi, bk_lo, b_tmp_k)
            take_values([act_buf[:, 2 * n:2 * n + 2, S:TC] for n in range(4)] + [bv_ctx[:, :, :]], j * VSETS_B + 2 * VSETS_A)

            def built(s):
                t, h = s // 2, s % 2
                b = 3 * (t // 4) + COL_TYPE[t % 4]
                dve.wait_ge(bias_ready, j * (2 * B_BUILDS) + (2 * b + h + 1))

            def bias_of(s):
                t, h = s // 2, s % 2
                return bias[:, h, (3 * (t // 4) + COL_TYPE[t % 4]) % 2, :]

            def gate(p, out, r):
                half_rows, cb = p // 4, p % 4
                y = act_buf[r, bass.ds(j, 1), half_rows * HALF:(half_rows + 1) * HALF].rearrange("p a (r c) -> p (a r) c", c=GRID)
                return out.rearrange("p (r c) -> p r c", c=16), y[:, :, cb * 16:(cb + 1) * 16]

            softmax(h0, p0, B_STEPS, lambda s: 0, bias_of, lambda s: NO_MAX, bprob_t, blog, built, gate)
        step.end(PAIRS)
        split_outputs(1, S)
        residual_sums(1, BO_CHUNK, LAT_CHUNKS)
        dve.wait_ge(ctx_loaded, 16 * 6)
        normalise(S // P + TC // P, S // P, last=True)

    ctx.close()


def columns_of(w, cols):
    return w[:, cols].reshape(KT, P, P).transpose(1, 0, 2).reshape(P, UNIT)


def four_tiles(w, ot):
    return w[:, ot * P:(ot + 2) * P].reshape(4, P, 2, P).transpose(1, 2, 0, 3).reshape(P, UNIT)


def weight_units(w_in, w_grp, w_out, a_in, a_out, b_in, b_out):
    units, span = [], np.arange(P)
    width = GROUPS * HALF
    for g in range(GROUPS):
        units += [columns_of(w_in, g * HALF + i * P + span) for i in range(4)]
        units += [columns_of(w_in, width + g * HALF + i * P + span) for i in range(4)]
        units += [four_tiles(w_grp[g], ot) for ot in (0, 2)]
        units += [four_tiles(w_out[g * HALF:(g + 1) * HALF], ot) for ot in (0, 2, 4, 6)]
    pairs = np.concatenate([pair_heads(jj) for jj in range(PAIRS)])
    for m in range(2):
        units += [columns_of(a_in, D + m * P + span), columns_of(a_in, D + 2 * P + m * P + span)]
        for i in range(4):
            heads = pair_heads(4 * m + i)
            units += [columns_of(a_in, heads), columns_of(a_in, D + 4 * P + heads)]
    units += [columns_of(a_out[pairs], ot * P + span) for ot in range(KT)]
    for j in range(PAIRS):
        units += [columns_of(b_in, part * D + j * P + span) for part in range(4)]
    units += [columns_of(b_out, ot * P + span) for ot in range(KT)]
    assert len(units) == ALL_UNITS
    return np.stack(units)


def pair_heads(jj):
    m, i = jj // 4, jj % 4
    return np.concatenate([(8 * m + 4 * h + i) * HD + np.arange(HD) for h in range(2)])


def turned(x):
    return x.T.reshape(KT, P, -1).transpose(1, 0, 2)


def by_feature(v):
    return v.reshape(-1, P).T


def shape_tables():
    t = {"ident": np.eye(P)}
    n = np.arange(PAD)
    t["corr"] = np.broadcast_to(np.stack([w / np.minimum(n + 1, w) for w in WINDOWS]), (P, GROUPS, PAD))
    p = np.arange(P)
    rr, qq = p // 16, p % 16
    row_mask = np.zeros((P, 2, KEY_ROWS))
    for half in range(2):
        first = np.clip(8 * half + rr - 4, 0, ROWS - 8)[:, None]
        key = 4 * half + np.arange(KEY_ROWS)
        row_mask[:, half] = np.where((key >= first) & (key < first + 8), 0, MASKED)
    col_mask = np.zeros((P, 3, KEY_COLS))
    for kind, cb in enumerate((0, 1, 3)):
        first = np.clip(cb * 16 + qq - 8, 0, GRID - 16)[:, None]
        key = KEY_COL[cb] + np.arange(KEY_COLS)
        col_mask[:, kind] = np.where((key >= first) & (key < first + 16), 0, MASKED)
    t["row_mask"], t["col_mask"] = row_mask, col_mask
    col = np.arange(P)
    before, behind = (np.where(seen, 0, MASKED) for seen in (col[None] >= p[:, None], col[None] <= p[:, None]))
    a_mask = np.zeros((P, 9, P))
    a_mask[:, 0], a_mask[:, 2], a_mask[:, 5] = before, behind, before
    a_mask = a_mask.reshape(P, 9 * P)
    t["a_mask"] = a_mask
    freq = np.float32(10000.0) ** (-(p % 16).astype(np.float32) / np.float32(16))
    tok = np.arange(S)
    place = np.where((p // 32 % 2 == 0)[:, None], tok // GRID, tok % GRID).astype(np.float32)
    angle = place * freq[:, None]
    t["rope_cos"] = np.cos(angle)
    t["rope_sin"] = np.sin(angle) * np.where(p % 32 < 16, -1, 1)[:, None]
    return t


def kernel(**inputs):
    import concourse.bacc as bacc
    from concourse.bass_utils import run_bass_kernel_spmd

    x = {n: np.asarray(v) for n, v in inputs.items()}
    arrays = shape_tables()
    arrays["weights"] = weight_units(x["pool_w_in"][0], x["pool_w_grp"][0], x["pool_w_out"][0], x["a_w_in_2"][0],
                                     x["a_w_out_2"][0], x["b_w_in_2"][0], x["b_w_out_2"][0])
    arrays["w_ada"] = x["w_ada_2"].transpose(0, 2, 1).reshape(ADA_UNITS, P, D)
    arrays["x_t"], arrays["ctx_t"] = turned(x["x"][0]), turned(x["ctx_2"][0])
    arrays["c_rows"] = np.stack([x["c_2"][0], x["c_ctx_2"]])
    arrays["vecs"] = np.concatenate([by_feature(x[n]) for n in ("ln_g", "ln_b")]
                                    + [by_feature(x[n][0]) for n in ("ln_g_2", "ln_b_2")]
                                    + [by_feature(x["pool_scale"][0]), by_feature(x["b_ada_2"])], axis=1)
    arrays["ln_g3"], arrays["ln_b3"] = x["ln_g_2"][1:2], x["ln_b_2"][1:2]
    arrays["sink"] = x["a_sink_2"][:, [8 * (jj // 4) + 4 * h + jj % 4 for jj in range(PAIRS) for h in range(2)]]
    tab = np.zeros((HEADS, TAB_R, TAB_C), np.float32)
    tab[:, 4:19, 16:47] = x["b_rel_bias_2"][0]
    arrays["bias_tab"] = tab[:, ::-1, ::-1].reshape(HEADS, TAB_R * TAB_C)
    arrays = {n: np.ascontiguousarray(v, dtype=np.float32) for n, v in arrays.items()}

    nc = bacc.Bacc("TRN2", target_bir_lowering=False, num_devices=1)
    aps = {n: nc.dram_tensor(n + "_in", v.shape, F32, kind="ExternalInput").ap() for n, v in arrays.items()}
    aps["out"] = nc.dram_tensor("out", (S // P, P, D), F32, kind="ExternalOutput").ap()
    build(nc, aps)
    r = run_bass_kernel_spmd(nc, [{n + "_in": v for n, v in arrays.items()}], core_ids=[0])
    return r.results[0]["out"].reshape(1, S, D)
```

```python
from contextlib import ExitStack

import numpy as np

import concourse.bass as bass
from concourse import mybir

F32 = mybir.dt.float32
F32R = mybir.dt.float32r
ALU = mybir.AluOpType
ACT = mybir.ActivationFunctionType

P = 128
D = 1024
S = 1024
C = 256
TC = S + C
KT = D // P
HALF = 512
UNIT = KT * P
HD = 64
HEADS = 16
PAIRS = HEADS // 2
Q_SCALE = HD ** -0.5
LN_EPS = 1e-5
ALPHA_1 = 2.0 ** 0.25
ALPHA_2 = 4.0 ** 0.25
MASKED = -1e30
NO_MAX = 3e38
SLOTS = 4

GROUPS = 4
WINDOWS = (2, 4, 8, 16)
PAD = 16
L1_UNITS = 14
L1_CHUNKS = 8 * 2 + 2 * 4 + 4 * 4
L1_ENDS = [2 * (n + 1) for n in range(8)] + [20, 24] + [28, 32, 36, 40]
ADA = 12
ADA_UNITS = 48

A_UNIT = GROUPS * L1_UNITS
AO_UNIT = A_UNIT + 20
B_UNIT = AO_UNIT + KT
BO_UNIT = B_UNIT + 4 * PAIRS
ALL_UNITS = BO_UNIT + KT
A_CHUNK = GROUPS * L1_CHUNKS
AO_CHUNK = A_CHUNK + 20 * 3
B_CHUNK = AO_CHUNK + 8 * 3
BO_CHUNK = B_CHUNK + 10 * PAIRS
LAT_CHUNKS = [(0, HALF), (HALF, HALF)]
ALL_CHUNKS = LAT_CHUNKS + [(S, C)]
MODS = [(ch, k) for ch in range(len(ALL_CHUNKS)) for k in range(KT)]
MOD_SLOTS = 4
ROW_SLOTS = 3


def mods_after(t, tiles):
    per = {4: (0, 2), 5: (2, 4), 6: (4, 6), 7: (6, 8), 8: (8, 12), 9: (12, 16)}
    rest = [n for v, (_, hi) in per.items() if v < tiles for n in [hi]][-1]
    if t == tiles:
        return range(rest, len(MODS))
    return range(*per.get(t, (0, 0)))

A_TILES = S // P + C // P
A_STEPS = 2 * A_TILES
GRID = 64
ROWS = S // GRID
B_TILES = 8
B_STEPS = 2 * B_TILES
KEY_COL = (0, 8, 24, 32)
COL_TYPE = (0, 1, 1, 2)
KEY_ROWS, KEY_COLS = 12, 32
LAT_KEYS = KEY_ROWS * KEY_COLS
KEYS = LAT_KEYS + C
TAB_R, TAB_C = 23, 63
TAB_RUN = TAB_R * TAB_C - (7 * TAB_C + 15)
TAB_ROWS = 16
B_BUILDS = 6
LAST_BIAS_USE = ((1, 6), (1, 7), (0, 0), (0, 2), (0, 3), (0, 4))
STEPS_A = PAIRS * A_STEPS
OT_A = PAIRS * A_TILES
VSETS_A, VSETS_B = 3, 5


def free_counts(first_half, l0, n):
    last = {}
    for l in range(l0, l0 + n):
        last[l % 2] = first_half + (l // 2 + 1)
    return last


class Chain:

    def __init__(self, eng, sem):
        self.eng, self.sem, self.base, self.local, self.at, self.per = eng, sem, 0, 0, 0, 0

    def begin(self, at, per):
        self.base += self.local if self.per == 0 else 0
        self.at, self.per, self.local = at, per, 0

    def end(self, times):
        assert self.local == self.per, (self.local, self.per)
        self.base += self.per * times
        self.at = self.per = self.local = 0

    def __call__(self, ins, alone=None):
        ins.then_inc(self.sem, 1)
        self.local += 1
        wait = self.eng.wait_ge(self.sem, self.at * self.per + (self.base + self.local))
        if alone is not None:
            wait.then_inc(alone, 1)


def build(nc, a):
    ctx = ExitStack()
    sems = {}

    def sem(name):
        sems[name] = ctx.enter_context(nc.semaphore(name))
        return sems[name]

    base = (nc.sbuf_base + 63) // 64 * 64
    at = [base]
    limit = nc.sbuf_usable_end

    def sb(name, shape, dt=F32, offset=None):
        size = 4 * int(np.prod(shape[1:]))
        size = (size + 31) // 32 * 32
        where = at[0] if offset is None else offset
        assert where + size <= limit, (name, where + size - limit)
        if offset is None:
            at[0] += size
        return nc.alloc_sbuf_tensor_at(name, shape, dt, offset=where)

    w_raw = sb("w_raw", [P, 2, UNIT])
    w_hi = sb("w_hi", [P, 2, UNIT], F32R)
    w_lo = sb("w_lo", [P, 2, UNIT], F32R)
    ident = sb("ident", [P, P])
    vecs = sb("vecs", [P, 4 * KT + 16 + ADA_UNITS])
    ln_g1, ln_b1, ln_g2, ln_b2 = (vecs[:, KT * n:KT * (n + 1)] for n in range(4))
    pool_scale = vecs[:, 4 * KT:4 * KT + 16]
    b_ada = vecs[:, 4 * KT + 16:]
    ada = sb("ada", [P, ADA_UNITS, 2])
    par = sb("par", [P, 12, KT])
    sink_neg = sb("sink_neg", [P, HEADS])
    corr = sb("corr", [P, GROUPS, PAD])
    minus_half = sb("minus_half", [P, 1])
    stats = sb("stats", [P, ROW_SLOTS, 12])
    mean_var = sb("mean_var", [P, ROW_SLOTS, 2])
    var_eps = sb("var_eps", [P, ROW_SLOTS])
    neg_mean = sb("neg_mean", [P, ROW_SLOTS])
    rstd = sb("rstd", [P, ROW_SLOTS])
    neg_max = sb("neg_max", [P, SLOTS])
    row_sum = sb("row_sum", [P, SLOTS])
    row_rec = sb("row_rec", [P, SLOTS])
    row_mask = sb("row_mask", [P, 2, KEY_ROWS])
    col_mask = sb("col_mask", [P, 3, KEY_COLS])
    ada_at = at[0]
    w_ada = sb("w_ada", [P, UNIT])
    act_buf = sb("act_buf", [P, KT, TC])
    region = at[0]

    x_hi = sb("x_hi", [P, KT, S], F32R)
    x_lo = sb("x_lo", [P, KT, S], F32R)
    m_hi = sb("m_hi", [P, 4, S], F32R)
    m_lo = sb("m_lo", [P, 4, S], F32R)
    sz01 = sb("sz01", [P, 2, S])
    g_at = at[0]
    g_hi = sb("g_hi", [P, 4, S], F32R)
    g_lo = sb("g_lo", [P, 4, S], F32R)
    u_pad = sb("u_pad", [P, PAD + S], offset=g_at)
    win = [sb(f"win{n}", [P, PAD + S], offset=g_at + (n + 1) * 4 * (PAD + S)) for n in range(2)]
    c_in = sb("c_in", [P, 2, D], offset=g_at + 3 * 4 * (PAD + S))

    def gate_tile(n):
        if n < 2:
            return sz01[:, n, :].rearrange("p (a b) -> p a b", b=C)
        return act_buf[:, 4 * (n - 2):4 * (n - 2) + 4, S:TC]

    at[0] = region
    u_hi = sb("u_hi", [P, KT, TC], F32R)
    u_lo = sb("u_lo", [P, KT, TC], F32R)
    after_u = at[0]
    x_hat = sb("x_hat", [P, 2, D], offset=after_u + 12288 + 8192)
    u_tmp = sb("u_tmp", [P, MOD_SLOTS, HALF], offset=after_u)
    out_tile = sb("out_tile", [P, 2, D], offset=after_u + 12288 + 16384)
    g_row = sb("g_row", [P, D], offset=after_u + 12288 + 24576)
    b_row = sb("b_row", [P, D], offset=after_u + 12288 + 28672)
    res = sb("res", [P, 2, TC], offset=after_u)

    def attention_part(x, q_len, v_tiles, slots):
        q_parts = [sb(f"{x}q_parts{h}", [P, q_len], F32R) for h in range(2)]
        k_hi = [sb(f"{x}k_hi{h}", [P, TC], F32R) for h in range(2)]
        k_lo = sb(x + "k_lo", [P, TC], F32R)
        v = sb(x + "v", [P, v_tiles, P])
        work = at[0]
        logits = [sb(f"{x}logits{n}", [P, KEYS + 2]) for n in range(slots)]
        probs_t = sb(x + "probs_t", [P, 2, KEYS // P, P])
        return q_parts, k_hi, k_lo, v, work, logits, probs_t

    aq_parts, ak_hi, ak_lo, av, work_a, alog, aprob_t = attention_part("a_", TC, 10, SLOTS - 1)
    alog.append(sb("a_logits_last", [P, KEYS + 2], offset=ada_at))
    rope_cos = sb("rope_cos", [P, S])
    rope_sin = sb("rope_sin", [P, S])
    a_mask = sb("a_mask", [P, 9 * P])
    a_tmp = sb("a_tmp", [P, TC], offset=work_a)
    a_swap = sb("a_swap", [P, S], offset=work_a + 4 * TC)
    at[0] = after_u
    bq_parts, bk_hi, bk_lo, bv_ctx, work_b, blog, bprob_t = attention_part("b_", S, C // P, SLOTS)
    bias = sb("bias", [P, 2, 2, KEYS])
    tab = [sb("tab0", [P, TAB_ROWS * TAB_C], offset=ada_at), sb("tab1", [P, TAB_ROWS * TAB_C])]

    def b_value(t):
        return bv_ctx[:, t - 16, :] if t >= 16 else act_buf[:, t // 2, S + t % 2 * P:S + (t % 2 + 1) * P]

    b_tmp_q = sb("b_tmp_q", [P, S], offset=work_b)
    b_tmp_k = sb("b_tmp_k", [P, TC], offset=work_b + 4 * S)
    b_vt = sb("b_vt", [P, 4 * HALF + C], offset=work_b)

    psum = ctx.enter_context(nc.psum_tensor("psum", [P, 8 * HALF], F32))

    def bank(n, count=1):
        return psum[:, n * HALF:(n + count) * HALF]

    pj = [bank(6), bank(7)]
    ps_score = [bank(0, 2), bank(2, 2)]
    ps_pt = bank(4, 2)
    ps_rows = [bank(2 * n, 2) for n in range(ROW_SLOTS)]
    ps_back = bank(6, 2)
    PT_ACT = HALF
    ps_out = [t[:, 0:P] for t in pj]
    c_silu = [bank(2 * who, 2) for who in range(2)]
    ada_products = bank(4, 2)

    residual = [nc.dram_tensor(f"residual{n}", [KT, P, TC if n == 0 else S], F32, kind="Internal").ap()
                for n in range(2)]

    w_loaded = [sem("w_loaded0"), sem("w_loaded1")]
    w_hi_done, w_split = sem("w_hi_done"), sem("w_split")
    ada_loaded, ada_done = sem("ada_loaded"), sem("ada_done")
    pj_done, pj_free = sem("pj_done"), [sem("pj_free0"), sem("pj_free1")]
    const_loaded, ctx_loaded = sem("const_loaded"), sem("ctx_loaded")
    x_loaded = [sem(f"x_loaded{k}") for k in range(KT)]
    x_hi_done, x_split, x_scaled, c_ready = sem("x_hi_done"), sem("x_split"), sem("x_scaled"), sem("c_ready")
    u_used, m_split, g_hi_done, g_split = sem("u_used"), sem("m_split"), sem("g_hi_done"), sem("g_split")
    ln_turned, ln_var, ln_rstd, ln_centred = sem("ln_turned"), sem("ln_var"), sem("ln_rstd"), sem("ln_centred")
    ln_norm, ln_back, ln_stored = sem("ln_norm"), sem("ln_back"), sem("ln_stored")
    par_ready = sem("par_ready")
    mod_done, mod_split = sem("mod_done"), sem("mod_split")
    res_ready, res_stored = sem("res_ready"), sem("res_stored")
    res_loaded = [sem("res_loaded0"), sem("res_loaded1")]
    q_split, k_split = sem("q_split"), sem("k_split")
    v_turned, v_ready = sem("v_turned"), sem("v_ready")
    tab_loaded, bias_ready = sem("tab_loaded"), sem("bias_ready")
    score_done, logit_done, prob_done = sem("score_done"), sem("logit_done"), sem("prob_done")
    rec_done, prob_scaled = sem("rec_done"), sem("prob_scaled")
    pt_done, pt_dve, pt_act = sem("pt_done"), sem("pt_dve"), sem("pt_act")
    pv_done, gated = sem("pv_done"), sem("gated")
    o_hi_done, o_split = sem("o_hi_done"), sem("o_split")
    out_scaled, out_ready = sem("out_scaled"), sem("out_ready")
    out_stored = [sem("out_stored0"), sem("out_stored1")]
    dve_step, pool_step = sem("dve_step"), sem("pool_step")
    dve_waited, pool_waited = sem("dve_waited"), sem("pool_waited")

    block = ctx.enter_context(nc.Block())

    def start_at_one(eng, ready, value, signals):
        for s in signals:
            eng.wait_ge(ready, value).then_inc(s, 1)

    def after(eng, signal, count):
        return eng.wait_ge(signal, count + 1)

    def dve_tiles(n):
        return max(1, n - 2)

    def one(ap):
        return ap.rearrange("a p n -> (a p) n")

    def col(t, n, lo=None, hi=None):
        lo, hi = lo or 0, hi or t.shape[2]
        return t[:, bass.ds(n, 1), lo:hi].rearrange("p a n -> p (a n)")

    def a_tile(t):
        latent, ctx = KEYS - C, (KEYS - C, S, C)
        if t >= S // P:
            return latent, [ctx], [8, 9], 3 * P
        if t == 0:
            return P, [(P, 0, 2 * P), ctx], [0, 1, 8, 9], P
        if t == S // P - 1:
            return P, [(P, (t - 1) * P, 2 * P), ctx], [t - 1, t, 8, 9], 5 * P
        return 0, [(0, (t - 1) * P, 3 * P), ctx], [t - 1, t, t + 1, 8, 9], 0

    def load_tab(sp, j, h):
        table = a["bias_tab"][bass.ds(2 * j + h, 1)]
        runs = bass.AP(tensor=table.tensor, offset=table.offset, ap=[[TAB_C, 8], [1, 16], [1, TAB_RUN]])
        sp.dma_start(tab[h][:, 0:TAB_RUN], runs).then_inc(tab_loaded, 16)

    def residual_loads(act, layer, c, chunks):
        tokens = (TC, S)[layer]

        def load(o, s):
            act.dma_start(res[:, s, 0:tokens], one(residual[layer][bass.ds(o, 1)])).then_inc(res_loaded[s], 16)

        act.wait_ge(res_stored, 16 * KT * (layer + 1))
        for s in range(2):
            load(s, s)
        with act.Fori(0, KT // 2 - 1) as i:
            for s in range(2):
                for b, v in free_counts(len(chunks) * i + c // 2, s * len(chunks), len(chunks)).items():
                    after(act, pj_free[b], v)
                load(2 * i + (2 + s), s)

    @block.sync
    def _(sp):
        def load_unit(n, slot):
            sp.dma_start(w_raw[:, slot, :], one(a["weights"][bass.ds(n, 1)])).then_inc(w_loaded[slot], 16)

        def next_unit(n, slot):
            sp.wait_ge(w_split, n + 1)
            load_unit(n + 2, slot)

        for k in range(KT):
            sp.dma_start(act_buf[:, k, 0:S], a["x_t"][:, k, :]).then_inc(x_loaded[k], 16)
            if k < 2:
                load_unit(k, k)
        with sp.Fori(0, GROUPS) as g:
            for l in range(L1_UNITS):
                next_unit(g * L1_UNITS + l, l % 2)
                if l < ADA:
                    after(sp, ada_done, g * ADA + l)
                    sp.dma_start(w_ada[:, :], one(a["w_ada"][bass.ds(g * ADA + l, 1)])).then_inc(ada_loaded, 16)
        sp.wait_ge(g_split, 8 * GROUPS)
        sp.dma_start(act_buf[:, :, S:TC], a["ctx_t"]).then_inc(ctx_loaded, 16)
        sp.wait_ge(pj_done, A_CHUNK)
        for dst, src in ((rope_cos, "rope_cos"), (rope_sin, "rope_sin"), (a_mask, "a_mask")):
            sp.dma_start(dst[:, :], a[src]).then_inc(ctx_loaded, 16)
        for n in (A_UNIT, A_UNIT + 1):
            next_unit(n, n % 2)
        with sp.Fori(0, KT) as k:
            sp.wait_ge(res_ready, k + 1)
            sp.dma_start(one(residual[0][bass.ds(k, 1)]), col(act_buf, k)).then_inc(res_stored, 16)
        with sp.Fori((A_UNIT + 2) // 2, B_UNIT // 2 + 1) as i:
            for s in range(2):
                next_unit(2 * i + s, s)
        for h in range(2):
            load_tab(sp, 0, h)
        with sp.Fori(0, KT) as k:
            sp.wait_ge(res_ready, k + (KT + 1))
            sp.dma_start(one(residual[1][bass.ds(k, 1)]), col(act_buf, k, 0, S)).then_inc(res_stored, 16)
        with sp.Fori(0, PAIRS - 1) as j:
            for l in range(4):
                next_unit(4 * j + (B_UNIT + 2 + l), l % 2)
            sp.wait_ge(bias_ready, (j + 1) * (2 * B_BUILDS))
            for h in range(2):
                load_tab(sp, j + 1, h)
        with sp.Fori((B_UNIT + 2 + 4 * (PAIRS - 1)) // 2, (ALL_UNITS - 2) // 2) as i:
            for s in range(2):
                next_unit(2 * i + s, s)
        after(sp, gated, OT_A + PAIRS * B_TILES)
        for dst, src in ((g_row, "ln_g3"), (b_row, "ln_b3")):
            sp.dma_start(dst[:, :], bass.AP(tensor=a[src].tensor, offset=0, ap=[[0, P], [1, D]])).then_inc(ctx_loaded, 16)
        for s in range(2):
            sp.wait_ge(ctx_loaded, 16 * 4).then_inc(out_stored[s], 16)
        with sp.Fori(0, S // P // 2) as i:
            for s in range(2):
                sp.wait_ge(out_ready, 2 * i + (s + 1))
                sp.dma_start(one(a["out"][bass.ds(2 * i + s, 1)]), out_tile[:, s, :]).then_inc(out_stored[s], 16)
        for s in range(2):
            sp.wait_ge(out_stored[s], 16 * (S // P // 2) + 16)
        sp.wait_ge(res_stored, 16 * 2 * KT)

    @block.gpsimd
    def _(pool):
        step = Chain(pool, pool_step)

        def loads(turn):
            return 16 * turn + 16

        def split(n, slot, loaded, used=None):
            pool.wait_ge(w_loaded[slot], loaded)
            if used is not None:
                pool.wait_ge(pj_done, used).then_inc(pool_waited, 1)
            pool.tensor_copy(w_hi[:, slot, :], w_raw[:, slot, :]).then_inc(w_hi_done, 1)
            pool.wait_ge(w_hi_done, n + 1)
            pool.tensor_tensor(w_lo[:, slot, :], w_raw[:, slot, :], w_hi[:, slot, :].bitcast(F32),
                               ALU.subtract).then_inc(w_split, 1)

        pool.memset(minus_half[:, :], -0.5).then_inc(pool_step, 1)
        step.base += 1
        for n in range(2):
            split(n, n, loads(0))
        with pool.Fori(0, GROUPS) as g:
            for l in range(L1_UNITS):
                split(g * L1_UNITS + (l + 2), l % 2,
                      loads(g * (L1_UNITS // 2) + (l + 2) // 2), g * L1_CHUNKS + L1_ENDS[l])

        def root(t):
            n = slice(t % ROW_SLOTS, t % ROW_SLOTS + 1)
            pool.tensor_tensor(rstd[:, n], var_eps[:, n], minus_half[:, :], ALU.pow).then_inc(ln_rstd, 1)

        def rstds(first, tiles):
            if first == 0:
                pool.wait_ge(pool_step, 1)
            for t in range(tiles):
                pool.wait_ge(ln_var, first + t + 1)
                if t >= ROW_SLOTS:
                    after(pool, ln_norm, first + t - ROW_SLOTS + 1)
                root(t)

        def residuals(layer):
            pool.wait_ge(par_ready, layer + 1)
            for k in range(KT):
                pool.wait_ge(mod_done, len(MODS) * layer + 2 * KT + k + 1)
                x = act_buf[:, k, 0:S]
                ins = pool.tensor_scalar(x, x, par[:, 4 + 6 * layer, k:k + 1], par[:, 5 + 6 * layer, k:k + 1],
                                         ALU.mult, ALU.add)
                if layer == 0:
                    x = act_buf[:, k, S:TC]
                    ins = pool.tensor_scalar(x, x, ALPHA_2, None, ALU.mult)
                ins.then_inc(res_ready, 1)

        rstds(0, S // P)
        residuals(0)
        for m in range(2):
            n, c = A_UNIT + 10 * m, A_CHUNK + 30 * m
            for l in range(2):
                split(n + l + 2, l, loads((n + l + 2) // 2), c + 3 * (l + 1))
            with pool.Fori(0, 4) as i:
                for l in range(2):
                    split(2 * i + (n + 4 + l), l, loads(i + (n + 4) // 2), 6 * i + (c + 9 + 3 * l))
        with pool.Fori(0, KT // 2) as i:
            for l in range(2):
                split(2 * i + (AO_UNIT + 2 + l), l, loads(i + (AO_UNIT + 2) // 2),
                      6 * i + (AO_CHUNK + 3 + 3 * l))
        after(pool, gated, OT_A)
        pool.memset(bias[:, :, :, LAT_KEYS:KEYS], 0.0).then_inc(pool_step, 1)
        step.base += 1
        rstds(S // P, TC // P)
        residuals(1)
        step.begin(0, 0)

        def bias_tile(j, b):
            half, kind, slot = b // 3, b % 3, b % 2
            d = -4 * half
            e = -8 * kind
            r0, c0 = 11 - d, 31 - e
            for h in range(2):
                back, tile = LAST_BIAS_USE[b]
                pool.wait_ge(logit_done, j * B_STEPS + (STEPS_A - back * B_STEPS + 2 * tile + h + 1))
                src = tab[h][:, :].rearrange("p (r c) -> p r c", c=TAB_C)
                src = src[:, r0 - KEY_ROWS + 1:r0 + 1, c0 - KEY_COLS + 1:c0 + 1][:, ::-1, ::-1]
                dst = bias[:, h, slot, 0:LAT_KEYS].rearrange("p (r c) -> p r c", c=KEY_COLS)
                cm = col_mask[:, kind, :].rearrange("p (a c) -> p a c", a=1).to_broadcast([P, KEY_ROWS, KEY_COLS])
                rm = row_mask[:, half, :].rearrange("p (r a) -> p r a", a=1).to_broadcast([P, KEY_ROWS, KEY_COLS])
                step(pool.tensor_tensor(dst, src, cm, ALU.add))
                pool.tensor_tensor(dst, dst, rm, ALU.add).then_inc(bias_ready, 1)

        with pool.Fori(0, PAIRS) as j:
            step.begin(j, 2 * B_BUILDS)
            pool.wait_ge(tab_loaded, (j + 1) * 32)
            for b in range(2):
                bias_tile(j, b)
            for l, end in enumerate((2, 5, 8, 10)):
                split(4 * j + (B_UNIT + 2 + l), l % 2,
                      loads(2 * j + (B_UNIT + 2 + l) // 2), 10 * j + (B_CHUNK + end))
            for b in range(2, B_BUILDS):
                bias_tile(j, b)
        step.end(PAIRS)
        with pool.Fori(0, KT // 2 - 1) as i:
            for l in range(2):
                split(2 * i + (BO_UNIT + 2 + l), l, loads(i + (BO_UNIT + 2) // 2),
                      4 * i + (BO_CHUNK + 2 + 2 * l))
        last = S // P + TC // P
        pool.wait_ge(ctx_loaded, 16 * 6)
        for t in range(S // P + 1):
            if t < S // P:
                pool.wait_ge(ln_var, last + t + 1)
                if t >= ROW_SLOTS:
                    after(pool, out_scaled, t - ROW_SLOTS + 1)
                root(t)
            if t:
                after(pool, out_scaled, t)
                out = out_tile[:, (t - 1) % 2, :]
                pool.tensor_tensor(out, out, b_row[:, :], ALU.add).then_inc(out_ready, 1)

    @block.tensor
    def _(pe):
        def product(out, w, x, first, last):
            (wh, wl), (xh, xl) = w, x
            pe.matmul(out, wh, xh, start=first, stop=False)
            pe.matmul(out, wh, xl, start=False, stop=False)
            return pe.matmul(out, wl, xh, start=False, stop=last)

        def project(n, slot, half, l0, x_hi, x_lo, chunks, kts=KT, ready=None):
            pe.wait_ge(w_split, n + 1)
            l = l0
            for o in range(KT // kts):
                for ch, (t0, tn) in enumerate(chunks):
                    if ready and o == 0:
                        pe.wait_ge(*ready[ch])
                    after(pe, pj_free[l % 2], half + l // 2)
                    out = pj[l % 2][:, 0:tn]
                    for k in range(kts):
                        w = (o * kts + k) * P
                        mm = product(out, (w_hi[:, slot, w:w + P], w_lo[:, slot, w:w + P]),
                                     (x_hi[:, k, t0:t0 + tn], x_lo[:, k, t0:t0 + tn]), k == 0, k == kts - 1)
                    mm.then_inc(pj_done, 1)
                    l += 1

        start_at_one(pe, x_split, 1, (ln_back, pv_done))
        pe.wait_ge(x_split, KT)
        with pe.Fori(0, GROUPS) as g:
            l = 0
            for u in range(L1_UNITS):
                if u == 8:
                    pe.wait_ge(m_split, g * 4 + 4)
                n, half = g * L1_UNITS + u, g * (L1_CHUNKS // 2)
                if u < 8:
                    project(n, u % 2, half, l, x_hi, x_lo, LAT_CHUNKS)
                    l += 2
                else:
                    ready = [(g_split, g * 8 + 7), (g_split, g * 8 + 8)] if u == 10 else None
                    project(n, u % 2, half, l, *((m_hi, m_lo) if u < 10 else (g_hi, g_lo)), LAT_CHUNKS, kts=4, ready=ready)
                    l += 4

        def normalise(first, tiles, chunks, last=False):
            def to_rows(t):
                if t >= ROW_SLOTS:
                    if last:
                        pe.wait_ge(ln_centred, t - ROW_SLOTS + 1)
                    else:
                        after(pe, ln_norm, first + t - ROW_SLOTS + 1)
                for k in range(KT):
                    tr = pe.transpose(ps_rows[t % ROW_SLOTS][:, k * P:(k + 1) * P], act_buf[:, k, t * P:(t + 1) * P],
                                      ident[:, :])
                tr.then_inc(ln_turned, 1)

            def to_columns(t):
                after(pe, ln_norm, first + t + 1)
                if first + t:
                    after(pe, ln_stored, first + t)
                for k in range(KT):
                    tr = pe.transpose(ps_back[:, k * P:(k + 1) * P], x_hat[:, t % 2, k * P:(k + 1) * P], ident[:, :])
                tr.then_inc(ln_back, 1)

            for b in range(2):
                after(pe, pj_free[b], chunks // 2)
            for t in range(ROW_SLOTS - 1):
                to_rows(t)
            for t in range(tiles):
                if t + ROW_SLOTS - 1 < tiles:
                    to_rows(t + ROW_SLOTS - 1)
                if not last:
                    to_columns(t)
            if not last:
                after(pe, ln_stored, first + tiles)

        normalise(0, S // P, A_CHUNK)

        def values(vt, sets, base, v_base):
            for n, tiles in enumerate(sets):
                if n >= 2:
                    pe.wait_ge(v_ready, v_base + (n - 1))
                for i, t in enumerate(tiles):
                    tr = pe.transpose(bank(4 + n % 2)[:, i * P:(i + 1) * P], vt[:, t * P:(t + 1) * P], ident[:, :])
                tr.then_inc(v_turned, 1)

        def wait_read(counts):
            for b, v in counts.items():
                after(pe, pj_free[b], v)

        def score(s, h0, scores):
            if s >= 2:
                pe.wait_ge(logit_done, h0 + (s - 1))
            for out, q, k in scores(s):
                mm = pe.matmul(out, q[0], k[0], start=True, stop=False)
                mm = pe.matmul(out, q[1], k[1], start=False, stop=True)
            mm.then_inc(score_done, 1)

        def attention(h0, p0, steps, scores, width, keys, logits, prob_t, v, free):
            def turn_probs(s):
                pe.wait_ge(prob_scaled, h0 + (s + 1))
                after(pe, pt_dve, h0 + s)
                after(pe, pt_act, h0 + s)
                c0, n = width(s), (KEYS - width(s)) // P
                for c in range(n):
                    at = c * P if c < dve_tiles(n) else PT_ACT + (c - dve_tiles(n)) * P
                    tr = pe.transpose(ps_pt[:, at:at + P], logits[s % SLOTS][:, c0 + c * P:c0 + (c + 1) * P], ident[:, :])
                tr.then_inc(pt_done, 1)

            def outputs(s):
                after(pe, pt_dve, h0 + (s + 1))
                after(pe, pt_act, h0 + (s + 1))
                p, h = s // 2, s % 2
                if s < 4:
                    after(pe, pj_free[p], free[p])
                elif h == 0:
                    after(pe, gated, p0 + p - 1)
                r, tiles = slice(h * HD, (h + 1) * HD), keys(p)
                for c, t in enumerate(tiles):
                    mm = pe.matmul(ps_out[p % 2][r, :], v(t)[:, r], prob_t[:, h, c, :], start=(c == 0),
                                   stop=(c == len(tiles) - 1))
                mm.then_inc(pv_done, 1)

            for s in range(steps):
                turn_probs(s)
                if s + 4 < steps:
                    score(s + 4, h0, scores)
                if s:
                    outputs(s - 1)
            outputs(steps - 1)

        def head_scores(h, q_parts, k_hi, k_lo, c, q, k):
            r = slice(h * HD, (h + 1) * HD)
            return c, (q(q_parts[h][:, :]), q(q_parts[h][r, :])), (k(k_hi[h][:, :]), k(k_lo[r, :]))

        def a_scores(s):
            t, h = s // 2, s % 2
            for c, k0, n in a_tile(t)[1]:
                yield head_scores(h, aq_parts, ak_hi, ak_lo, ps_score[h][:, P + c:P + c + n],
                                  lambda q: q[:, t * P:(t + 1) * P], lambda k: k[:, k0:k0 + n])

        for m in range(2):
            n, c = A_UNIT + 10 * m, A_CHUNK + 30 * m
            if m:
                after(pe, gated, 4 * A_TILES)
            for l in range(3):
                after(pe, mod_split, KT * (l + 1))
                project(n, 0, c // 2, l, u_hi, u_lo, ALL_CHUNKS[l:l + 1])
            project(n + 1, 1, c // 2, 3, u_hi, u_lo, ALL_CHUNKS)
            wait_read(free_counts(c // 2, 3, 3))
            values(a_tmp, [range(0, 4), range(4, 8), range(8, 10)], VSETS_A * m, VSETS_A * m)
            with pe.Fori(0, 4) as i:
                half = 3 * i + (c // 2 + 3)
                h0, p0 = i * A_STEPS + 4 * m * A_STEPS, i * A_TILES + 4 * m * A_TILES
                after(pe, gated, p0)
                project(2 * i + (n + 2), 0, half, 0, u_hi, u_lo, ALL_CHUNKS)
                project(2 * i + (n + 3), 1, half, 3, u_hi, u_lo, LAT_CHUNKS)
                pe.wait_ge(k_split, 4 * (m + 1))
                pe.wait_ge(q_split, 2 * i + 2 * (4 * m + 1))
                pe.wait_ge(v_ready, VSETS_A * (m + 1))
                for s in range(2):
                    score(s, h0, a_scores)
                project(2 * i + (n + 3), 1, half, 5, u_hi, u_lo, ALL_CHUNKS[2:])
                for s in range(2, 4):
                    score(s, h0, a_scores)
                attention(h0, p0, A_STEPS, a_scores, lambda s: a_tile(s // 2)[0], lambda p: a_tile(p)[2],
                          alog, aprob_t, lambda t: av[:, t, :], free_counts(half, 0, 6))

        def output_projection(n, c, chunks, layer):
            count = 2 * len(chunks)
            split = layer * KT * len(ALL_CHUNKS)
            ready = [(o_split, split + KT * (l + 1)) for l in range(len(chunks))]
            with pe.Fori(0, KT // 2) as i:
                for s in range(2):
                    project(2 * i + (n + s), s, (count // 2) * i + c // 2, s * len(chunks), u_hi, u_lo, chunks,
                            ready=None if s else ready)

        output_projection(AO_UNIT, AO_CHUNK, ALL_CHUNKS, 0)
        normalise(S // P, TC // P, B_CHUNK)

        def b_scores(s):
            t, h = s // 2, s % 2
            half, cb = t // 4, t % 4

            def near(k):
                return k[:, 0:S].rearrange("p (r c) -> p r c", c=GRID)[
                    :, 4 * half:4 * half + KEY_ROWS, KEY_COL[cb]:KEY_COL[cb] + KEY_COLS]

            for c, n, k in ((0, LAT_KEYS, near), (LAT_KEYS, C, lambda k: k[:, S:TC])):
                yield head_scores(h, bq_parts, bk_hi, bk_lo, ps_score[h][:, P + c:P + c + n],
                                  lambda q: q[:, t * P:(t + 1) * P], k)

        def b_keys(p):
            half, cb = p // 4, p % 4
            return [cb * 4 + half + n for n in range(3)] + [16, 17]

        with pe.Fori(0, PAIRS) as j:
            n, half = 4 * j + B_UNIT, 5 * j + B_CHUNK // 2
            h0, p0 = j * B_STEPS + STEPS_A, j * B_TILES + OT_A
            after(pe, gated, p0)
            for l in range(2):
                after(pe, mod_split, len(MODS) + KT * (l + 1))
                project(n, 0, half, l, u_hi, u_lo, LAT_CHUNKS[l:l + 1])
            after(pe, mod_split, 2 * len(MODS))
            project(n + 1, 1, half, 2, u_hi, u_lo, ALL_CHUNKS)
            project(n + 2, 0, half, 5, u_hi, u_lo, ALL_CHUNKS)
            project(n + 3, 1, half, 8, u_hi, u_lo, LAT_CHUNKS[:1])
            wait_read(free_counts(half, 5, 3))
            v0 = j * VSETS_B + 2 * VSETS_A
            values(b_vt, [range(0, 4), range(4, 8), range(8, 12), range(12, 16), range(16, 18)], v0, v0)
            pe.wait_ge(k_split, 4 * j + 4 * 3)
            pe.wait_ge(q_split, 2 * j + 2 * (PAIRS + 1))
            for s in range(2):
                score(s, h0, b_scores)
            project(n + 3, 1, half, 9, u_hi, u_lo, LAT_CHUNKS[1:])
            for s in range(2, 4):
                score(s, h0, b_scores)
            pe.wait_ge(v_ready, v0 + VSETS_B)
            attention(h0, p0, B_STEPS, b_scores, lambda s: 0, b_keys, blog, bprob_t, b_value, free_counts(half, 0, 10))
        output_projection(BO_UNIT, BO_CHUNK, LAT_CHUNKS, 1)
        normalise(S // P + TC // P, S // P, BO_CHUNK + 2 * KT, last=True)

    @block.scalar
    def _(act):
        loads = [(ident[:, :], a["ident"]), (vecs[:, :], a["vecs"]),
                 (corr[:, :, :], a["corr"]), (row_mask[:, :, :], a["row_mask"]), (col_mask[:, :, :], a["col_mask"]),
                 (sink_neg[:, :], bass.AP(tensor=a["sink"].tensor, offset=0, ap=[[0, P], [1, HEADS]])),
                 (c_in[:, :, :], bass.AP(tensor=a["c_rows"].tensor, offset=0, ap=[[0, P], [D, 2], [1, D]]))]
        for dst, src in loads:
            act.dma_start(dst, src).then_inc(const_loaded, 16)

        def wait_chunk(c):
            act.wait_ge(pj_done, c + 1)

        start_at_one(act, x_loaded[0], 16, (*pj_free, ln_stored, pt_act))
        for k in range(KT):
            act.wait_ge(x_loaded[k], 16)
            act.activation(x_hi[:, k, :], act_buf[:, k, 0:S], ACT.Copy).then_inc(x_hi_done, 1)
        act.wait_ge(const_loaded, 16 * len(loads))
        for who in range(2):
            act.activation(c_silu[who], c_in[:, who, :], ACT.Silu).then_inc(c_ready, 1)
        for k in range(KT):
            act.wait_ge(x_split, k + 1)
            act.activation(act_buf[:, k, 0:S], act_buf[:, k, 0:S], ACT.Copy, scale=ALPHA_1).then_inc(x_scaled, 1)
        with act.Fori(0, GROUPS) as g:
            c, half = g * L1_CHUNKS, g * (L1_CHUNKS // 2)
            for i in range(4):
                after(act, u_used, g * 4 + i)
                for h in range(2):
                    wait_chunk(c + (2 * i + h))
                    act.activation(u_pad[:, PAD + h * HALF:PAD + (h + 1) * HALF], pj[h], ACT.Copy).then_inc(pj_free[h], 1)
            for i in range(4):
                for h in range(2):
                    wait_chunk(c + (8 + 2 * i + h))
                    act.activation(gate_tile(i)[:, 2 * h:2 * h + 2, :], pj[h].rearrange("p (a b) -> p a b", b=C),
                                   ACT.Silu).then_inc(pj_free[h], 1)
            for n in range(8):
                i, h = n // 2, n % 2
                after(act, pj_free[h], half + 9 + i)
                act.activation(g_hi[:, i, h * HALF:(h + 1) * HALF].rearrange("p (a b) -> p a b", b=C),
                               gate_tile(i)[:, 2 * h:2 * h + 2, :], ACT.Copy).then_inc(g_hi_done, 1)

        def modulate(layer, n):
            ch, k = MODS[n]
            t0, tn = ALL_CHUNKS[ch]
            q = 6 * layer + (2 if ch == 2 else 0)
            n += len(MODS) * layer
            if n >= MOD_SLOTS:
                after(act, mod_split, n - MOD_SLOTS + 1)
            f, o = par[:, q, k:k + 1], par[:, q + 1, k:k + 1]
            x = act_buf[:, k, t0:t0 + tn]
            act.activation(u_tmp[:, n % MOD_SLOTS, 0:tn], x, ACT.Identity, scale=f, bias=o)
            act.activation(u_hi[:, k, t0:t0 + tn], x, ACT.Identity, scale=f, bias=o).then_inc(mod_done, 1)

        def normalise(first, tiles, layer):
            for t in range(tiles):
                for n in mods_after(t, tiles):
                    modulate(layer, n)
                act.wait_ge(ln_back, first + t + 2)
                act.activation(act_buf[:, :, t * P:(t + 1) * P], ps_back.rearrange("p (k n) -> p k n", n=P),
                               ACT.Copy).then_inc(ln_stored, 1)
                if t == 3:
                    act.wait_ge(par_ready, layer + 1)
                if t % 4 == 3 or t == tiles - 1:
                    after(act, ln_stored, first + t + 1)
            if layer == 0:
                act.wait_ge(ctx_loaded, 16 * 4)
            for n in mods_after(tiles, tiles):
                modulate(layer, n)

        def centre(tiles):
            for t in range(tiles):
                act.wait_ge(ln_var, S // P + TC // P + t + 1)
                if t >= 2:
                    after(act, out_scaled, t - 1)
                n = t % ROW_SLOTS
                act.activation(x_hat[:, t % 2, :], ps_rows[n], ACT.Identity, bias=neg_mean[:, n:n + 1]).then_inc(ln_centred, 1)

        def take_projection(c, half, l0, chunks, dst, func=ACT.Copy, scale=1.0):
            for n, (t0, tn) in enumerate(chunks):
                l = l0 + n
                wait_chunk(c + l)
                act.activation(dst[:, t0:t0 + tn], pj[l % 2][:, 0:tn], func, scale=scale).then_inc(pj_free[l % 2], 1)

        def probs(s, h0, width, end, logits):
            act.wait_ge(logit_done, h0 + (s + 1))
            c0, n, lg = width(s), s % SLOTS, logits[s % SLOTS]
            act.activation(lg[:, c0:end], lg[:, c0 + 1:end + 1], ACT.Exp, scale=-1.0,
                           bias=neg_max[:, n:n + 1], accum_out=row_sum[:, n:n + 1]).then_inc(prob_done, 1)

        def scale(s, h0, width, end, logits):
            act.wait_ge(rec_done, h0 + (s + 1))
            n, pr = s % SLOTS, logits[s % SLOTS][:, width(s):KEYS]
            act.activation(pr, pr, ACT.Copy, scale=row_rec[:, n:n + 1]).then_inc(prob_scaled, 1)

        def first_probs(*soft):
            for s in range(2):
                probs(s, *soft)
            for s in range(2):
                scale(s, *soft)

        def softmax(steps, prob_t, *soft):
            h0, width = soft[:2]
            for p in range(steps // 2):
                for s in (2 * p, 2 * p + 1):
                    act.wait_ge(pt_done, h0 + (s + 1))
                    n = (KEYS - width(s)) // P
                    d = dve_tiles(n)
                    act.activation(prob_t[:, s % 2, d:n, :], ps_pt[:, PT_ACT:PT_ACT + (n - d) * P].rearrange(
                        "p (t q) -> p t q", q=P), ACT.Copy).then_inc(pt_act, 1)
                    if s + 2 < steps:
                        probs(s + 2, *soft)
                for s in (2 * p + 2, 2 * p + 3):
                    if s < steps:
                        scale(s, *soft)

        def split_outputs(chunks, tiles):
            after(act, gated, tiles)
            for t0, tn in chunks:
                with act.Fori(0, KT) as k:
                    act.activation(col(u_hi, k, t0, t0 + tn), col(act_buf, k, t0, t0 + tn), ACT.Copy).then_inc(o_hi_done, 1)

        normalise(0, S // P, 0)
        for m in range(2):
            c = A_CHUNK + 30 * m
            if m:
                after(act, pv_done, 4 * A_STEPS)
            take_projection(c, None, 0, ALL_CHUNKS, a_tmp)
            act.wait_ge(k_split, 4 * (m + 1))
            take_projection(c, None, 3, ALL_CHUNKS, a_tmp)
            if m == 0:
                act.wait_ge(res_stored, 16 * KT)
            with act.Fori(0, 4) as i:
                ci = 6 * i + (c + 6)
                act.wait_ge(v_turned, VSETS_A * (m + 1))
                h0, p0 = i * A_STEPS + 4 * m * A_STEPS, i * A_TILES + 4 * m * A_TILES
                after(act, pv_done, h0)
                take_projection(ci, None, 0, ALL_CHUNKS, a_tmp, scale=Q_SCALE)
                gates = col(act_buf, i + 4 * m)
                take_projection(ci, None, 3, LAT_CHUNKS, gates, func=ACT.Silu)
                soft = h0, lambda s: a_tile(s // 2)[0], KEYS + 1, alog
                first_probs(*soft)
                take_projection(ci, None, 5, ALL_CHUNKS[2:], gates, func=ACT.Silu)
                softmax(A_STEPS, aprob_t, *soft)
        split_outputs(ALL_CHUNKS, OT_A)
        residual_loads(act, 0, AO_CHUNK, ALL_CHUNKS)
        normalise(S // P, TC // P, 1)
        with act.Fori(0, PAIRS) as j:
            c = 10 * j + B_CHUNK
            h0, p0 = j * B_STEPS + STEPS_A, j * B_TILES + OT_A
            after(act, pv_done, h0)
            for h in range(2):
                wait_chunk(c + h)
                act.activation(b_tmp_q[:, h * HALF:(h + 1) * HALF].rearrange("p (b r c) -> p b r c", b=4, r=8),
                               pj[h].rearrange("p (r b c) -> p b r c", b=4, r=8), ACT.Copy,
                               scale=Q_SCALE).then_inc(pj_free[h], 1)
            take_projection(c, None, 2, ALL_CHUNKS, b_tmp_k)
            act.wait_ge(k_split, 4 * j + 4 * 3)
            for n, (t0, tn) in enumerate(ALL_CHUNKS):
                l = 5 + n
                wait_chunk(c + l)
                if n < 2:
                    src = pj[l % 2].rearrange("p (r c) -> p r c", c=GRID)
                    for cb in range(4):
                        dst = b_vt[:, cb * HALF + n * C:cb * HALF + (n + 1) * C].rearrange("p (r c) -> p r c", c=KEY_COLS)
                        ins = act.activation(dst, src[:, :, KEY_COL[cb]:KEY_COL[cb] + KEY_COLS], ACT.Copy)
                else:
                    ins = act.activation(b_vt[:, 4 * HALF:4 * HALF + C], pj[l % 2][:, 0:tn], ACT.Copy)
                ins.then_inc(pj_free[l % 2], 1)
            act.wait_ge(res_stored, 16 * 2 * KT)
            gates = col(act_buf, j, 0, S)
            take_projection(c, None, 8, LAT_CHUNKS[:1], gates, func=ACT.Silu)
            soft = h0, lambda s: 0, KEYS, blog
            first_probs(*soft)
            take_projection(c, None, 9, LAT_CHUNKS[1:], gates, func=ACT.Silu)
            softmax(B_STEPS, bprob_t, *soft)
        split_outputs(LAT_CHUNKS, OT_A + PAIRS * B_TILES)
        residual_loads(act, 1, BO_CHUNK, LAT_CHUNKS)
        centre(S // P)

    @block.vector
    def _(dve):
        step = Chain(dve, dve_step)

        def wait_chunk(c):
            dve.wait_ge(pj_done, c + 1)

        start_at_one(dve, x_loaded[0], 16, (ada_done, u_used, ln_norm, mod_split, pt_dve, gated, out_scaled))
        for k in range(KT):
            dve.wait_ge(x_hi_done, k + 1)
            dve.tensor_tensor(x_lo[:, k, :], act_buf[:, k, 0:S], x_hi[:, k, :].bitcast(F32), ALU.subtract).then_inc(x_split, 1)

        dve.wait_ge(const_loaded, 16 * 7)
        step(dve.tensor_scalar(sink_neg[:, :], sink_neg[:, :], -1.0, None, ALU.mult))

        def window(g, i):
            w, half = WINDOWS[g], g * (L1_CHUNKS // 2)
            for b, v in free_counts(half, 2 * i, 2).items():
                after(dve, pj_free[b], v)
            src, lo, sh = u_pad, 0, 1
            for n in range(g + 1):
                dst = win[n % 2]
                lo += sh
                step(dve.tensor_tensor(dst[:, lo:PAD + S], src[:, lo:PAD + S], src[:, lo - sh:PAD + S - sh], ALU.add))
                src, sh = dst, 2 * sh
            step(dve.tensor_tensor(src[:, PAD:2 * PAD], src[:, PAD:2 * PAD], corr[:, g, :], ALU.mult))
            m = win[(g + 1) % 2]
            dve.scalar_tensor_tensor(m[:, PAD:], src[:, PAD:], 1.0 / w, u_pad[:, PAD:], ALU.mult,
                                     ALU.subtract).then_inc(u_used, 1)
            after(dve, u_used, 4 * g + i + 1)
            step(dve.tensor_copy(m_hi[:, i, :], m[:, PAD:]))
            dve.tensor_tensor(m_lo[:, i, :], m[:, PAD:], m_hi[:, i, :].bitcast(F32), ALU.subtract).then_inc(m_split, 1)
            dve.wait_ge(m_split, 4 * g + i + 1)

        def modulation(n):
            dve.wait_ge(ada_loaded, 16 * (n + 1))
            dve.wait_ge(c_ready, 2)
            for who in range(2):
                ins = dve.tensor_tensor_reduce(ada_products, w_ada[:, :], c_silu[who], 1.0, b_ada[:, n:n + 1], ALU.mult, ALU.add,
                                               ada[:, n, who:who + 1])
                if who == 0:
                    step(ins)
            ins.then_inc(ada_done, 1)
            after(dve, ada_done, n + 1)

        def factors():
            after(dve, ada_done, ADA_UNITS)
            for layer, g, b in ((0, ln_g1, ln_b1), (1, ln_g2, ln_b2)):
                n, q = 24 * layer, 6 * layer
                for who in range(2):
                    shift, scale = ada[:, n:n + KT, who], ada[:, n + KT:n + 2 * KT, who]
                    f, o = par[:, q + 2 * who, :], par[:, q + 2 * who + 1, :]
                    if layer == 0 and who == 1:
                        step(dve.tensor_scalar(f, scale, 1.0, None, ALU.add))
                        step(dve.tensor_copy(o, shift))
                        continue
                    step(dve.tensor_scalar(f, scale, 1.0, None, ALU.add))
                    step(dve.tensor_tensor(o, f, b, ALU.mult))
                    step(dve.tensor_tensor(o, o, shift, ALU.add))
                    step(dve.tensor_tensor(f, f, g, ALU.mult))
                step(dve.tensor_scalar(par[:, q + 4, :], g, ALPHA_2, None, ALU.mult))
                dve.tensor_scalar(par[:, q + 5, :], b, ALPHA_2, None, ALU.mult).then_inc(par_ready, 1)

        for g in range(GROUPS):
            c = g * L1_CHUNKS
            step(dve.memset(u_pad[:, 0:PAD], 0.0))
            for i in range(4):
                window(g, i)
                modulation(ADA * g + i)
            for i in range(4, 8):
                modulation(ADA * g + i)
            def gated_low(n):
                i, h = n // 2, n % 2
                dve.wait_ge(g_hi_done, 8 * g + n + 1)
                dve.tensor_tensor(g_lo[:, i, h * HALF:(h + 1) * HALF].rearrange("p (a b) -> p a b", b=C),
                                  gate_tile(i)[:, 2 * h:2 * h + 2, :],
                                  g_hi[:, i, h * HALF:(h + 1) * HALF].bitcast(F32).rearrange("p (a b) -> p a b", b=C),
                                  ALU.subtract).then_inc(g_split, 1)

            for n in range(8):
                i, h = n // 2, n % 2
                wait_chunk(c + 16 + n)
                gt = gate_tile(i)[:, 2 * h:2 * h + 2, :]
                dve.scalar_tensor_tensor(gt, pj[h].rearrange("p (a b) -> p a b", b=C), pool_scale[:, 4 * g + i:4 * g + i + 1],
                                         gt, ALU.mult, ALU.mult).then_inc(pj_free[h], 1)
                if n == 3:
                    modulation(ADA * g + 8)
                if n:
                    gated_low(n - 1)
            gated_low(7)
            modulation(ADA * g + 9)
            if g == 0:
                dve.wait_ge(x_scaled, KT)
            for o in range(KT):
                for h in range(2):
                    wait_chunk(c + 24 + 2 * o + h)
                    y = act_buf[:, o, h * HALF:(h + 1) * HALF]
                    dve.tensor_tensor(y, pj[h], y, ALU.add).then_inc(pj_free[h], 1)
                if o in (1, 3):
                    modulation(ADA * g + 10 + o // 2)
                if o == 4 and g == GROUPS - 1:
                    factors()

        def statistics(t, first, last=False):
            n, rows = t % ROW_SLOTS, ps_rows[t % ROW_SLOTS]
            dve.wait_ge(ln_turned, first + t + 1)
            dve.bn_stats(stats[:, n, 0:6], rows[:, 0:HALF])
            step(dve.bn_stats(stats[:, n, 6:12], rows[:, HALF:D]))
            step(dve.bn_aggr(mean_var[:, n, :], stats[:, n, :]))
            if last:
                dve.tensor_scalar(neg_mean[:, n:n + 1], mean_var[:, n, 0:1], -1.0, None, ALU.mult)
            dve.tensor_scalar(var_eps[:, n:n + 1], mean_var[:, n, 1:2], LN_EPS, None, ALU.add).then_inc(ln_var, 1)

        def low_part(layer, n):
            ch, k = MODS[n]
            t0, tn = ALL_CHUNKS[ch]
            n += len(MODS) * layer
            dve.wait_ge(mod_done, n + 1)
            dve.tensor_tensor(u_lo[:, k, t0:t0 + tn], u_tmp[:, n % MOD_SLOTS, 0:tn], u_hi[:, k, t0:t0 + tn].bitcast(F32),
                              ALU.subtract).then_inc(mod_split, 1)

        def normalise(first, tiles, layer):
            statistics(0, first)
            for t in range(tiles):
                if t + 1 < tiles:
                    statistics(t + 1, first)
                n = t % ROW_SLOTS
                dve.wait_ge(ln_rstd, first + t + 1)
                if first + t >= 2:
                    after(dve, ln_back, first + t - 1)
                dve.tensor_scalar(x_hat[:, t % 2, :], ps_rows[n], mean_var[:, n, 0:1], rstd[:, n:n + 1], ALU.subtract,
                                  ALU.mult).then_inc(ln_norm, 1)
                for n in mods_after(t, tiles):
                    low_part(layer, n)
            for n in mods_after(tiles, tiles):
                low_part(layer, n)
            after(dve, mod_split, len(MODS) * (layer + 1))

        def normalise_last(first, tiles):
            dve.wait_ge(ctx_loaded, 16 * 6)
            statistics(0, first, last=True)
            for t in range(tiles):
                if t + 1 < tiles:
                    statistics(t + 1, first, last=True)
                n, place = t % ROW_SLOTS, t % 2
                dve.wait_ge(ln_rstd, first + t + 1)
                dve.wait_ge(ln_centred, t + 1)
                dve.wait_ge(out_stored[place], 16 * (t // 2 + 1))
                dve.scalar_tensor_tensor(out_tile[:, place, :], x_hat[:, place, :], rstd[:, n:n + 1], g_row[:, :], ALU.mult,
                                         ALU.mult).then_inc(out_scaled, 1)

        heads = (slice(0, HD), slice(HD, P))

        def split_queries(parts, src):
            for r, part in zip(heads, parts):
                step(dve.tensor_copy(part[r, :], src[r, :]))
            for r, o, part in zip(heads, heads[::-1], parts):
                dve.tensor_tensor(part[o, :], src[r, :], part[r, :].bitcast(F32), ALU.subtract).then_inc(q_split, 1)

        def split_keys(hi, lo, src):
            for r, part in zip(heads, hi):
                step(dve.tensor_copy(part[r, :], src[r, :]))
            for r, o, part in zip(heads, heads[::-1], hi):
                dve.tensor_copy(part[o, :], src[r, :]).then_inc(k_split, 1)
                dve.tensor_tensor(lo[r, :], src[r, :], part[r, :].bitcast(F32), ALU.subtract).then_inc(k_split, 1)

        swap = [(n + 16) % 32 for n in range(32)]

        def rotate():
            step(dve.stream_shuffle(a_swap[:, :], a_tmp[:, 0:S], swap))
            step(dve.tensor_tensor(a_swap[:, :], a_swap[:, :], rope_sin[:, :], ALU.mult))
            step(dve.tensor_tensor(a_tmp[:, 0:S], a_tmp[:, 0:S], rope_cos[:, :], ALU.mult))
            step(dve.tensor_tensor(a_tmp[:, 0:S], a_tmp[:, 0:S], a_swap[:, :], ALU.add))

        def take_values(places, v_base):
            for n, v in enumerate(places):
                dve.wait_ge(v_turned, v_base + (n + 1))
                rows, width = v.shape[1:]
                dve.tensor_copy(v, bank(4 + n % 2)[:, 0:rows * width].rearrange("p (t n) -> p t n", n=width)).then_inc(v_ready, 1)

        def softmax(h0, p0, steps, width, mask, start, prob_t, logits, ready, gate):
            def logit(s):
                if s >= SLOTS:
                    dve.wait_ge(pt_done, h0 + (s - SLOTS + 1))
                ready(s)
                dve.wait_ge(score_done, h0 + (s + 1)).then_inc(dve_waited, 1)
                c0, n = width(s), s % SLOTS
                dve.tensor_tensor_reduce(logits[n][:, c0 + 1:KEYS + 1], ps_score[s % 2][:, P + c0:P + KEYS], mask(s), -1.0,
                                         start(s), ALU.add, ALU.min, neg_max[:, n:n + 1]).then_inc(logit_done, 1)

            def reciprocal(s):
                dve.wait_ge(prob_done, h0 + (s + 1))
                n = s % SLOTS
                dve.reciprocal(row_rec[:, n:n + 1], row_sum[:, n:n + 1]).then_inc(rec_done, 1)

            def take_probs(s):
                dve.wait_ge(pt_done, h0 + (s + 1))
                d = dve_tiles((KEYS - width(s)) // P)
                dve.tensor_copy(prob_t[:, s % 2, 0:d, :], ps_pt[:, 0:d * P].rearrange("p (t q) -> p t q", q=P)).then_inc(pt_dve, 1)

            def gate_output(p):
                after(dve, pv_done, h0 + (2 * p + 2))
                out, y = gate(p, ps_out[p % 2])
                dve.tensor_tensor(y, out, y, ALU.mult).then_inc(gated, 1)

            for s in range(2):
                logit(s)
            for s in range(2):
                reciprocal(s)
            for s in range(2, 4):
                logit(s)
            for p in range(steps // 2):
                for s in (2 * p, 2 * p + 1):
                    take_probs(s)
                    if s % 2 and s + 1 < steps:
                        reciprocal(s + 1)
                    if s + 4 < steps:
                        logit(s + 4)
                if 2 * p + 3 < steps:
                    reciprocal(2 * p + 3)
                if p:
                    gate_output(p - 1)
            gate_output(steps // 2 - 1)

        def split_outputs(layer, chunks):
            for l, (t0, tn) in enumerate(chunks):
                with dve.Fori(0, KT) as k:
                    dve.wait_ge(o_hi_done, k + (layer * KT * len(ALL_CHUNKS) + l * KT + 1))
                    dve.tensor_tensor(col(u_lo, k, t0, t0 + tn), col(act_buf, k, t0, t0 + tn),
                                      col(u_hi, k, t0, t0 + tn).bitcast(F32), ALU.subtract).then_inc(o_split, 1)

        def residual_sums(layer, c, chunks):
            dve.wait_ge(o_split, KT * len(ALL_CHUNKS) + layer * KT * len(LAT_CHUNKS))
            count = len(chunks)
            with dve.Fori(0, KT // 2) as i:
                for s in range(2):
                    o = 2 * i + s
                    dve.wait_ge(res_loaded[s], i * 16 + (layer * 16 * (KT // 2) + 16))
                    for n, (t0, tn) in enumerate(chunks):
                        l = s * count + n
                        wait_chunk(2 * count * i + (c + l))
                        g = ada[:, bass.ds(o + (24 * layer + 16), 1), n // 2].rearrange("p a -> p a")
                        dve.scalar_tensor_tensor(col(act_buf, o, t0, t0 + tn), pj[l % 2][:, 0:tn], g, res[:, s, t0:t0 + tn],
                                                 ALU.mult, ALU.add).then_inc(pj_free[l % 2], 1)

        normalise(0, S // P, 0)
        dve.wait_ge(ctx_loaded, 16 * 4)
        for m in range(2):
            c = A_CHUNK + 30 * m
            for b, v in free_counts(c // 2, 0, 3).items():
                after(dve, pj_free[b], v)
            rotate()
            split_keys(ak_hi, ak_lo, a_tmp)
            take_values([av[:, 0:4, :], av[:, 4:8, :], av[:, 8:10, :]], VSETS_A * m)
            with dve.Fori(0, 4) as i:
                step.begin(i, 7)
                half = 3 * i + (c // 2 + 3)
                h0, p0 = i * A_STEPS + 4 * m * A_STEPS, i * A_TILES + 4 * m * A_TILES
                for b, v in free_counts(half, 0, 3).items():
                    after(dve, pj_free[b], v).then_inc(dve_waited, 1)
                rotate()
                split_queries(aq_parts, a_tmp)
                dve.wait_ge(q_split, 2 * i + 2 * (4 * m + 1))
                for n in range(SLOTS):
                    ins = dve.tensor_copy(alog[n][:, KEYS + 1:KEYS + 2], sink_neg[:, bass.ds(2 * i + (8 * m + n % 2), 1)])
                step(ins)

                def gate(p, out):
                    return out, col(act_buf, i + 4 * m, p * P, (p + 1) * P)

                softmax(h0, p0, A_STEPS, lambda s: a_tile(s // 2)[0],
                        lambda s: a_mask[:, a_tile(s // 2)[3]:a_tile(s // 2)[3] + KEYS - a_tile(s // 2)[0]],
                        lambda s: alog[s % SLOTS][:, KEYS + 1:KEYS + 2], aprob_t, alog, lambda s: None, gate)
            step.end(4)
        split_outputs(0, ALL_CHUNKS)
        residual_sums(0, AO_CHUNK, ALL_CHUNKS)
        normalise(S // P, TC // P, 1)
        with dve.Fori(0, PAIRS) as j:
            step.begin(j, 4)
            half = 5 * j + B_CHUNK // 2
            h0, p0 = j * B_STEPS + STEPS_A, j * B_TILES + OT_A
            for b, v in free_counts(half, 0, 2).items():
                after(dve, pj_free[b], v)
            split_queries(bq_parts, b_tmp_q)
            for b, v in free_counts(half, 2, 3).items():
                after(dve, pj_free[b], v)
            split_keys(bk_hi, bk_lo, b_tmp_k)
            take_values([act_buf[:, 2 * n:2 * n + 2, S:TC] for n in range(4)] + [bv_ctx[:, :, :]], j * VSETS_B + 2 * VSETS_A)

            def built(s):
                t, h = s // 2, s % 2
                b = 3 * (t // 4) + COL_TYPE[t % 4]
                dve.wait_ge(bias_ready, j * (2 * B_BUILDS) + (2 * b + h + 1))

            def bias_of(s):
                t, h = s // 2, s % 2
                return bias[:, h, (3 * (t // 4) + COL_TYPE[t % 4]) % 2, :]

            def gate(p, out):
                half_rows, cb = p // 4, p % 4
                y = act_buf[:, bass.ds(j, 1), half_rows * HALF:(half_rows + 1) * HALF].rearrange("p a (r c) -> p (a r) c", c=GRID)
                return out.rearrange("p (r c) -> p r c", c=16), y[:, :, cb * 16:(cb + 1) * 16]

            softmax(h0, p0, B_STEPS, lambda s: 0, bias_of, lambda s: NO_MAX, bprob_t, blog, built, gate)
        step.end(PAIRS)
        split_outputs(1, LAT_CHUNKS)
        residual_sums(1, BO_CHUNK, LAT_CHUNKS)
        normalise_last(S // P + TC // P, S // P)

    ctx.close()


def columns_of(w, cols):
    return w[:, cols].reshape(KT, P, P).transpose(1, 0, 2).reshape(P, UNIT)


def four_tiles(w, ot):
    return w[:, ot * P:(ot + 2) * P].reshape(4, P, 2, P).transpose(1, 2, 0, 3).reshape(P, UNIT)


def weight_units(w_in, w_grp, w_out, a_in, a_out, b_in, b_out):
    units, span = [], np.arange(P)
    width = GROUPS * HALF
    for g in range(GROUPS):
        units += [columns_of(w_in, g * HALF + i * P + span) for i in range(4)]
        units += [columns_of(w_in, width + g * HALF + i * P + span) for i in range(4)]
        units += [four_tiles(w_grp[g], ot) for ot in (0, 2)]
        units += [four_tiles(w_out[g * HALF:(g + 1) * HALF], ot) for ot in (0, 2, 4, 6)]
    pairs = np.concatenate([pair_heads(jj) for jj in range(PAIRS)])
    for m in range(2):
        units += [columns_of(a_in, D + m * P + span), columns_of(a_in, D + 2 * P + m * P + span)]
        for i in range(4):
            heads = pair_heads(4 * m + i)
            units += [columns_of(a_in, heads), columns_of(a_in, D + 4 * P + heads)]
    units += [columns_of(a_out[pairs], ot * P + span) for ot in range(KT)]
    for j in range(PAIRS):
        units += [columns_of(b_in, part * D + j * P + span) for part in range(4)]
    units += [columns_of(b_out, ot * P + span) for ot in range(KT)]
    assert len(units) == ALL_UNITS
    return np.stack(units)


def pair_heads(jj):
    m, i = jj // 4, jj % 4
    return np.concatenate([(8 * m + 4 * h + i) * HD + np.arange(HD) for h in range(2)])


def turned(x):
    return x.T.reshape(KT, P, -1).transpose(1, 0, 2)


def by_feature(v):
    return v.reshape(-1, P).T


def shape_tables():
    t = {"ident": np.eye(P)}
    n = np.arange(PAD)
    t["corr"] = np.broadcast_to(np.stack([w / np.minimum(n + 1, w) for w in WINDOWS]), (P, GROUPS, PAD))
    p = np.arange(P)
    rr, qq = p // 16, p % 16
    row_mask = np.zeros((P, 2, KEY_ROWS))
    for half in range(2):
        first = np.clip(8 * half + rr - 4, 0, ROWS - 8)[:, None]
        key = 4 * half + np.arange(KEY_ROWS)
        row_mask[:, half] = np.where((key >= first) & (key < first + 8), 0, MASKED)
    col_mask = np.zeros((P, 3, KEY_COLS))
    for kind, cb in enumerate((0, 1, 3)):
        first = np.clip(cb * 16 + qq - 8, 0, GRID - 16)[:, None]
        key = KEY_COL[cb] + np.arange(KEY_COLS)
        col_mask[:, kind] = np.where((key >= first) & (key < first + 16), 0, MASKED)
    t["row_mask"], t["col_mask"] = row_mask, col_mask
    col = np.arange(P)
    before, behind = (np.where(seen, 0, MASKED) for seen in (col[None] >= p[:, None], col[None] <= p[:, None]))
    a_mask = np.zeros((P, 9, P))
    a_mask[:, 0], a_mask[:, 2], a_mask[:, 5] = before, behind, before
    a_mask = a_mask.reshape(P, 9 * P)
    t["a_mask"] = a_mask
    freq = np.float32(10000.0) ** (-(p % 16).astype(np.float32) / np.float32(16))
    tok = np.arange(S)
    place = np.where((p // 32 % 2 == 0)[:, None], tok // GRID, tok % GRID).astype(np.float32)
    angle = place * freq[:, None]
    t["rope_cos"] = np.cos(angle)
    t["rope_sin"] = np.sin(angle) * np.where(p % 32 < 16, -1, 1)[:, None]
    return t


def kernel(**inputs):
    import concourse.bacc as bacc
    from concourse.bass_utils import run_bass_kernel_spmd

    x = {n: np.asarray(v) for n, v in inputs.items()}
    arrays = shape_tables()
    arrays["weights"] = weight_units(x["pool_w_in"][0], x["pool_w_grp"][0], x["pool_w_out"][0], x["a_w_in_2"][0],
                                     x["a_w_out_2"][0], x["b_w_in_2"][0], x["b_w_out_2"][0])
    arrays["w_ada"] = x["w_ada_2"].transpose(0, 2, 1).reshape(ADA_UNITS, P, D)
    arrays["x_t"], arrays["ctx_t"] = turned(x["x"][0]), turned(x["ctx_2"][0])
    arrays["c_rows"] = np.stack([x["c_2"][0], x["c_ctx_2"]])
    arrays["vecs"] = np.concatenate([by_feature(x[n]) for n in ("ln_g", "ln_b")]
                                    + [by_feature(x[n][0]) for n in ("ln_g_2", "ln_b_2")]
                                    + [by_feature(x["pool_scale"][0]), by_feature(x["b_ada_2"])], axis=1)
    arrays["ln_g3"], arrays["ln_b3"] = x["ln_g_2"][1:2], x["ln_b_2"][1:2]
    arrays["sink"] = x["a_sink_2"][:, [8 * (jj // 4) + 4 * h + jj % 4 for jj in range(PAIRS) for h in range(2)]]
    tab = np.zeros((HEADS, TAB_R, TAB_C), np.float32)
    tab[:, 4:19, 16:47] = x["b_rel_bias_2"][0]
    arrays["bias_tab"] = tab[:, ::-1, ::-1].reshape(HEADS, TAB_R * TAB_C)
    arrays = {n: np.ascontiguousarray(v, dtype=np.float32) for n, v in arrays.items()}

    nc = bacc.Bacc("TRN2", target_bir_lowering=False, num_devices=1)
    aps = {n: nc.dram_tensor(n + "_in", v.shape, F32, kind="ExternalInput").ap() for n, v in arrays.items()}
    aps["out"] = nc.dram_tensor("out", (S // P, P, D), F32, kind="ExternalOutput").ap()
    build(nc, aps)
    r = run_bass_kernel_spmd(nc, [{n + "_in": v for n, v in arrays.items()}], core_ids=[0])
    return r.results[0]["out"].reshape(1, S, D)
```
